# Optimizing a Trainium2 kernel written in Bass

```python
import jax, jax.numpy as jnp
from jax import lax
import numpy as np

D_MODEL = 2048
BATCH = 1
SEQ = 256
DEPTH = 1
DEC_BATCH = 8
DEC_SEQ = 4
PAST_LEN = 1024
PAGE_SIZE = 128

MLSTM_HEADS = 8
MLSTM_DH = 128
MLSTM_W = MLSTM_HEADS * MLSTM_DH
MLSTM_CHUNK = 64
MOBA_HEADS = 8
MOBA_DH = 128
MOBA_W = MOBA_HEADS * MOBA_DH
MOBA_BLOCK = 256
MOBA_TOPK = 3
MOBA_QCHUNK = 32
N_MEM = 256
XATTN_HEADS = 4
XATTN_DH = 128
XATTN_W = XATTN_HEADS * XATTN_DH
D_FF = -(-8 * D_MODEL // (3 * 256)) * 256
NORM_EPS = 1e-6
IN_SPLITS = (MLSTM_W, MLSTM_W, MLSTM_W, MLSTM_W, 2 * MLSTM_HEADS, MOBA_W, MOBA_W, MOBA_W, D_MODEL, D_MODEL)
IN_WIDTH = sum(IN_SPLITS)
IN_OFFSETS = tuple(sum(IN_SPLITS[:i + 1]) for i in range(len(IN_SPLITS) - 1))

kernel_name = 'hybrid_mlstm_moba_xattn_decode_step'

def rms_norm(x, g):
    xf = x.astype(jnp.float32)
    y = xf * lax.rsqrt(jnp.mean(xf * xf, axis=-1, keepdims=True) + NORM_EPS)
    return (y * g.astype(jnp.float32)).astype(x.dtype)

def alibi_slopes(n):
    return jnp.exp2(-8.0 * jnp.arange(1, n + 1, dtype=jnp.float32) / n)

def mlstm_chunkwise(q, k, v, ig, lf, C0, n0, m0):
    B, T, H, DH = q.shape
    L = MLSTM_CHUNK if T % MLSTM_CHUNK == 0 else T
    nc = T // L

    def chunks(a):
        return jnp.moveaxis(a.reshape((B, nc, L) + a.shape[2:]), 1, 0)

    causal = jnp.tril(jnp.ones((L, L), dtype=bool))[None, :, :, None]

    def step(carry, xs):
        C, n, m = carry
        qc, kc, vc, igc, lfc = xs
        b = jnp.cumsum(lfc, axis=1)
        logw = jnp.where(causal, b[:, :, None, :] - b[:, None, :, :] + igc[:, None, :, :], -jnp.inf)
        log_prev = b + m[:, None, :]
        m_t = jnp.maximum(log_prev, jnp.max(logw, axis=2))
        w = jnp.exp(logw - m_t[:, :, None, :])
        w_prev = jnp.exp(log_prev - m_t)
        s = jnp.einsum('bjhd,bshd->bjsh', qc, kc) * w
        num = jnp.einsum('bjsh,bshe->bjhe', s, vc) + w_prev[..., None] * jnp.einsum('bjhd,bhde->bjhe', qc, C)
        den = jnp.sum(s, axis=2) + w_prev * jnp.einsum('bjhd,bhd->bjh', qc, n)
        h = num / jnp.maximum(jnp.abs(den), jnp.exp(-m_t))[..., None]
        m_end = m_t[:, -1]
        w_end = jnp.exp(b[:, -1:] - b + igc - m_end[:, None])
        decay = jnp.exp(b[:, -1] + m - m_end)
        C = decay[..., None, None] * C + jnp.einsum('bsh,bshd,bshe->bhde', w_end, kc, vc)
        n = decay[..., None] * n + jnp.einsum('bsh,bshd->bhd', w_end, kc)
        return (C, n, m_end), h

    (C, n, m), hs = lax.scan(step, (C0, n0, m0), (chunks(q), chunks(k), chunks(v), chunks(ig), chunks(lf)))
    return jnp.moveaxis(hs, 0, 1).reshape(B, T, H, DH), C, n, m

def moba_attention(q, pos, k_all, v_all):
    B, T, H, DH = q.shape
    NB = k_all.shape[1] // MOBA_BLOCK
    kb = k_all.reshape(B, NB, MOBA_BLOCK, H, DH)
    vb = v_all.reshape(B, NB, MOBA_BLOCK, H, DH)
    kbar = jnp.mean(kb, axis=2, dtype=jnp.float32)
    topk = min(MOBA_TOPK, NB)
    slopes = alibi_slopes(H)
    qb = MOBA_QCHUNK if T % MOBA_QCHUNK == 0 else T
    nq = T // qb
    q_chunks = jnp.moveaxis(q.reshape(B, nq, qb, H, DH), 1, 0)
    pos_chunks = pos.reshape(nq, qb)
    b_idx = jnp.arange(B)[:, None, None, None]
    h_idx = jnp.arange(H)[None, None, :, None]
    blk_ids = jnp.arange(NB)
    offs = jnp.arange(MOBA_BLOCK)

    def attend(args):
        qq, pp = args
        own = pp // MOBA_BLOCK
        gate = jnp.einsum('bthd,bnhd->bthn', qq.astype(jnp.float32), kbar)
        past_blk = (blk_ids[None, :] < own[:, None])[None, :, None, :]
        gate = jnp.where(past_blk, gate, -jnp.inf)
        _, top = lax.top_k(gate, topk)
        own_b = jnp.broadcast_to(own[None, :, None, None], (B, qb, H, 1)).astype(top.dtype)
        sel = jnp.concatenate([top, own_b], axis=-1)
        blk_ok = jnp.concatenate([top < own_b, jnp.ones_like(own_b, dtype=bool)], axis=-1)
        kg = kb[b_idx, sel, :, h_idx]
        vg = vb[b_idx, sel, :, h_idx]
        dist = pp[None, :, None, None, None] - (sel[..., None] * MOBA_BLOCK + offs)
        ok = blk_ok[..., None] & (dist >= 0)
        s = (jnp.einsum('bthd,bthnkd->bthnk', qq, kg).astype(jnp.float32)
             - slopes[None, None, :, None, None] * dist.astype(jnp.float32))
        s = jnp.where(ok, s, -jnp.inf)
        p = jax.nn.softmax(s.reshape(B, qb, H, -1), axis=-1).reshape(s.shape)
        return jnp.einsum('bthnk,bthnkd->bthd', p.astype(vg.dtype), vg).astype(q.dtype)

    out = lax.map(attend, (q_chunks, pos_chunks))
    return jnp.moveaxis(out, 0, 1).reshape(B, T, H, DH)

def memory_kv(mem, norm_mem, w_xk, w_xv):
    B, M, _ = mem.shape
    mn = rms_norm(mem, norm_mem)
    return ((mn @ w_xk).reshape(B, M, XATTN_HEADS, XATTN_DH),
            (mn @ w_xv).reshape(B, M, XATTN_HEADS, XATTN_DH))

def cross_attend(xn, mem_k, mem_v, w_xq, w_xo):
    B, T, _ = xn.shape
    q = (xn @ w_xq).reshape(B, T, XATTN_HEADS, XATTN_DH) * (XATTN_DH ** -0.5)
    s = jnp.einsum('bthd,bmhd->bhtm', q, mem_k).astype(jnp.float32)
    p = jax.nn.softmax(s, axis=-1).astype(mem_v.dtype)
    o = jnp.einsum('bhtm,bmhd->bthd', p, mem_v).reshape(B, T, XATTN_W).astype(xn.dtype)
    return o @ w_xo

def decoder_layer(x, pos, C0, n0, m0, past_k, past_v, mem_k, mem_v, W):
    B, T, _ = x.shape
    f32 = jnp.float32
    xn = rms_norm(x, W['norm_mix'])
    q_m, k_m, v_m, o_m, if_pre, q_a, k_a, v_a, g_m, g_a = jnp.split(xn @ W['w_in'], IN_OFFSETS, axis=-1)
    gates = if_pre.astype(f32) + W['b_if'].astype(f32)
    ig = gates[..., :MLSTM_HEADS]
    lf = jax.nn.log_sigmoid(gates[..., MLSTM_HEADS:])
    hm = lambda a: a.reshape(B, T, MLSTM_HEADS, MLSTM_DH).astype(f32)
    h_m, C, n, m = mlstm_chunkwise(hm(q_m), hm(k_m) * (MLSTM_DH ** -0.5), hm(v_m), ig, lf,
                                   C0.astype(f32), n0.astype(f32), m0.astype(f32))
    h_m = (h_m * lax.rsqrt(jnp.mean(h_m * h_m, axis=-1, keepdims=True) + NORM_EPS)
           * W['mh_gain'].astype(f32).reshape(MLSTM_HEADS, MLSTM_DH))
    h_m = (h_m.reshape(B, T, MLSTM_W) * jax.nn.sigmoid(o_m.astype(f32))).astype(x.dtype)
    ha = lambda a: a.reshape(B, T, MOBA_HEADS, MOBA_DH)
    k_a, v_a = ha(k_a), ha(v_a)
    if past_k is None:
        k_all, v_all = k_a, v_a
    else:
        k_all = jnp.concatenate([past_k, k_a.astype(past_k.dtype)], axis=1)
        v_all = jnp.concatenate([past_v, v_a.astype(past_v.dtype)], axis=1)
    pad = (-k_all.shape[1]) % MOBA_BLOCK
    if pad:
        k_all = jnp.pad(k_all, ((0, 0), (0, pad), (0, 0), (0, 0)))
        v_all = jnp.pad(v_all, ((0, 0), (0, pad), (0, 0), (0, 0)))
    h_a = moba_attention(ha(q_a) * (MOBA_DH ** -0.5), pos, k_all, v_all).reshape(B, T, MOBA_W)
    u = jax.nn.sigmoid(g_m) * (h_m @ W['w_proj_m']) + jax.nn.sigmoid(g_a) * (h_a @ W['w_proj_a'])
    x = x + u @ W['w_out']
    x = x + cross_attend(rms_norm(x, W['norm_xattn']), mem_k, mem_v, W['w_xq'], W['w_xo'])
    xf = rms_norm(x, W['norm_ffn'])
    x = x + (jax.nn.silu(xf @ W['w_ffn_gate']) * (xf @ W['w_ffn_up'])) @ W['w_ffn_down']
    return x, k_a, v_a, C, n, m

def setup_inputs(seed: int = 0) -> dict:
    key = jax.random.key(seed)
    ks = iter(jax.random.split(key, 48))
    n_pages = PAST_LEN // PAGE_SIZE
    n_used = DEC_BATCH * n_pages
    n_phys = n_used + max(1, n_used // 4)
    D, L = D_MODEL, DEPTH

    def nrm(shape, scale=1.0):
        return scale * jax.random.normal(next(ks), shape, jnp.float32)

    def gain(n):
        return 1.0 + nrm((L, n), 0.01)

    page_table = jax.random.permutation(next(ks), n_phys)[:n_used].reshape(DEC_BATCH, n_pages).astype(jnp.int32)
    b_if = jnp.concatenate([nrm((L, MLSTM_HEADS), 0.1),
                            jnp.linspace(3.0, 6.0, MLSTM_HEADS, dtype=jnp.float32)[None] + nrm((L, MLSTM_HEADS), 0.1)], axis=-1)
    return {
        'x_prompt': nrm((BATCH, SEQ, D)),
        'x_sample': nrm((DEC_BATCH, DEC_SEQ, D)),
        'cache_k': nrm((L, n_phys, PAGE_SIZE, MOBA_HEADS, MOBA_DH)),
        'cache_v': nrm((L, n_phys, PAGE_SIZE, MOBA_HEADS, MOBA_DH)),
        'cache_mem_k': nrm((L, DEC_BATCH, N_MEM, XATTN_HEADS, XATTN_DH)),
        'cache_mem_v': nrm((L, DEC_BATCH, N_MEM, XATTN_HEADS, XATTN_DH)),
        'state_C': nrm((L, DEC_BATCH, MLSTM_HEADS, MLSTM_DH, MLSTM_DH), 0.5),
        'state_n': 0.5 * jnp.abs(nrm((L, DEC_BATCH, MLSTM_HEADS, MLSTM_DH))),
        'state_m': nrm((L, DEC_BATCH, MLSTM_HEADS)),
        'page_table': page_table,
        'mem_prompt': nrm((BATCH, N_MEM, D)),
        'norm_mix': gain(D),
        'w_in': nrm((L, D, IN_WIDTH), D ** -0.5),
        'b_if': b_if,
        'mh_gain': gain(MLSTM_W),
        'w_proj_m': nrm((L, MLSTM_W, D), MLSTM_W ** -0.5),
        'w_proj_a': nrm((L, MOBA_W, D), MOBA_W ** -0.5),
        'w_out': nrm((L, D, D), D ** -0.5),
        'norm_xattn': gain(D),
        'norm_mem': gain(D),
        'w_xq': nrm((L, D, XATTN_W), D ** -0.5),
        'w_xk': nrm((L, D, XATTN_W), D ** -0.5),
        'w_xv': nrm((L, D, XATTN_W), D ** -0.5),
        'w_xo': nrm((L, XATTN_W, D), XATTN_W ** -0.5),
        'norm_ffn': gain(D),
        'w_ffn_gate': nrm((L, D, D_FF), D ** -0.5),
        'w_ffn_up': nrm((L, D, D_FF), D ** -0.5),
        'w_ffn_down': nrm((L, D_FF, D), D_FF ** -0.5),
        'norm_final': 1.0 + nrm((D,), 0.01),
    }

def reference(x_prompt, x_sample, cache_k, cache_v, cache_mem_k, cache_mem_v, state_C, state_n, state_m,
              page_table, mem_prompt, norm_mix, w_in, b_if, mh_gain, w_proj_m, w_proj_a, w_out,
              norm_xattn, norm_mem, w_xq, w_xk, w_xv, w_xo, norm_ffn, w_ffn_gate, w_ffn_up, w_ffn_down,
              norm_final):
    B, T, _ = x_prompt.shape
    DB, TS, _ = x_sample.shape
    past = page_table.shape[1] * cache_k.shape[2]
    pos_p = jnp.arange(T, dtype=jnp.int32)
    pos_s = past + jnp.arange(TS, dtype=jnp.int32)
    hp, hs = x_prompt, x_sample
    kp_l, vp_l, Cp_l, np_l, mp_l, mkp_l, mvp_l = [], [], [], [], [], [], []
    ks_l, vs_l, Cs_l, ns_l, ms_l = [], [], [], [], []
    for l in range(DEPTH):
        W = dict(norm_mix=norm_mix[l], w_in=w_in[l], b_if=b_if[l], mh_gain=mh_gain[l],
                 w_proj_m=w_proj_m[l], w_proj_a=w_proj_a[l], w_out=w_out[l],
                 norm_xattn=norm_xattn[l], w_xq=w_xq[l], w_xo=w_xo[l],
                 norm_ffn=norm_ffn[l], w_ffn_gate=w_ffn_gate[l], w_ffn_up=w_ffn_up[l],
                 w_ffn_down=w_ffn_down[l])
        mk_p, mv_p = memory_kv(mem_prompt, norm_mem[l], w_xk[l], w_xv[l])
        C0 = jnp.zeros((B, MLSTM_HEADS, MLSTM_DH, MLSTM_DH), jnp.float32)
        n0 = jnp.zeros((B, MLSTM_HEADS, MLSTM_DH), jnp.float32)
        m0 = jnp.zeros((B, MLSTM_HEADS), jnp.float32)
        hp, kp, vp, Cp, n_p, mp = decoder_layer(hp, pos_p, C0, n0, m0, None, None, mk_p, mv_p, W)
        past_k = cache_k[l][page_table].reshape(DB, past, MOBA_HEADS, MOBA_DH)
        past_v = cache_v[l][page_table].reshape(DB, past, MOBA_HEADS, MOBA_DH)
        hs, k_s, v_s, Cs, n_s, ms = decoder_layer(hs, pos_s, state_C[l], state_n[l], state_m[l],
                                                  past_k, past_v, cache_mem_k[l], cache_mem_v[l], W)
        kp_l.append(kp); vp_l.append(vp); Cp_l.append(Cp); np_l.append(n_p); mp_l.append(mp)
        mkp_l.append(mk_p); mvp_l.append(mv_p)
        ks_l.append(k_s); vs_l.append(v_s); Cs_l.append(Cs); ns_l.append(n_s); ms_l.append(ms)
    y_prompt = rms_norm(hp, norm_final)
    y_sample = rms_norm(hs, norm_final)
    k_prompt = jnp.stack(kp_l)
    v_prompt = jnp.stack(vp_l)
    C_prompt = jnp.stack(Cp_l).astype(state_C.dtype)
    n_prompt = jnp.stack(np_l).astype(state_n.dtype)
    m_prompt = jnp.stack(mp_l).astype(state_m.dtype)
    mem_k_prompt = jnp.stack(mkp_l)
    mem_v_prompt = jnp.stack(mvp_l)
    k_sample = jnp.stack(ks_l).astype(cache_k.dtype)
    v_sample = jnp.stack(vs_l).astype(cache_v.dtype)
    C_sample = jnp.stack(Cs_l).astype(state_C.dtype)
    n_sample = jnp.stack(ns_l).astype(state_n.dtype)
    m_sample = jnp.stack(ms_l).astype(state_m.dtype)
    return (y_prompt, y_sample, k_prompt, v_prompt, C_prompt, n_prompt, m_prompt, mem_k_prompt, mem_v_prompt,
            k_sample, v_sample, C_sample, n_sample, m_sample)


_drawn_inputs = setup_inputs


def setup_inputs(seed=0):
    import zlib

    import numpy as np

    out = dict(_drawn_inputs(seed))
    spreads = {}
    factors = {'norm_mix': 3.188,
     'mh_gain': 8.0,
     'norm_xattn': 8.0,
     'norm_mem': 5.703,
     'norm_ffn': 7.738,
     'norm_final': 5.702}
    for name, (base, spread) in spreads.items():
        noise = np.random.default_rng([zlib.crc32(name.encode()), seed]).standard_normal(out[name].shape)
        drawn = base * np.exp(spread * noise) if base else spread * noise
        out[name] = __import__('jax').numpy.asarray(drawn.astype(out[name].dtype))
    for name, factor in factors.items():
        out[name] = (out[name] * factor).astype(out[name].dtype)
    return out
```

```python
import numpy as np

import concourse.bass as bass
from concourse import mybir
from contextlib import ExitStack

F32 = mybir.dt.float32
F32R = mybir.dt.float32r
I32 = mybir.dt.int32
ACT = mybir.ActivationFunctionType
ALU = mybir.AluOpType
AX = mybir.AxisListType.X
ds = bass.ds

P = 128
D = 2048
KT = D // P
TP, NB, TS = 256, 8, 4
NS = NB * TS
NT = TP + NS
H, DH = 8, 128
XH = 4
FF = 5632
PAGES, PAST = 8, 1024
BLOCKS = 4
MEM = 256
FH = FF // P // 2
FU = FH // 2
OWN = NS - TS
NEG = -1e30
EPS = 1e-6
SCALE = float(DH) ** -0.5
W_IF = 4 * H * DH
W_QA = W_IF + 2 * H
W_GM = W_QA + 3 * H * DH
W_GA = W_GM + D
SLOTS = 3
UNIT = KT * 256
CONST = dict(ident=128, cadd=384, cdist=384, sadd=32, tri=128, tris=32, lastp=128, lasts=32,
             bmask=8, lastm=8, slopes=8, rank=4)
CW = sum(CONST.values())


def constants():
    at = np.arange(P)
    c = {}
    c["ident"] = np.eye(P)
    late = at[:, None] - at[None, :]
    tri = np.where(late >= 0, 0.0, NEG)
    c["cadd"] = np.concatenate([tri, np.zeros((P, P)), tri], 1)
    c["cdist"] = np.concatenate([np.where(late >= 0, -late, NEG), -(late + P), np.where(late >= 0, -late, NEG)], 1)
    s = np.arange(NS)
    same = s[:, None] // TS == s[None, :] // TS
    c["sadd"] = np.where(same & (s[:, None] >= s[None, :]), 0.0, NEG)
    c["tri"] = (at[:, None] <= at[None, :]) * 1.0
    c["tris"] = (same & (s[:, None] <= s[None, :])) * 1.0
    c["lastp"] = np.repeat((at == P - 1)[:, None] * 1.0, P, 1)
    c["lasts"] = (same & (s[:, None] % TS == TS - 1)) * 1.0
    c["bmask"] = (s[:, None] // TS == np.arange(NB)[None, :]) * 1.0
    c["lastm"] = (s[:, None] == TS * np.arange(NB)[None, :] + TS - 1) * 1.0
    slope = 2.0 ** (-8.0 * np.arange(1, H + 1) / H)
    c["slopes"] = np.repeat(slope[None], P, 0)
    c["rank"] = np.repeat(np.arange(1.0, BLOCKS + 1)[None], P, 0)
    blob = np.zeros((P, CW), np.float32)
    o = 0
    for name, w in CONST.items():
        blob[:c[name].shape[0], o:o + w] = c[name]
        o += w
    r = np.arange(NS)
    h, t = r // TS, r % TS
    dec = np.full((NS, PAST + OWN + NS), NEG, np.float32)
    dec[:, :PAST] = -slope[h][:, None] * (PAST + t[:, None] - np.arange(PAST)[None])
    own = np.arange(TS)[None]
    dec[:, PAST + OWN:PAST + NS] = np.where(own <= t[:, None], -slope[h][:, None] * (t[:, None] - own), NEG)
    return blob, dec


class Phase:

    def __init__(self, plan, iters, units, convs, tiles, slots=range(10 ** 3)):
        self.loads0, self.reads0 = list(plan["loads"]), list(plan["reads"])
        self.conv0, self.tile0 = plan["convs"], plan["tiles"]
        self.units, self.convs, self.tiles, self.iters = units, convs, tiles, iters
        self.slots = [s % SLOTS for s in slots[:len(units)]]
        self.loads_per = [16 * sum(d for u, (d, r) in enumerate(units) if self.slots[u] == s) for s in range(SLOTS)]
        self.reads_per = [sum(r for u, (d, r) in enumerate(units) if self.slots[u] == s) for s in range(SLOTS)]
        for s in range(SLOTS):
            plan["loads"][s] += iters * self.loads_per[s]
            plan["reads"][s] += iters * self.reads_per[s]
        plan["convs"] += iters * convs
        plan["tiles"] += iters * tiles
        assert iters == 1 or (convs % 2 == 0 and tiles % 2 == 0)

    def slot(self, u):
        return self.slots[u]

    def landed(self, i, u):
        s = self.slots[u]
        mine = 16 * sum(d for v, (d, r) in enumerate(self.units) if self.slots[v] == s and v <= u)
        return i * self.loads_per[s] + (self.loads0[s] + mine)

    def reads(self, i, u, n=0):
        s = self.slots[u]
        mine = sum(r for v, (d, r) in enumerate(self.units) if self.slots[v] == s and v < u)
        return i * self.reads_per[s] + (self.reads0[s] + mine + n)

    def conv(self, i, c):
        return i * self.convs + (self.conv0 + c)

    def half(self, c):
        return (self.conv0 + c) % 2

    def bank(self, t):
        return (self.tile0 + t) % 2

    def evacs(self, i, t):
        return i * (self.tiles // 2) + (self.tile0 + t) // 2


def wait(eng, sem, value):
    if not (isinstance(value, int) and value <= 0):
        eng.wait_ge(sem, value)


def hold(eng, sem, value):
    if not (isinstance(value, int) and value <= 0):
        eng.wait_ge(sem, value)
        eng.nop(nofuse=True)


class Chain:

    def __init__(self, eng, sem):
        self.eng, self.sem, self.base, self.k, self.i, self.per = eng, sem, 0, 0, 0, 0

    def loop(self, i, per):
        if isinstance(self.i, int) and self.i == 0 and self.per == 0:
            self.base += self.k
        self.i, self.per, self.k = i, per, 0

    def end(self, n):
        assert self.k == self.per, (self.k, self.per)
        self.base += n * self.per
        self.i, self.per, self.k = 0, 0, 0

    def run(self, ins):
        ins.then_inc(self.sem, 1)
        self.k += 1

    def sync(self):
        self.eng.wait_ge(self.sem, self.i * self.per + (self.base + self.k))


def build(nc, a, o):
    N_PHYS = a["cache_k"].shape[1]
    plan = dict(loads=[0] * SLOTS, reads=[0] * SLOTS, convs=0, tiles=0)
    two = (1, 2)
    p_in = Phase(plan, 1, [(2, 1), (1, 1)], 0, 0)
    p_gate = Phase(plan, 1, [(1, 1)], 1, 1)
    p_ml = Phase(plan, 4, [two] * 4, 8, 8)
    p_mo = Phase(plan, 4, [two] * 3, 6, 6)
    p_d0 = Phase(plan, 1, [(4, 1)] * 2, 0, 0)
    p_d = Phase(plan, NB - 1, [(4, 1)] * 4, 0, 0, (0, 1, 0, 2))
    p_d8 = Phase(plan, 1, [(4, 1)] * 2, 0, 0, (0, 2))
    p_mx = Phase(plan, 8, [two, two, (2, 2)], 6, 4)
    p_wo = Phase(plan, 4, [two] * 2, 4, 4)
    p_min = Phase(plan, 1, [(2, 1)], 0, 0)
    p_mem = Phase(plan, 1, [two] * 4, 8, 8)
    p_xq = Phase(plan, 1, [two] * 2, 4, 4)
    p_xk = Phase(plan, 1, [(1, 1)] * 2, 0, 0)
    p_xv = Phase(plan, 1, [(1, 1)] * 2, 0, 0)
    p_xo = Phase(plan, 1, [two] * 2, 4, 0)
    p_up, p_dn = [], []
    for _ in range(2):
        p_up.append(Phase(plan, FH // 2, [two] * 2, 4, 4))
        p_dn.append(Phase(plan, 8, [two] * 2, 4, 2))

    ctx = ExitStack()
    with ctx:
        arena_at = (nc.sbuf_base + 31) // 32 * 32
        top = [arena_at]

        def at(name, shape, offset, dt=F32):
            return nc.alloc_sbuf_tensor_at(name, shape, dt, offset=offset)

        def put(name, shape, dt=F32):
            off = top[0]
            n = 4 * int(np.prod(shape[1:]))
            top[0] = off + (n + 31) // 32 * 32
            assert top[0] <= nc.sbuf_usable_end, (name, top[0])
            return at(name, shape, off, dt)

        def sem(name):
            return ctx.enter_context(nc.semaphore(name))

        raw = [put(f"raw{s}", [P, UNIT]) for s in range(SLOTS)]
        wh = [put(f"w_hi{s}", [P, KT, P], F32R) for s in range(2)]
        wl = [put(f"w_lo{s}", [P, KT, P], F32R) for s in range(2)]
        xT = put("xT", [P, KT, NT])
        xh, xl = put("xn_hi", [P, KT, NT], F32R), put("xn_lo", [P, KT, NT], F32R)
        blob = put("consts", [P, CW])
        ones = put("ones", [P, P])
        grow = put("gain_rows", [88, P])
        gains = put("gains", [P, 88])
        bif = put("b_if", [16, 1])
        K = {}
        off = 0
        for name, w in CONST.items():
            K[name] = blob[:, off:off + w]
            off += w
        ident = K["ident"]
        free0 = top[0]
        hmh, hml = put("hm_hi", [P, H, NT], F32R), put("hm_lo", [P, H, NT], F32R)
        ha0 = top[0]
        hah, hal = put("ha_hi", [P, H, NT], F32R), put("ha_lo", [P, H, NT], F32R)
        s0 = top[0]

        top[0] = free0
        sq = put("n_sq", [P, 2, NT])
        ntmp = put("n_tmp", [P, 2, NT])
        nms, nr, nu = put("n_ms", [P, NT]), put("n_r", [P, NT]), put("n_u", [P, NT])

        top[0] = ha0
        htmp = put("m_htmp", [P, 2, NT])
        gT = at("m_gT", [16, NT], ha0)
        arow = at("m_arow", [H, 2, NT], ha0)
        gtok = put("m_gtok", [P, 3, 16])
        lf, btok, atok, m0tok, mt = [put(f"m_{n}", [P, 3, H]) for n in ("lf", "b", "a", "m0", "mt")]
        aT = put("m_aT", [H, NT])
        m0bc = put("m_m0bc", [P, NB * H])
        n0raw, n0T, nnew = put("m_n0", [64, P]), put("m_n0T", [P, 64]), put("m_nnew", [P, 64])
        nP = put("m_nP", [P, H])
        noutS, noutP = put("m_noutS", [64, P]), put("m_noutP", [H, P])
        mq, mk, mv, mo = [put(f"m_{n}T", [P, 2, NT]) for n in "qkvo"]
        mK, mV = put("m_Ktok", [P, 3, 2, P]), put("m_Vtok", [P, 3, 2, P + 1])
        C0 = put("m_C0", [P, 2, NB, P])
        vexp = put("m_vexp", [32, NB, P])
        X, swt = put("m_X", [P, 2, 416]), put("m_SwT", [P, 2, 416])
        hs = put("m_hs", [P, 3, 2, P + 1])
        kw = put("m_kw", [P, 2, 2, P])
        gm, g, ng, wprev, emm, wend, den, rden, rd2, ss, sc = [put(f"m_s{n}", [P, 3, 2]) for n in range(11)]
        decay = put("m_decay", [P, 2, NB])
        gl8, qn8, wsel = put("m_gl8", [32, 2, NB]), put("m_qn8", [32, 2, NB]), put("m_wsel", [32, 2, NB])
        qn = put("m_qn", [32, 2])
        qc, tq = put("m_qc", [P, 2, 32]), put("m_tq", [32, 2, P])
        cP = put("m_cP", [P, 2, P + 1])
        ntA = put("m_ntA", [P, 2, NB])

        top[0] = s0
        qs, ks = put("a_qs", [P, H, NS]), put("a_ks", [P, H, NS])
        Vs = put("a_Vs", [NS, H, P])
        aq, ak, av = [put(f"a_{n}T", [P, 2, NT]) for n in "qkv"]
        pX, pXT = put("a_P", [P, 2, 384]), put("a_PT", [P, 2, 384])
        kst, vst = put("a_kst", [P, 3, 2, P]), put("a_vst", [P, 3, 2, P])
        arm, asum = put("a_max", [P, 2, 2]), put("a_sum", [P, 2, 2])
        atmp = put("a_tmp", [P, 2, TP])

        dtab = put("d_table", [NS, PAST + OWN + NS])
        ptab = put("d_pages", [1, NB * PAGES], I32)
        moba_end = top[0]
        top[0] = s0 + 4 * (2 * H * NS + H * P)
        KTb = [put(f"d_KT{n}", [P, 4, P]) for n in range(2)]
        hsd = put("d_h", [P, H, NS])
        qpad = put("d_qpad", [P, H * (NS + TS)])
        gs, geq, pen = put("d_gate", [NS, BLOCKS]), put("d_eq", [NS, BLOCKS]), put("d_pen", [NS, BLOCKS])
        dmn, dmx, dsum = put("d_min", [NS, 1]), put("d_max", [NS, 1]), put("d_sum", [NS, 1])
        DP = put("d_P", [NS, PAST + NS])
        PT = put("d_PT", [P, PAGES + 1, NS])
        hrow = put("d_hrow", [NS, H * P])
        assert top[0] <= moba_end - 4 * (PAST + OWN + NS) - 4 * NB * PAGES

        top[0] = s0
        U = put("x_u", [P, KT, NT])
        sg = put("x_gates", [P, 4, NT])
        ut = put("x_tmp", [P, 2, NT])

        top[0] = s0
        memT = put("c_memT", [P, KT, MEM])
        top[0] = ha0
        mkT, mvT = put("c_mkT", [P, XH, MEM]), put("c_mvT", [P, XH, MEM])
        mKt, mVt = put("c_mKtok", [P, 2, XH * DH]), put("c_mVtok", [P, 2, XH * DH])
        top[0] = s0
        xP, xPT = put("c_P", [P, XH, 2, MEM]), put("c_PT", [P, XH, 2 * MEM])
        octx = put("c_ctx", [P, XH, NT])
        ctxh, ctxl = put("c_ctx_hi", [P, XH, NT], F32R), put("c_ctx_lo", [P, XH, NT], F32R)
        xmx, xsm = put("c_max", [P, XH, 2]), put("c_sum", [P, XH, 2])
        smx, ssm = put("c_smax", [P, 1]), put("c_ssum", [P, 1])
        top[0] = free0
        xq = put("c_qT", [P, XH, NT])
        xKT = [put(f"c_KT{n}", [P, 4, P]) for n in range(2)]
        xST, xDP, xPTs = [put(f"c_{n}", [P, 2, P]) for n in ("ST", "Ps", "PTs")]

        top[0] = free0
        fah, fal = put("f_hi", [P, FH, NT], F32R), put("f_lo", [P, FH, NT], F32R)
        fg, fe, fa = [put(f"f_{n}", [P, 2, NT]) for n in ("g", "e", "a")]
        yout = at("y_tok", [P, 3, D], arena_at)

        B = [ctx.enter_context(nc.psum_tensor(f"bank{b}", [P, 512], F32)) for b in range(8)]
        G = B[0:2]

        PARAMS = 16 * 13
        ML_DVE, MO_DVE = 38, 7
        sqb = X[:].rearrange("p h c -> p (h c)")[:, 0:768].rearrange("p (r h c) -> p r h c", r=3, h=2)

        def sems(prefix, names):
            return [sem(prefix + n) for n in names.split()]
        const_in, ones_set, params_in, outs = sems("", "const_in ones_set params_in small_outputs_stored")
        landed = [sem(f"raw_landed{s}") for s in range(SLOTS)]
        slot_read = [sem(f"slot_read{s}") for s in range(SLOTS)]
        hi_ready, gemm_done = sems("", "hi_ready gemm_done")
        evac_done = [sem(f"evac_done{b}") for b in range(2)]
        tp_done, tp_even, tp_odd, gains_t, gains_set = sems("", "tp_done tp_even_copied tp_odd_copied gains_transposed gains_set")
        sq_ready, sq_used, ms_ready, ln_ready, r_ready, nt_ready, nh_ready, xn_ready = sems(
            "norm_", "sq_ready sq_used ms_ready ln_ready r_ready tmp_ready hi_ready xn_ready")
        dch, ach, pch = sems("", "dve_order act_order pool_order")
        g_t, g_tok, g_abs, g_lf, g_cum, g_a, g_aT, g_aTs = sems(
            "gate_", "transposed tokens softplus lf cumsum a aT aT_copied")
        (m_mem, m_zero, m_arow, m_s1, m_g, m_em, m_w, m_qc, m_ktr, m_kc, m_gl, m_gls, m_we, m_sw, m_s2, m_swt, m_tq, m_kw,
         m_vx, m_s3, m_hs, m_sq, m_ms, m_sc, m_hsr, m_s4, m_tmp, m_hi, m_lo, m_cadd, m_cp, m_cdec, m_c0in, m_c0s,
         m_cps, m_vtr, m_vc, m_n, m_nt, m_no) = sems("m_", "buffers_set m0_zeroed arow scores g_ready em_ready "
            "w_ready qc_copied k_transposed k_copied glast_psum glast_exponents wend_ready sw_ready sw_transposed swt_copied "
            "tq_ready kw_ready vexp_ready numerators numerators_copied squares meansq rstd h_scaled "
            "h_transposed tmp_ready h_hi h_lo c_added cp_ready c_decayed c_in c_stored cp_stored v_transposed v_copied "
            "n_ready n_transposed n_out_ready")
        (a_s1, a_x, a_p, a_pn, a_ptr, a_ptc, a_pv, a_tmp, a_hi, a_lo, a_ktr, a_kc, a_vtr, a_vc, a_ks, a_vs, a_vcp) = sems(
            "a_", "scores x_ready p_ready p_scaled p_transposed pt_copied pv tmp_ready h_hi h_lo k_transposed k_copied "
            "v_transposed v_copied k_stored v_stored v_sample_copied")
        (d_tab, d_pg, d_q, d_tr, d_ss, d_kta, d_ktd, d_sc, d_sm, d_p, d_pn, d_ptr, d_ptc, d_pva, d_pvb, d_va, d_vb, d_ht, d_h,
         d_hi, d_lo) = sems("d_", "table_in pages_in q_ready k_transposed scores_done k_copied_even k_copied_odd scores_of_batch "
            "exponents_ready p_ready p_scaled p_transposed pt_copied pv_first_heads pv_last_heads "
            "h_rows_first h_rows_last h_transposed h_ready h_hi h_lo")
        x_p, x_pe, x_uhi, x_ulo = sems("x_", "products products_read u_hi u_lo")
        (c_kvt, c_kvc, c_out, c_s, c_x, c_p, c_pn, c_ptr, c_ptc, c_pv,
         c_sc, c_st, c_rows, c_sx, c_sp, c_spn, c_spt, c_spc, c_spv, c_ctx, c_chi, c_clo, c_xo) = sems("c_",
            "kv_transposed kv_copied kv_stored scores x_ready p_ready p_scaled p_transposed "
            "pt_copied pv s_scores_done s_copied s_rows s_x_ready "
            "s_p_ready s_p_scaled s_p_transposed s_pt_copied s_pv ctx_ready ctx_hi ctx_lo xo_added")
        f_a, f_hi, f_lo = sems("f_", "a_ready hi lo")
        y_r, y_out = sems("y_", "rows_ready stored")
        block = ctx.enter_context(nc.Block())
        w_in = a["w_in"].rearrange("l (t p) n -> p (l t) n", p=P)

        def src256(s, j):
            return raw[s][:].rearrange("p (k c) -> p k c", c=256)[:, :, j * P:(j + 1) * P]

        def like(half, src):
            k, c = src.shape[1:]
            return half[:].rearrange("p k c -> p (k c)")[:, 0:k * c].rearrange("p (k c) -> p k c", c=c)

        def tok3(bank):
            return bank[:, 0:384].rearrange("p (r c) -> p r c", c=P)

        def xo_src(j):
            return raw[p_xo.slot(j // 2)][:].rearrange("p (k c) -> p k c", c=1024)[:, :, (j % 2) * 512:(j % 2) * 512 + 512]

        gate_src = raw[0][:, 0:KT * P].rearrange("p (k c) -> p k c", c=P)

        @block.sync
        def _(sp):
            sp.dma_start(blob[:], a["blob"]).then_inc(const_in, 16)

            def load(ph, i, u, dst, src):
                s = ph.slot(u)
                hold(sp, slot_read[s], ph.reads(i, u))
                sp.dma_start(dst, src).then_inc(landed[s], 16)

            def full(ph, u):
                return raw[ph.slot(u)][:].rearrange("p (k c) -> p k c", c=256)

            xp = a["x_prompt"].rearrange("b (t p) d -> (b t) p d", p=P)
            for t in range(2):
                sp.dma_start(raw[0][:, t * D:(t + 1) * D], xp[t]).then_inc(landed[0], 16)
            sp.dma_start(raw[1][0:NS, 0:D], a["x_sample"].rearrange("b t d -> (b t) d")).then_inc(landed[1], 16)
            for n, name in enumerate(("norm_mix", "norm_xattn", "norm_mem", "norm_ffn")):
                sp.dma_start(grow[16 * n:16 * n + 16, :], a[name].rearrange("l (k p) -> (l k) p", p=P)).then_inc(params_in, 16)
            sp.dma_start(grow[64:80, :], a["norm_final"].rearrange("(k p) -> k p", p=P)).then_inc(params_in, 16)
            sp.dma_start(grow[80:88, :], a["mh_gain"].rearrange("l (k p) -> (l k) p", p=P)).then_inc(params_in, 16)
            sp.dma_start(bif[:], a["b_if"].rearrange("l (k a) -> (l k) a", a=1)).then_inc(params_in, 16)
            sp.dma_start(n0raw[:], a["state_n"].rearrange("l b h d -> (l b h) d")).then_inc(params_in, 16)
            sp.dma_start(m0bc[:], a["state_m"].rearrange("l b h -> (l b h)").partition_broadcast(P)).then_inc(params_in, 16)
            sp.wait_ge(m_zero, 1)
            for t in range(TS):
                sp.dma_start(m0tok[t:NS:TS, 2, :], a["state_m"][0]).then_inc(params_in, 16)
            load(p_gate, 0, 0, gate_src, w_in[:, :, W_IF:W_IF + P])

            def ml(i):
                for u, part in enumerate((2, 0, 1, 3)):
                    load(p_ml, i, u, full(p_ml, u), w_in[:, :, ds(i * 256 + part * H * DH, 256)])

            def mo_(i):
                for u, part in enumerate((2, 0, 1)):
                    load(p_mo, i, u, full(p_mo, u), w_in[:, :, ds(i * 256 + (W_QA + part * H * DH), 256)])
            ml(0)
            with sp.Fori(1, 4) as i:
                ml(i)
            with sp.Fori(0, 4) as i:
                mo_(i)

            sp.wait_ge(a_s1, 1)
            sp.dma_start(dtab[:], a["dec"]).then_inc(d_tab, 16)
            sp.dma_start(ptab[:], a["page_table"].rearrange("b n -> (b n)").unsqueeze(0)).then_inc(d_pg, 16)
            sp.wait_ge(d_pg, 16)

            def pages(ph, i, u, b, first, cache):
                s = ph.slot(u)
                hold(sp, slot_read[s], ph.reads(i, u))
                for n in range(4):
                    page = sp.value_load(ptab[0:1, ds(b * PAGES + (first + n), 1)], min_val=0, max_val=N_PHYS - 1)
                    sp.dma_start(raw[s][:, n * H * DH:(n + 1) * H * DH],
                                 cache[0, ds(page, 1)].rearrange("a t h d -> (a t) (h d)")).then_inc(landed[s], 16)
            for u in range(2):
                pages(p_d0, 0, u, 0, 4 * u, a["cache_k"])
            with sp.Fori(1, NB) as b:
                for u in range(2):
                    pages(p_d, b - 1, u, b, 4 * u, a["cache_k"])
                for u in range(2):
                    pages(p_d, b - 1, 2 + u, b - 1, 4 * u, a["cache_v"])
            for u in range(2):
                pages(p_d8, 0, u, NB - 1, 4 * u, a["cache_v"])

            def wt(name):
                return a[name].rearrange("l (t p) n -> p (l t) n", p=P)
            w_pm, w_pa, w_out = wt("w_proj_m"), wt("w_proj_a"), wt("w_out")
            with sp.Fori(0, 8) as i:
                load(p_mx, i, 0, full(p_mx, 0), w_in[:, :, ds(i * 256 + W_GM, 256)])
                load(p_mx, i, 1, full(p_mx, 1), w_in[:, :, ds(i * 256 + W_GA, 256)])
                load(p_mx, i, 2, full(p_mx, 2)[:, 0:8], w_pm[:, :, ds(i * 256, 256)])
                sp.dma_start(full(p_mx, 2)[:, 8:16], w_pa[:, :, ds(i * 256, 256)]).then_inc(landed[p_mx.slot(2)], 16)
            with sp.Fori(0, 4) as i:
                for u in range(2):
                    load(p_wo, i, u, full(p_wo, u), w_out[:, :, ds(i * 512 + u * 256, 256)])

            mp = a["mem_prompt"].rearrange("b (t p) d -> (b t) p d", p=P)
            load(p_min, 0, 0, raw[0][:, 0:D], mp[0])
            sp.dma_start(raw[0][:, D:2 * D], mp[1]).then_inc(landed[0], 16)
            for u in range(4):
                load(p_mem, 0, u, full(p_mem, u), wt(("w_xv", "w_xk")[u // 2])[:, :, (u % 2) * 256:(u % 2) * 256 + 256])
            for u in range(2):
                load(p_xq, 0, u, full(p_xq, u), wt("w_xq")[:, :, u * 256:u * 256 + 256])
            for ph, name in ((p_xk, "cache_mem_k"), (p_xv, "cache_mem_v")):
                for u in range(2):
                    load(ph, 0, u, raw[ph.slot(u)][:].rearrange("p (b c) -> p b c", c=XH * DH),
                         a[name][0, 4 * u:4 * u + 4].rearrange("b (m p) h d -> p (b m) (h d)", p=P))
            for u in range(2):
                load(p_xo, 0, u, raw[p_xo.slot(u)][:].rearrange("p (k c) -> p k c", c=1024), wt("w_xo")[:, :, u * 1024:(u + 1) * 1024])
            w_g, w_u, w_d = wt("w_ffn_gate"), wt("w_ffn_up"), wt("w_ffn_down")
            for f in range(2):
                with sp.Fori(0, FH // 2) as i:
                    load(p_up[f], i, 0, full(p_up[f], 0), w_g[:, :, ds(i * 256 + f * FH * P, 256)])
                    load(p_up[f], i, 1, full(p_up[f], 1), w_u[:, :, ds(i * 256 + f * FH * P, 256)])
                with sp.Fori(0, 8) as i:
                    for u in range(2):
                        k0 = f * FH + u * FU
                        load(p_dn[f], i, u, full(p_dn[f], u)[:, 0:FU], w_d[:, k0:k0 + FU, ds(i * 256, 256)])

        @block.gpsimd
        def _(gp):
            nc.gpsimd.memset(ones[:], 1.0).then_inc(ones_set, 1)
            nc.gpsimd.memset(m0tok[:], 0.0).then_inc(m_zero, 1)
            for buf in (gtok, gm, wend, hs):
                nc.gpsimd.memset(buf[:], 0.0)
            nc.gpsimd.memset(mV[:], 1.0).then_inc(m_mem, 1)
            cs = a["state_C"].rearrange("l b h k v -> k (l h) b v")
            co = o["C_sample"].rearrange("l b h k v -> k (l h) b v")
            cpo = o["C_prompt"].rearrange("l b h k v -> k (l b h) v")

            def load_c(i):
                for hh in range(2):
                    gp.dma_start(C0[:, hh, :, :], cs[:, ds(2 * i + hh, 1), :, :].rearrange("k h b v -> k (h b) v")).then_inc(m_c0in, 16)

            def update(i):
                hold(gp, m_s1, i + 1)
                hold(gp, m_we, 2 * i + 2)
                for hh in range(2):
                    nc.gpsimd.tensor_tensor(C0[:, hh, :, :], C0[:, hh, :, :], decay[:, hh, :].unsqueeze(2).broadcast_to([P, NB, P]),
                                            ALU.mult).then_inc(m_cdec, 1)
                hold(gp, m_cp, i + 1)
                gp.dma_start(cpo[:, ds(2 * i, 2), :], cP[:, :, 0:P]).then_inc(m_cps, 16)
                for hh in range(2):
                    hold(gp, m_cadd, 2 * i + hh + 1)
                    gp.dma_start(co[:, ds(2 * i + hh, 1), :, :].rearrange("k h b v -> k (h b) v"), C0[:, hh, :, :]).then_inc(m_c0s, 16)
            load_c(0)
            with gp.Fori(0, 3) as i:
                update(i)
                hold(gp, m_c0s, 32 * i + 32)
                load_c(i + 1)
            update(3)
            gp.wait_ge(m_no, 2)
            gp.dma_start(o["m_prompt"].rearrange("l b h -> (l b) h"), mt[P - 1:P, 1, :]).then_inc(outs, 16)
            gp.dma_start(o["m_sample"].rearrange("l b h -> (l b) h"), mt[TS - 1:NS:TS, 2, :]).then_inc(outs, 16)
            gp.dma_start(o["n_sample"].rearrange("l b h d -> (l b h) d"), noutS[:]).then_inc(outs, 16)
            gp.dma_start(o["n_prompt"].rearrange("l b h d -> (l b h) d"), noutP[:]).then_inc(outs, 16)

            def store_kv(i, ready, stored, st, op, os_):
                hold(gp, ready, i + 1)
                for t in range(2):
                    gp.dma_start(op[0, 0, t * P:(t + 1) * P, ds(2 * i, 2), :], st[:, t, :, :]).then_inc(stored, 16)
                gp.dma_start(os_.rearrange("l b t h d -> (l b t) h d")[:, ds(2 * i, 2), :], st[0:NS, 2, :, :]).then_inc(stored, 16)
            with gp.Fori(0, 4) as i:
                store_kv(i, a_vc, a_vs, vst, o["v_prompt"], o["v_sample"])
                nc.gpsimd.tensor_copy(Vs[:, ds(2 * i, 2), :], vst[0:NS, 2, :, :]).then_inc(a_vcp, 1)
                store_kv(i, a_kc, a_ks, kst, o["k_prompt"], o["k_sample"])
            gp.wait_ge(c_kvc, 4)
            for st, name in ((mVt, "mem_v_prompt"), (mKt, "mem_k_prompt")):
                for t in range(2):
                    gp.dma_start(o[name][0, 0, t * P:(t + 1) * P].rearrange("t h d -> t (h d)"), st[:, t, :]).then_inc(c_out, 16)
            yp = o["y_prompt"].rearrange("b (t p) d -> (b t) p d", p=P)
            for t in range(3):
                gp.wait_ge(tp_even, 9 + 2 * t + 2)
                gp.wait_ge(tp_odd, 8 + 2 * t + 2)
                dst = yp[t] if t < 2 else o["y_sample"].rearrange("b t d -> (b t) d")
                gp.dma_start(dst, yout[0:(P, P, NS)[t], t, :]).then_inc(y_out, 16)
            gp.wait_ge(c_out, 64)
            gp.wait_ge(y_out, 48)
            gp.wait_ge(m_c0s, 128)
            gp.wait_ge(m_cps, 64)
            gp.wait_ge(a_ks, 16 * 12)
            gp.wait_ge(a_vs, 16 * 12)
            gp.wait_ge(outs, 64)

        @block.scalar
        def _(act):
            ac = Chain(act, ach)

            def hi(ph, i, u, c, src):
                act.wait_ge(landed[ph.slot(u)], ph.landed(i, u))
                wait(act, gemm_done, ph.conv(i, c - 1))
                nc.scalar.activation(like(wh[ph.half(c)], src), src, ACT.Copy).then_inc(hi_ready, 1)

            def norm(q, src, n):
                for k in range(KT):
                    wait(act, sq_used, KT * q + k - 1)
                    nc.scalar.activation(sq[:, k % 2, 0:n], src[:, k, :], ACT.Square).then_inc(sq_ready, 1)
                act.wait_ge(ms_ready, q + 1)
                nc.scalar.activation(nu[:, 0:n], nms[:, 0:n], ACT.Ln).then_inc(ln_ready, 1)
                act.wait_ge(ln_ready, q + 1)
                nc.scalar.activation(nr[:, 0:n], nu[:, 0:n], ACT.Exp, scale=-0.5).then_inc(r_ready, 1)

            def norm_hi(q, n):
                for k in range(KT):
                    act.wait_ge(nt_ready, KT * q + k + 1)
                    nc.scalar.activation(xh[:, k, 0:n], ntmp[:, k % 2, 0:n], ACT.Copy).then_inc(nh_ready, 1)

            for n in (0, 2, 4, 6, 8):
                act.wait_ge(tp_done, n + 1)
                if n < 8:
                    t, k4 = n // 4, n % 4
                    nc.scalar.activation(xT[:, 4 * k4:4 * k4 + 4, t * P:(t + 1) * P],
                                         B[2 + n % 4][:].rearrange("p (k c) -> p k c", c=P), ACT.Copy).then_inc(tp_even, 1)
                else:
                    nc.scalar.activation(xT[:, :, TP:NT], B[2][:].rearrange("p (k c) -> p k c", c=NS), ACT.Copy).then_inc(tp_even, 1)
            act.wait_ge(tp_even, 5)
            act.wait_ge(tp_odd, 4)
            norm(0, xT, NT)
            norm_hi(0, NT)

            hi(p_gate, 0, 0, 0, gate_src)
            act.wait_ge(params_in, PARAMS)
            act.wait_ge(gemm_done, 1)
            nc.scalar.activation(gT[:], G[0][0:16, 0:NT], ACT.Identity, bias=bif[:]).then_inc(evac_done[0], 1)
            act.wait_ge(g_tok, 1)
            ac.run(nc.scalar.activation(lf[:], gtok[:, :, H:2 * H], ACT.Abs))
            ac.sync()
            ac.run(nc.scalar.activation(lf[:], lf[:], ACT.Exp, scale=-1.0))
            ac.sync()
            nc.scalar.activation(lf[:], lf[:], ACT.Ln, bias=1.0).then_inc(g_abs, 1)

            def ml_evac(i, t):
                u, hh = t // 2, t % 2
                act.wait_ge(gemm_done, p_ml.conv(i, t + 1))
                src = G[p_ml.bank(t)][:, 0:NT]
                if u == 3:
                    ins = nc.scalar.activation(mo[:, hh, :], src, ACT.Exp, scale=-1.0)
                else:
                    ins = nc.scalar.activation((mv, mq, mk)[u][:, hh, :], src, ACT.Copy, scale=SCALE if u == 2 else 1.0)
                ins.then_inc(evac_done[p_ml.bank(t)], 1)

            def ml_attn(p, j):
                if j == 0:
                    act.wait_ge(m_g, p + 1)
                    nc.scalar.activation(wprev[:], wprev[:], ACT.Exp).then_inc(m_em, 1)
                    nc.scalar.activation(emm[:], emm[:], ACT.Exp).then_inc(m_em, 1)
                    for hh in range(2):
                        nc.scalar.activation(X[:, hh, 0:P], X[:, hh, 0:P], ACT.Exp, bias=ng[:, 0, hh:hh + 1])
                        nc.scalar.activation(X[:, hh, P:384], X[:, hh, P:384], ACT.Exp, bias=ng[:, 1, hh:hh + 1])
                        nc.scalar.activation(X[0:32, hh, 384:416], X[0:32, hh, 384:416], ACT.Exp,
                                             bias=ng[0:32, 2, hh:hh + 1]).then_inc(m_w, 1)
                if j == 1:
                    act.wait_ge(m_gls, p + 1)
                    nc.scalar.activation(wend[:], wend[:], ACT.Exp).then_inc(m_we, 1)
                    nc.scalar.activation(decay[:], decay[:], ACT.Exp).then_inc(m_we, 1)
                    act.wait_ge(m_ktr, p + 1)
                    for hh in range(2):
                        src = tok3(B[7 - hh])
                        nc.scalar.activation(mK[:, 0:2, hh, :], src[:, 0:2, :], ACT.Copy)
                        nc.scalar.activation(mK[0:32, 2, hh, :], src[0:32, 2, :], ACT.Copy).then_inc(m_kc, 1)
                if j == 2:
                    act.wait_ge(m_s2, p + 1)
                    for hh in range(2):
                        nc.scalar.activation(swt[:, hh, 0:384], B[4 + hh][:, 0:384], ACT.Copy)
                        nc.scalar.activation(swt[0:32, hh, 384:416], B[4 + hh][0:32, 384:416], ACT.Copy).then_inc(m_swt, 1)
                if j == 3:
                    act.wait_ge(m_hs, p + 1)
                    nc.scalar.activation(sqb, hs[:, :, :, 0:P], ACT.Square).then_inc(m_sq, 1)
                    act.wait_ge(m_ms, p + 1)
                    ac.run(nc.scalar.activation(ss[:], ss[:], ACT.Ln))
                    ac.sync()
                    nc.scalar.activation(ss[:], ss[:], ACT.Exp, scale=-0.5).then_inc(m_sc, 1)
                if j == 5:
                    act.wait_ge(m_tmp, 2 * p + 2)
                    nc.scalar.activation(hmh[:, ds(2 * p, 2), :], htmp[:], ACT.Copy).then_inc(m_hi, 1)

            def ml_body(i, gemm, attn):
                for j in range(8):
                    if gemm:
                        hi(p_ml, i, j // 2, j, src256(p_ml.slot(j // 2), j % 2))
                        if j >= 2:
                            ml_evac(i, j - 2)
                    if attn:
                        if j < 2:
                            ml_evac(i - 1, 6 + j)
                        ml_attn(i - 1, j)
                    if gemm and j == 5:
                        act.wait_ge(m_vtr, i + 1)
                        for hh in range(2):
                            src = tok3(B[6 + hh])
                            nc.scalar.activation(mV[:, 0:2, hh, 0:P], src[:, 0:2, :], ACT.Copy)
                            nc.scalar.activation(mV[0:32, 2, hh, 0:P], src[0:32, 2, :], ACT.Copy).then_inc(m_vc, 1)
            act.wait_ge(m_mem, 1)
            ml_body(0, True, False)
            with act.Fori(1, 4) as i:
                ac.loop(i - 1, 1)
                ml_body(i, True, True)
            ac.loop(3, 1)
            ml_body(4, False, True)
            ac.end(4)

            def mo_evac(i, t):
                u, hh = t // 2, t % 2
                act.wait_ge(gemm_done, p_mo.conv(i, t + 1))
                src = G[p_mo.bank(t)]
                scale = SCALE if u == 1 else 1.0
                if u:
                    nc.scalar.activation((qs, ks)[u - 1][:, ds(2 * i + hh, 1), :], src[:, TP:NT].unsqueeze(1), ACT.Copy, scale=scale)
                nc.scalar.activation((av, aq, ak)[u][:, hh, :], src[:, 0:NT], ACT.Copy, scale=scale).then_inc(evac_done[p_mo.bank(t)], 1)

            def tok_copy(transposed, n, banks, dst, copied):
                act.wait_ge(transposed, n)
                for hh in range(2):
                    src = tok3(banks[hh])
                    nc.scalar.activation(dst[:, 0:2, hh, :], src[:, 0:2, :], ACT.Copy)
                    last = nc.scalar.activation(dst[0:32, 2, hh, :], src[0:32, 2, :], ACT.Copy)
                last.then_inc(copied, 1)

            def mo_attn(p, j):
                if j == 2:
                    act.wait_ge(a_x, p + 1)
                    for hh in range(2):
                        nc.scalar.activation(pX[:, hh, 0:P], pX[:, hh, 0:P], ACT.Exp, bias=arm[:, hh, 0:1], accum_out=asum[:, hh, 0:1])
                        last = nc.scalar.activation(pX[:, hh, P:384], pX[:, hh, P:384], ACT.Exp, bias=arm[:, hh, 1:2], accum_out=asum[:, hh, 1:2])
                    last.then_inc(a_p, 1)
                if j == 3:
                    act.wait_ge(a_ptr, p + 1)
                    for hh in range(2):
                        last = nc.scalar.activation(pXT[:, hh, :], B[4 + hh][:, 0:384], ACT.Copy)
                    last.then_inc(a_ptc, 1)
                    tok_copy(a_ktr, p + 1, (B[7], B[2]), kst, a_kc)
                if j == 4:
                    act.wait_ge(a_tmp, p + 1)
                    nc.scalar.activation(hah[:, ds(2 * p, 2), 0:TP], atmp[:], ACT.Copy).then_inc(a_hi, 1)
                if j == 5:
                    act.wait_ge(a_ks, 48 * p + 48)

            def mo_body(i, gemm, attn):
                for j in range(6):
                    if gemm:
                        hi(p_mo, i, j // 2, j, src256(p_mo.slot(j // 2), j % 2))
                        if j == 2 and not attn:
                            act.wait_ge(m_c0s, 128)
                            act.wait_ge(m_cps, 64)
                            act.wait_ge(outs, 64)
                        if j >= 2:
                            mo_evac(i, j - 2)
                    if attn:
                        if j < 2:
                            mo_evac(i - 1, 4 + j)
                        mo_attn(i - 1, j)
                    if gemm and j == 5:
                        wait(act, a_vs, 48 * i)
                        wait(act, a_vcp, i)
                        tok_copy(a_vtr, i + 1, (B[4], B[5]), vst, a_vc)
            mo_body(0, True, False)
            with act.Fori(1, 4) as i:
                mo_body(i, True, True)
            mo_body(4, False, True)

            def k_copies(kts, tr_sem, ss_sem, mine, base, i, parity, copy, between=None):
                for n in range(parity, 16, 2):
                    act.wait_ge(tr_sem, i * 16 + (base + n + 1))
                    act.wait_ge(ss_sem, i * 16 + (base + n + 1))
                    copy(kts[n % 2][:], B[2 + n % 4][:].rearrange("p (h c) -> p h c", c=P)).then_inc(mine, 1)
                    if n == 4 and between:
                        between()

            def a_copy(dst, src):
                return nc.scalar.activation(dst, src, ACT.Copy)

            def d_batch(b, k, v):
                def pt_copy():
                    act.wait_ge(d_ptr, b)
                    a_copy(PT[:, 0:PAGES, :], B[0][:, 0:PAGES * NS].rearrange("p (n c) -> p n c", c=NS))
                    a_copy(PT[0:NS, PAGES, :], B[0][0:NS, PAGES * NS:(PAGES + 1) * NS]).then_inc(d_ptc, 1)
                if k:
                    k_copies(KTb, d_tr, d_ss, d_kta, 0, b, 0, a_copy, pt_copy if v else None)
                    act.wait_ge(d_sm, b + 1)
                    nc.scalar.activation(DP[:], DP[:], ACT.Exp, bias=dmx[:], accum_out=dsum[:]).then_inc(d_p, 1)
                else:
                    pt_copy()
                if v:
                    act.wait_ge(d_pva, b)
                    a_copy(hrow[:, 0:4 * P], B[2][0:NS, :]).then_inc(d_va, 1)
            d_batch(0, True, False)
            with act.Fori(1, NB) as b:
                d_batch(b, True, True)
            d_batch(NB, False, True)
            act.wait_ge(d_h, NB + 1)
            a_copy(hah[:, :, TP:NT], hsd[:]).then_inc(d_hi, 1)

            def mx_evac(i, t):
                act.wait_ge(gemm_done, p_mx.conv(i, t + 1))
                nc.scalar.activation(sg[:, t, :], G[p_mx.bank(t)][:, 0:NT], ACT.Exp, scale=-1.0).then_inc(evac_done[p_mx.bank(t)], 1)

            def mx_body(i):
                for j in range(6):
                    hi(p_mx, i, j // 2, j, src256(p_mx.slot(j // 2), j % 2))
                    if j == 2:
                        act.wait_ge(x_pe, 4 * i + 4)
                    if j >= 2:
                        mx_evac(i, j - 2)
            with act.Fori(0, 8) as i:
                mx_body(i)
            act.wait_ge(x_pe, 4 * 8 + 4)
            for q in range(4):
                a_copy(xh[:, 4 * q:4 * q + 4, :], U[:, 4 * q:4 * q + 4, :]).then_inc(x_uhi, 1)
            with act.Fori(0, 4) as i:
                for j in range(4):
                    hi(p_wo, i, j // 2, j, src256(p_wo.slot(j // 2), j % 2))

            for n in (0, 2, 4, 6):
                act.wait_ge(tp_done, 9 + n + 1)
                t, k4 = n // 4, n % 4
                a_copy(memT[:, 4 * k4:4 * k4 + 4, t * P:(t + 1) * P], B[2 + n % 4][:].rearrange("p (k c) -> p k c", c=P)).then_inc(tp_even, 1)
            act.wait_ge(tp_even, 5 + 4)
            act.wait_ge(tp_odd, 4 + 4)
            norm(1, memT, MEM)
            norm_hi(1, MEM)
            for j in range(10):
                if j < 8:
                    hi(p_mem, 0, j // 2, j, src256(p_mem.slot(j // 2), j % 2))
                if j >= 2:
                    act.wait_ge(gemm_done, p_mem.conv(0, j - 1))
                    t = j - 2
                    a_copy((mvT, mkT)[t // 4][:, t % 4, :], G[p_mem.bank(t)][:, 0:MEM]).then_inc(evac_done[p_mem.bank(t)], 1)
            for n in range(4):
                act.wait_ge(c_kvt, n + 1)
                a_copy((mVt, mKt)[n // 2][:, n % 2, :], B[2 + n][:]).then_inc(c_kvc, 1)

            norm(2, xT, NT)
            norm_hi(2, NT)
            for j in range(6):
                if j < 4:
                    hi(p_xq, 0, j // 2, j, src256(p_xq.slot(j // 2), j % 2))
                if j >= 2:
                    t = j - 2
                    act.wait_ge(gemm_done, p_xq.conv(0, t + 1))
                    nc.scalar.activation(xq[:, t, :], G[p_xq.bank(t)][:, 0:NT], ACT.Copy, scale=SCALE).then_inc(evac_done[p_xq.bank(t)], 1)
            act.wait_ge(c_x, 1)
            for h in range(XH):
                for r in range(2):
                    last = nc.scalar.activation(xP[:, h, r, :], xP[:, h, r, :], ACT.Exp, bias=xmx[:, h, r:r + 1], accum_out=xsm[:, h, r:r + 1])
            last.then_inc(c_p, 1)
            act.wait_ge(c_ptr, 1)
            for h in range(XH):
                last = a_copy(xPT[:, h, :], B[2 + h][:])
            last.then_inc(c_ptc, 1)
            k_copies(xKT, d_tr, d_ss, d_kta, 128, 0, 0, a_copy)
            act.wait_ge(c_sx, 1)
            nc.scalar.activation(xDP[:], xDP[:], ACT.Exp, bias=smx[:], accum_out=ssm[:]).then_inc(c_sp, 1)
            act.wait_ge(c_spt, 1)
            a_copy(xPTs[:], B[2][:, 0:2 * P].rearrange("p (m c) -> p m c", c=P)).then_inc(c_spc, 1)
            act.wait_ge(c_ctx, 3)
            a_copy(ctxh[:], octx[:]).then_inc(c_chi, 1)
            for j in range(4):
                hi(p_xo, 0, j // 2, j, xo_src(j))

            act.wait_ge(c_xo, 4)
            act.wait_ge(c_out, 64)
            norm(3, xT, NT)
            norm_hi(3, NT)

            def up_evac(f, i, t):
                ph = p_up[f]
                act.wait_ge(gemm_done, ph.conv(i, t + 1))
                a_copy(fg[:, t, :], G[ph.bank(t)][:, 0:NT])
                nc.scalar.activation(fe[:, t, :], G[ph.bank(t)][:, 0:NT], ACT.Exp, scale=-1.0).then_inc(evac_done[ph.bank(t)], 1)

            def up_hi(f, i):
                act.wait_ge(f_a, i * 2 + (2 + f * FH))
                a_copy(fah[:, ds(i * 2, 2), :], fa[:]).then_inc(f_hi, 1)

            def up_body(f, i, first):
                for j in range(4):
                    hi(p_up[f], i, j // 2, j, src256(p_up[f].slot(j // 2), j % 2))
                    if j == 2 and not first:
                        up_hi(f, i - 1)
                    if j >= 2:
                        up_evac(f, i, j - 2)
            for f in range(2):
                up_body(f, 0, True)
                with act.Fori(1, FH // 2) as i:
                    up_body(f, i, False)
                up_hi(f, FH // 2 - 1)
                with act.Fori(0, 8) as i:
                    for j in range(4):
                        hi(p_dn[f], i, j // 2, j, src256(p_dn[f].slot(j // 2), j % 2)[:, 0:FU])
            act.wait_ge(evac_done[p_dn[1].bank(0)], p_dn[1].evacs(8, 0))
            act.wait_ge(evac_done[p_dn[1].bank(1)], p_dn[1].evacs(8, 1))
            norm(4, xT, NT)
            for n in range(0, 12, 2):
                act.wait_ge(tp_done, 17 + n + 1)
                rows_ = (P, P, NS)[n // 4]
                a_copy(yout[0:rows_, n // 4, (n % 4) * 512:(n % 4) * 512 + 512], B[2 + n % 4][0:rows_, :]).then_inc(tp_even, 1)

        @block.vector
        def _(dve):
            dc = Chain(dve, dch)

            def lo(ph, i, u, c, src):
                dve.wait_ge(hi_ready, ph.conv(i, c + 1))
                nc.vector.tensor_tensor(like(wl[ph.half(c)], src), src, like(wh[ph.half(c)], src).bitcast(F32),
                                        ALU.subtract).then_inc(slot_read[ph.slot(u)], 1)

            def norm(q, n):
                dve.wait_ge(sq_used, KT * (q + 1))
                nc.vector.tensor_scalar(nms[:, 0:n], B[2][:, 0:n], 1.0 / D, EPS, ALU.mult, ALU.add).then_inc(ms_ready, 1)
                dve.wait_ge(r_ready, q + 1)
                dve.wait_ge(ms_ready, q + 1)
                dc.run(nc.vector.tensor_tensor(nu[:, 0:n], nr[:, 0:n], nr[:, 0:n], ALU.mult))
                dc.sync()
                dc.run(nc.vector.tensor_tensor(nu[:, 0:n], nu[:, 0:n], nms[:, 0:n], ALU.mult))
                dc.sync()
                dc.run(nc.vector.tensor_scalar(nu[:, 0:n], nu[:, 0:n], -0.5, 1.5, ALU.mult, ALU.add))
                dc.sync()
                dc.run(nc.vector.tensor_tensor(nr[:, 0:n], nr[:, 0:n], nu[:, 0:n], ALU.mult))
                dc.sync()

            def norm_apply(q, src, gain, n):
                for k in range(KT + 1):
                    if k < KT:
                        nc.vector.scalar_tensor_tensor(ntmp[:, k % 2, 0:n], src[:, k, :], gains[:, gain + k:gain + k + 1],
                                                       nr[:, 0:n], ALU.mult, ALU.mult).then_inc(nt_ready, 1)
                    if k:
                        dve.wait_ge(nh_ready, KT * q + k)
                        nc.vector.tensor_tensor(xl[:, k - 1, 0:n], ntmp[:, (k - 1) % 2, 0:n], xh[:, k - 1, 0:n].bitcast(F32),
                                                ALU.subtract).then_inc(xn_ready, 1)
                        dve.wait_ge(xn_ready, KT * q + k)

            for n in (1, 3, 5, 7):
                dve.wait_ge(tp_done, n + 1)
                t, k4 = n // 4, n % 4
                nc.vector.tensor_copy(xT[:, 4 * k4:4 * k4 + 4, t * P:(t + 1) * P],
                                      B[2 + n % 4][:].rearrange("p (k c) -> p k c", c=P)).then_inc(tp_odd, 1)
            dve.wait_ge(gains_t, 1)
            nc.vector.tensor_copy(gains[:], B[6][:, 0:88]).then_inc(gains_set, 1)
            nc.vector.tensor_copy(n0T[:], B[7][:, 0:64]).then_inc(gains_set, 1)
            dve.wait_ge(gains_set, 2)
            dve.wait_ge(tp_even, 5)
            dve.wait_ge(tp_odd, 4)
            norm(0, NT)
            norm_apply(0, xT, 0, NT)

            lo(p_gate, 0, 0, 0, gate_src)
            dve.wait_ge(g_t, 1)
            dve.wait_ge(m_mem, 1)
            dc.run(nc.vector.tensor_copy(gtok[:, 0:2, :], B[3][:, 0:32].rearrange("p (r c) -> p r c", c=16)))
            nc.vector.tensor_copy(gtok[0:32, 2, :], B[3][0:32, 32:48]).then_inc(g_tok, 1)
            dve.wait_ge(g_tok, 1)
            dve.wait_ge(g_abs, 1)
            dc.sync()
            nc.vector.scalar_tensor_tensor(lf[:], gtok[:, :, H:2 * H], 0.0, lf[:], ALU.min, ALU.subtract).then_inc(g_lf, 1)
            dc.run(nc.vector.memset(btok[:], 0.0))
            dc.sync()
            dve.wait_ge(g_cum, 1)
            dc.run(nc.vector.tensor_copy(btok[:, 0:2, :], B[4][:, 0:16].rearrange("p (r c) -> p r c", c=H)))
            dc.run(nc.vector.tensor_copy(btok[0:32, 2, :], B[4][0:32, 16:24]))
            dc.sync()
            nc.vector.tensor_tensor(atok[:], gtok[:, :, 0:H], btok[:], ALU.subtract).then_inc(g_a, 1)
            dve.wait_ge(g_aT, 1)
            nc.vector.tensor_copy(aT[:], B[5][0:H, 0:NT]).then_inc(g_aTs, 1)
            dve.wait_ge(g_aTs, 1)
            dve.wait_ge(params_in, PARAMS)
            m0v = m0bc[:].rearrange("p (b h) -> p h b", h=H)
            n0v = n0T[:].rearrange("p (b h) -> p h b", h=H)
            nnv = nnew[:].rearrange("p (b h) -> p h b", h=H)

            def ml_arow(p):
                for hh in range(2):
                    nc.vector.tensor_scalar(arow[:, hh, :], aT[:], ident[0:H, ds(2 * p + hh, 1)], None, ALU.mult).then_inc(m_arow, 1)

            def vexp_of(hh):
                nc.vector.tensor_tensor(vexp[:], mV[0:32, 2, hh, 0:P].unsqueeze(1).broadcast_to([32, NB, P]),
                                        wsel[:, hh, :].unsqueeze(2).broadcast_to([32, NB, P]), ALU.mult).then_inc(m_vx, 1)

            def c_add(p, hh):
                dve.wait_ge(m_cdec, 2 * p + hh + 1)
                for q in range(2):
                    half = C0[:, hh, 4 * q:4 * q + 4, :].rearrange("p b v -> p (b v)")
                    last = nc.vector.tensor_tensor(half, half, B[4 + q][:, :], ALU.add)
                last.then_inc(m_cadd, 1)

            def ml_attn(p, j):
                pair = ds(2 * p, 2)
                if j == 0:
                    dve.wait_ge(m_s1, p + 1)
                    dc.run(nc.vector.tensor_copy(qc[:], B[6][:, 0:64].rearrange("p (h c) -> p h c", h=2)))
                    dc.run(nc.vector.tensor_tensor(qn8[:], B[6][0:32, 64:80].rearrange("p (h b) -> p h b", b=NB),
                                                   K["bmask"][0:32].unsqueeze(1).broadcast_to([32, 2, NB]), ALU.mult))
                    for hh in range(2):
                        A = B[4 + hh]
                        dc.run(nc.vector.tensor_tensor_reduce(out=X[:, hh, 0:P], in0=A[:, 0:P], in1=K["cadd"][:, 0:P], scale=1.0,
                                                              scalar=NEG, op0=ALU.add, op1=ALU.max, accum_out=gm[:, 0, hh:hh + 1]))
                        dc.run(nc.vector.tensor_tensor_reduce(out=X[:, hh, P:384], in0=A[:, 0:TP], in1=K["cadd"][:, P:384], scale=1.0,
                                                              scalar=NEG, op0=ALU.add, op1=ALU.max, accum_out=gm[:, 1, hh:hh + 1]))
                        dc.run(nc.vector.tensor_tensor_reduce(out=X[0:32, hh, 384:416], in0=A[0:32, TP:NT], in1=K["sadd"][0:32], scale=1.0,
                                                              scalar=NEG, op0=ALU.add, op1=ALU.max, accum_out=gm[0:32, 2, hh:hh + 1]))
                    dc.sync()
                    dc.run(nc.vector.tensor_tensor(g[:], gm[:], m0tok[:, :, pair], ALU.max))
                    dc.sync()
                    dc.run(nc.vector.tensor_scalar(ng[:], g[:], -1.0, None, ALU.mult))
                    dc.run(nc.vector.tensor_tensor(wprev[:], m0tok[:, :, pair], g[:], ALU.subtract))
                    dc.run(nc.vector.tensor_tensor(mt[:, :, pair], btok[:, :, pair], g[:], ALU.add))
                    dc.run(nc.vector.tensor_tensor(gl8[:], g[0:32, 2, :].unsqueeze(2).broadcast_to([32, 2, NB]),
                                                   K["lastm"][0:32].unsqueeze(1).broadcast_to([32, 2, NB]), ALU.mult))
                    dc.sync()
                    dc.run(nc.vector.reduce_sum(qn[:], qn8[:], AX))
                    nc.vector.tensor_scalar(emm[:], mt[:, :, pair], -1.0, None, ALU.mult).then_inc(m_g, 1)
                if j == 1:
                    dve.wait_ge(m_gl, p + 1)
                    dc.run(nc.vector.tensor_tensor(wend[:, 0:2, :], atok[:, 0:2, pair], B[4][:, 0:2].unsqueeze(1).broadcast_to([P, 2, 2]), ALU.subtract))
                    dc.run(nc.vector.tensor_tensor(wend[0:32, 2, :], atok[0:32, 2, pair], B[4][0:32, 2:4], ALU.subtract))
                    nc.vector.tensor_tensor(decay[:], m0v[:, pair, :], B[4][:, 4:20].rearrange("p (h b) -> p h b", b=NB), ALU.subtract).then_inc(m_gls, 1)
                    for hh in range(2):
                        dve.wait_ge(m_w, 2 * p + hh + 1)
                        dc.run(nc.vector.tensor_tensor(X[:, hh, 0:384], X[:, hh, 0:384], B[2 + hh][:, 0:384], ALU.mult))
                        nc.vector.tensor_tensor(X[0:32, hh, 384:416], X[0:32, hh, 384:416], B[2 + hh][0:32, 384:416], ALU.mult).then_inc(m_sw, 1)
                if j == 2:
                    dve.wait_ge(m_we, 2 * p + 2)
                    dve.wait_ge(m_kc, 2 * p + 2)
                    for hh in range(2):
                        dc.run(nc.vector.tensor_scalar(wsel[:, hh, :], K["bmask"][0:32], wend[0:32, 2, hh:hh + 1], None, ALU.mult))
                    for hh in range(2):
                        for r in range(2):
                            last = nc.vector.tensor_scalar(kw[:, r, hh, :], mK[:, r, hh, :], wend[:, r, hh:hh + 1], None, ALU.mult)
                    last.then_inc(m_kw, 1)
                    dc.sync()
                    vexp_of(0)
                    dve.wait_ge(m_s2, p + 1)
                    dve.wait_ge(m_em, 2 * p + 2)
                    for hh in range(2):
                        dc.run(nc.vector.tensor_scalar(tq[:, hh, :], B[6][0:32, hh * P:(hh + 1) * P], wprev[0:32, 2, hh:hh + 1], None, ALU.mult))
                    dve.wait_ge(evac_done[p_ml.bank(7)], p_ml.evacs(p, 7) + 1)
                    dve.wait_ge(evac_done[p_ml.bank(6)], p_ml.evacs(p, 6) + 1)
                    dc.run(nc.vector.tensor_scalar(mo[:], mo[:], 1.0, None, ALU.add))
                    dc.sync()
                    dc.run(nc.vector.reciprocal(mo[:], mo[:]))
                    dc.run(nc.vector.tensor_tensor(qn[:], qn[:], wprev[0:32, 2, :], ALU.mult))
                    dc.sync()
                if j == 3:
                    dve.wait_ge(m_s3, p + 1)
                    for hh in range(2):
                        N = B[2 + hh]
                        dc.run(nc.vector.tensor_copy(hs[:, 0:2, hh, :], N[:, 0:2 * (P + 1)].rearrange("p (r c) -> p r c", c=P + 1)))
                        dc.run(nc.vector.tensor_tensor(hs[0:32, 2, hh, 0:P], tq[:, hh, :], N[0:32, 258:386], ALU.add))
                        last = nc.vector.tensor_tensor(hs[0:32, 2, hh, P:P + 1], qn[:, hh:hh + 1], N[0:32, 386:387], ALU.add)
                    last.then_inc(m_hs, 1)
                    dve.wait_ge(m_hs, p + 1)
                    dc.sync()
                    dc.run(nc.vector.scalar_tensor_tensor(den[:], hs[:, :, :, P], -1.0, hs[:, :, :, P], ALU.mult, ALU.max))
                    dc.sync()
                    dc.run(nc.vector.tensor_tensor(den[:], den[:], emm[:], ALU.max))
                    dc.sync()
                    dc.run(nc.vector.reciprocal(rden[:], den[:]))
                    dc.sync()
                    dc.run(nc.vector.tensor_tensor(rd2[:], rden[:], rden[:], ALU.mult))
                    dve.wait_ge(m_sq, p + 1)
                    dc.run(nc.vector.reduce_sum(ss[:], sqb, AX))
                    dc.sync()
                    dc.run(nc.vector.tensor_tensor(ss[:], ss[:], rd2[:], ALU.mult))
                    dc.sync()
                    nc.vector.tensor_scalar(ss[:], ss[:], 1.0 / DH, EPS, ALU.mult, ALU.add).then_inc(m_ms, 1)
                    c_add(p, 0)
                    vexp_of(1)
                    nc.vector.tensor_copy(cP[:], B[7][:, 0:2 * (P + 1)].rearrange("p (h c) -> p h c", h=2)).then_inc(m_cp, 1)
                    dc.run(nc.vector.tensor_tensor(ntA[:], n0v[:, pair, :], decay[:], ALU.mult))
                    dc.sync()
                    dc.run(nc.vector.tensor_tensor(nnv[:, pair, :], ntA[:], B[7][:, 258:274].rearrange("p (h b) -> p h b", b=NB), ALU.add))
                    dve.wait_ge(m_cp, p + 1)
                    nc.vector.tensor_copy(nP[:, pair], cP[:, :, P]).then_inc(m_n, 1)
                    dve.wait_ge(m_sc, p + 1)
                    dc.run(nc.vector.tensor_tensor(sc[:], ss[:], rden[:], ALU.mult))
                    dc.sync()
                    nc.vector.tensor_tensor(hs[:, :, :, 0:P], hs[:, :, :, 0:P], sc[:].unsqueeze(3).broadcast_to([P, 3, 2, P]), ALU.mult).then_inc(m_hsr, 1)
                if j == 4:
                    dve.wait_ge(m_s4, p + 1)
                    for hh in range(2):
                        nc.vector.scalar_tensor_tensor(htmp[:, hh, :], B[2 + hh][:, 0:NT], gains[:, ds(2 * p + (80 + hh), 1)], mo[:, hh, :],
                                                       ALU.mult, ALU.mult).then_inc(m_tmp, 1)
                    c_add(p, 1)
                if j == 6:
                    dve.wait_ge(m_hi, p + 1)
                    nc.vector.tensor_tensor(hml[:, pair, :], htmp[:], hmh[:, pair, :].bitcast(F32), ALU.subtract).then_inc(m_lo, 1)
                if j == 7:
                    dve.wait_ge(m_lo, p + 1)
                    dve.wait_ge(m_cps, 16 * p + 16)

            def ml_body(i, gemm, attn):
                if attn:
                    ml_arow(i - 1)
                for j in range(8):
                    if gemm:
                        lo(p_ml, i, j // 2, j, src256(p_ml.slot(j // 2), j % 2))
                    if attn:
                        ml_attn(i - 1, j)
            ml_body(0, True, False)
            with dve.Fori(1, 4) as i:
                dc.loop(i - 1, ML_DVE)
                ml_body(i, True, True)
            dc.loop(3, ML_DVE)
            ml_body(4, False, True)
            dc.end(4)
            dve.wait_ge(m_nt, 1)
            nc.vector.tensor_copy(noutS[:], B[2][0:64, 0:P]).then_inc(m_no, 1)
            nc.vector.tensor_copy(noutP[:], B[2][0:H, P:2 * P]).then_inc(m_no, 1)

            def mo_attn(p, j):
                pair = ds(2 * p, 2)
                if j == 2:
                    dve.wait_ge(a_s1, p + 1)
                    for hh in range(2):
                        dc.run(nc.vector.scalar_tensor_tensor(pX[:, hh, :], K["cdist"], K["slopes"][:, ds(2 * p + hh, 1)], B[2 + hh][:, 0:384],
                                                              ALU.mult, ALU.add))
                    dc.sync()
                    for hh in range(2):
                        dc.run(nc.vector.reduce_max(arm[:, hh, 0:1], pX[:, hh, 0:P], AX))
                        dc.run(nc.vector.reduce_max(arm[:, hh, 1:2], pX[:, hh, P:384], AX))
                    dc.sync()
                    nc.vector.tensor_scalar(arm[:], arm[:], -1.0, None, ALU.mult).then_inc(a_x, 1)
                    dve.wait_ge(a_p, p + 1)
                    dc.run(nc.vector.reciprocal(asum[:], asum[:]))
                    dc.sync()
                    for hh in range(2):
                        nc.vector.tensor_scalar(pX[:, hh, 0:P], pX[:, hh, 0:P], asum[:, hh, 0:1], None, ALU.mult)
                        last = nc.vector.tensor_scalar(pX[:, hh, P:384], pX[:, hh, P:384], asum[:, hh, 1:2], None, ALU.mult)
                    last.then_inc(a_pn, 1)
                if j == 4:
                    dve.wait_ge(a_pv, p + 1)
                    nc.vector.tensor_copy(atmp[:], B[6][:].rearrange("p (h c) -> p h c", h=2)).then_inc(a_tmp, 1)
                    dve.wait_ge(a_hi, p + 1)
                    nc.vector.tensor_tensor(hal[:, pair, 0:TP], atmp[:], hah[:, pair, 0:TP].bitcast(F32), ALU.subtract).then_inc(a_lo, 1)

            def mo_body(i, gemm, attn):
                for j in range(6):
                    if gemm:
                        lo(p_mo, i, j // 2, j, src256(p_mo.slot(j // 2), j % 2))
                    if attn:
                        mo_attn(i - 1, j)
            mo_body(0, True, False)
            with dve.Fori(1, 4) as i:
                dc.loop(i - 1, MO_DVE)
                mo_body(i, True, True)
            dc.loop(3, MO_DVE)
            mo_body(4, False, True)
            dc.end(4)

            def k_copies(kts, tr_sem, ss_sem, mine, base, i):
                for n in range(1, 16, 2):
                    dve.wait_ge(tr_sem, i * 16 + (base + n + 1))
                    dve.wait_ge(ss_sem, i * 16 + (base + n + 1))
                    nc.vector.tensor_copy(kts[1][:], B[2 + n % 4][:].rearrange("p (h c) -> p h c", c=P)).then_inc(mine, 1)

            def d_batch(b, k, v):
                if k:
                    nc.vector.tensor_copy(qpad[:].rearrange("p (h c) -> p h c", c=NS + TS)[:, :, 0:TS],
                                          qs[:, :, ds(b * TS, TS)]).then_inc(d_q, 1)
                    k_copies(KTb, d_tr, d_ss, d_ktd, 0, b)
                    dve.wait_ge(d_sc, b + 1)
                    for q in range(2):
                        dc.run(nc.vector.reduce_sum(gs[:, 2 * q:2 * q + 2], B[6 + q][0:NS, :].rearrange("p (n c) -> p n c", c=256), AX))
                    dc.sync()
                    dc.run(nc.vector.tensor_reduce(dmn[:], gs[:], AX, ALU.min))
                    dc.sync()
                    dc.run(nc.vector.scalar_tensor_tensor(geq[:], gs[:], dmn[:], K["rank"][0:NS], ALU.is_equal, ALU.mult))
                    dc.sync()
                    dc.run(nc.vector.reduce_max(dmx[:], geq[:], AX))
                    dc.sync()
                    dc.run(nc.vector.tensor_scalar(pen[:], geq[:], dmx[:], NEG, ALU.is_equal, ALU.mult))
                    dc.sync()
                    for n in range(BLOCKS):
                        dc.run(nc.vector.scalar_tensor_tensor(DP[:, n * 256:(n + 1) * 256], B[6 + n // 2][0:NS, (n % 2) * 256:(n % 2) * 256 + 256],
                                                              pen[:, n:n + 1], dtab[:, n * 256:(n + 1) * 256], ALU.add, ALU.add))
                    dc.run(nc.vector.tensor_tensor(DP[:, PAST:], B[1][0:NS, 256:256 + NS], dtab[:, ds(b * -TS + (PAST + OWN), NS)], ALU.add))
                    dc.sync()
                    dc.run(nc.vector.reduce_max(dmx[:], DP[:], AX))
                    dc.sync()
                    nc.vector.tensor_scalar(dmx[:], dmx[:], -1.0, None, ALU.mult).then_inc(d_sm, 1)
                    dve.wait_ge(d_p, b + 1)
                    dc.run(nc.vector.reciprocal(dsum[:], dsum[:]))
                    dc.sync()
                    nc.vector.tensor_scalar(DP[:], DP[:], dsum[:], None, ALU.mult).then_inc(d_pn, 1)
                if v:
                    dve.wait_ge(d_pvb, b)
                    nc.vector.tensor_copy(hrow[:, 4 * P:], B[3][0:NS, :]).then_inc(d_vb, 1)
                    dve.wait_ge(d_ht, b)
                    nc.vector.tensor_copy(hsd[:, :, ds(b * TS - TS, TS)],
                                          B[1][:, 0:H * (NS + TS)].rearrange("p (h c) -> p h c", c=NS + TS)[:, :, 0:TS]).then_inc(d_h, 1)
            dve.wait_ge(a_kc, 4)
            dve.wait_ge(a_ks, 16 * 12)
            dve.wait_ge(a_vs, 16 * 12)
            dve.wait_ge(a_vcp, 4)
            dve.wait_ge(a_lo, 4)
            dve.wait_ge(d_tab, 16)
            dc.run(nc.vector.memset(qpad[:], 0.0))
            dc.sync()
            nc.vector.engine_nop().then_inc(d_h, 1)
            d_batch(0, True, False)
            D_DVE = 13
            with dve.Fori(1, NB) as b:
                dc.loop(b - 1, D_DVE)
                d_batch(b, True, True)
            dc.end(NB - 1)
            d_batch(NB, False, True)
            dve.wait_ge(d_hi, 1)
            nc.vector.tensor_tensor(hal[:, :, TP:NT], hsd[:], hah[:, :, TP:NT].bitcast(F32), ALU.subtract).then_inc(d_lo, 1)
            dve.wait_ge(d_lo, 1)

            def mx_tail(i, j):
                dve.wait_ge(x_p, i * 2 + (j + 1))
                dc.run(nc.vector.tensor_tensor(ut[:, 0, :], B[2 + 2 * j][:, 0:NT], sg[:, j, :], ALU.mult))
                dc.run(nc.vector.tensor_tensor(ut[:, 1, :], B[3 + 2 * j][:, 0:NT], sg[:, 2 + j, :], ALU.mult))
                dc.sync()
                nc.vector.tensor_tensor(U[:, ds(i * 2 + j, 1), :], ut[:, 0:1, :], ut[:, 1:2, :], ALU.add).then_inc(x_pe, 2)
                dve.wait_ge(x_pe, 4 * i + (2 * j + 6))

            nc.vector.engine_nop().then_inc(x_pe, 4)
            with dve.Fori(0, 8) as i:
                dc.loop(i, 6)
                for j in range(6):
                    lo(p_mx, i, j // 2, j, src256(p_mx.slot(j // 2), j % 2))
                for t in (2, 3):
                    dve.wait_ge(evac_done[p_mx.bank(t)], p_mx.evacs(i, t) + 1)
                dc.run(nc.vector.tensor_scalar(sg[:], sg[:], 1.0, None, ALU.add))
                dc.sync()
                dc.run(nc.vector.reciprocal(sg[:], sg[:]))
                dc.sync()
                for j in range(2):
                    mx_tail(i, j)
            dc.end(8)
            for q in range(4):
                dve.wait_ge(x_uhi, q + 1)
                nc.vector.tensor_tensor(xl[:, 4 * q:4 * q + 4, :], U[:, 4 * q:4 * q + 4, :], xh[:, 4 * q:4 * q + 4, :].bitcast(F32),
                                        ALU.subtract).then_inc(x_ulo, 1)

            def add_to_x(ph, i, t, conv, m):
                dve.wait_ge(gemm_done, ph.conv(i, conv + 1))
                nc.vector.tensor_tensor(xT[:, m, :], xT[:, m, :], G[ph.bank(t)][:, 0:NT].unsqueeze(1), ALU.add).then_inc(evac_done[ph.bank(t)], 1)

            def wo_body(i, first):
                for j in range(4):
                    lo(p_wo, i, j // 2, j, src256(p_wo.slot(j // 2), j % 2))
                    if j >= 2:
                        add_to_x(p_wo, i, j - 2, j - 2, ds(i * 4 + (j - 2), 1))
                    elif not first:
                        add_to_x(p_wo, i - 1, j + 2, j + 2, ds(i * 4 + (j - 2), 1))
            wo_body(0, True)
            with dve.Fori(1, 4) as i:
                wo_body(i, False)
            add_to_x(p_wo, 3, 2, 2, ds(14, 1))
            add_to_x(p_wo, 3, 3, 3, ds(15, 1))

            for n in (1, 3, 5, 7):
                dve.wait_ge(tp_done, 9 + n + 1)
                t, k4 = n // 4, n % 4
                nc.vector.tensor_copy(memT[:, 4 * k4:4 * k4 + 4, t * P:(t + 1) * P],
                                      B[2 + n % 4][:].rearrange("p (k c) -> p k c", c=P)).then_inc(tp_odd, 1)
            dve.wait_ge(tp_even, 5 + 4)
            dve.wait_ge(tp_odd, 4 + 4)
            norm(1, MEM)
            norm_apply(1, memT, 32, MEM)
            for j in range(8):
                lo(p_mem, 0, j // 2, j, src256(p_mem.slot(j // 2), j % 2))
            norm(2, NT)
            norm_apply(2, xT, 16, NT)
            for j in range(4):
                lo(p_xq, 0, j // 2, j, src256(p_xq.slot(j // 2), j % 2))

            dve.wait_ge(c_s, 1)
            for h in range(XH):
                dc.run(nc.vector.tensor_copy(xP[:, h, :, :], B[2 + h][:].rearrange("p (r c) -> p r c", c=MEM)))
            dc.sync()
            dc.run(nc.vector.reduce_max(xmx[:], xP[:], AX))
            dc.sync()
            nc.vector.tensor_scalar(xmx[:], xmx[:], -1.0, None, ALU.mult).then_inc(c_x, 1)
            dve.wait_ge(c_p, 1)
            dc.run(nc.vector.reciprocal(xsm[:], xsm[:]))
            dc.sync()
            nc.vector.tensor_tensor(xP[:], xP[:], xsm[:].unsqueeze(3).broadcast_to([P, XH, 2, MEM]), ALU.mult).then_inc(c_pn, 1)
            for q in range(2):
                dve.wait_ge(c_pv, q + 1)
                nc.vector.tensor_copy(octx[:, 2 * q:2 * q + 2, 0:TP], B[6 + q][:].rearrange("p (h c) -> p h c", c=TP)).then_inc(c_ctx, 1)
            k_copies(xKT, d_tr, d_ss, d_ktd, 128, 0)
            dve.wait_ge(c_sc, 1)
            nc.vector.tensor_copy(xST[:], B[6][:, 0:256].rearrange("p (m c) -> p m c", c=P)).then_inc(c_st, 1)
            dve.wait_ge(c_rows, 1)
            dc.run(nc.vector.tensor_copy(xDP[:], B[2][:, 0:256].rearrange("p (m c) -> p m c", c=P)))
            dc.sync()
            dc.run(nc.vector.reduce_max(smx[:], xDP[:].rearrange("p m c -> p (m c)"), AX))
            dc.sync()
            nc.vector.tensor_scalar(smx[:], smx[:], -1.0, None, ALU.mult).then_inc(c_sx, 1)
            dve.wait_ge(c_sp, 1)
            dc.run(nc.vector.reciprocal(ssm[:], ssm[:]))
            dc.sync()
            nc.vector.tensor_scalar(xDP[:], xDP[:], ssm[:], None, ALU.mult).then_inc(c_spn, 1)
            dve.wait_ge(c_spv, 1)
            for u in range(2):
                last = nc.vector.tensor_copy(octx[:, :, TP + 16 * u:TP + 16 * u + 16].rearrange("p h (b t) -> p b h t", t=TS),
                                             B[5 + u][:, 0:64].rearrange("p (b h t) -> p b h t", h=XH, t=TS))
            last.then_inc(c_ctx, 1)
            dve.wait_ge(c_ctx, 3)
            dve.wait_ge(c_chi, 1)
            nc.vector.tensor_tensor(ctxl[:], octx[:], ctxh[:].bitcast(F32), ALU.subtract).then_inc(c_clo, 1)

            def xo_add(c):
                dve.wait_ge(gemm_done, p_xo.conv(0, c + 1))
                for m in range(4):
                    last = nc.vector.tensor_tensor(xT[:, 4 * c + m, :], xT[:, 4 * c + m, :], B[4 * (c % 2) + m][:, 0:NT], ALU.add)
                last.then_inc(c_xo, 1)
            for j in range(6):
                if j < 4:
                    lo(p_xo, 0, j // 2, j, xo_src(j))
                if j >= 2:
                    xo_add(j - 2)
            dve.wait_ge(c_xo, 4)
            dve.wait_ge(c_out, 64)

            norm(3, NT)
            norm_apply(3, xT, 48, NT)

            def up_sig(f, i):
                for t in range(2):
                    dve.wait_ge(evac_done[p_up[f].bank(t)], p_up[f].evacs(i, t) + 1)
                dc.run(nc.vector.tensor_scalar(fe[:], fe[:], 1.0, None, ALU.add))
                dc.sync()
                dc.run(nc.vector.reciprocal(fe[:], fe[:]))
                dc.sync()
                dc.run(nc.vector.tensor_tensor(fg[:], fg[:], fe[:], ALU.mult))
                dc.sync()

            def up_mul(f, i, t):
                dve.wait_ge(gemm_done, p_up[f].conv(i, t + 3))
                nc.vector.tensor_tensor(fa[:, t, :], fg[:, t, :], G[p_up[f].bank(t + 2)][:, 0:NT], ALU.mult).then_inc(f_a, 1)
                nc.vector.engine_nop().then_inc(evac_done[p_up[f].bank(t + 2)], 1)

            def up_lo(f, i):
                dve.wait_ge(f_hi, i + (1 + f * (FH // 2)))
                nc.vector.tensor_tensor(fal[:, ds(i * 2, 2), :], fa[:], fah[:, ds(i * 2, 2), :].bitcast(F32), ALU.subtract).then_inc(f_lo, 1)

            def up_body(f, i, first):
                for j in range(4):
                    if j < 2 and not first:
                        up_mul(f, i - 1, j)
                    lo(p_up[f], i, j // 2, j, src256(p_up[f].slot(j // 2), j % 2))
                    if j == 3 and not first:
                        up_lo(f, i - 1)
                up_sig(f, i)
                if not first:
                    dve.wait_ge(f_lo, i + f * (FH // 2))
            for f in range(2):
                up_body(f, 0, True)
                with dve.Fori(1, FH // 2) as i:
                    dc.loop(i - 1, 3)
                    up_body(f, i, False)
                dc.end(FH // 2 - 1)
                up_mul(f, FH // 2 - 1, 0)
                up_mul(f, FH // 2 - 1, 1)
                up_lo(f, FH // 2 - 1)
                ph = p_dn[f]

                def dn_body(i, first):
                    for j in range(4):
                        lo(ph, i, j // 2, j, src256(ph.slot(j // 2), j % 2)[:, 0:FU])
                        if j < 2 and not first:
                            add_to_x(ph, i - 1, j, j + 2, ds(i * 2 + (j - 2), 1))
                dn_body(0, True)
                with dve.Fori(1, 8) as i:
                    dn_body(i, False)
                add_to_x(ph, 7, 0, 2, ds(14, 1))
                add_to_x(ph, 7, 1, 3, ds(15, 1))
                dve.wait_ge(f_lo, (f + 1) * (FH // 2))
            dve.wait_ge(evac_done[p_dn[1].bank(0)], p_dn[1].evacs(8, 0))
            dve.wait_ge(evac_done[p_dn[1].bank(1)], p_dn[1].evacs(8, 1))
            norm(4, NT)
            for k in range(KT):
                nc.vector.scalar_tensor_tensor(xT[:, k, :], xT[:, k, :], gains[:, 64 + k:65 + k], nr[:], ALU.mult, ALU.mult).then_inc(y_r, 1)
            for n in range(1, 12, 2):
                dve.wait_ge(tp_done, 17 + n + 1)
                rows_ = (P, P, NS)[n // 4]
                nc.vector.tensor_copy(yout[0:rows_, n // 4, (n % 4) * 512:(n % 4) * 512 + 512], B[2 + n % 4][0:rows_, :]).then_inc(tp_odd, 1)

        @block.tensor
        def _(pe):
            mm = nc.tensor.matmul

            def tile(ph, i, u, c, t, n=NT, reads=1):
                s, half, bank = ph.slot(u), ph.half(c), ph.bank(t)
                pe.wait_ge(slot_read[s], ph.reads(i, u, c % 2 + 1))
                wait(pe, evac_done[bank], ph.evacs(i, t))
                for k in range(KT):
                    out = G[bank][:, 0:n]
                    mm(out, wh[half][:, k, :], xh[:, k, 0:n], start=k == 0, stop=False)
                    mm(out, wh[half][:, k, :], xl[:, k, 0:n], start=False, stop=False)
                    last = mm(out, wl[half][:, k, :], xh[:, k, 0:n], start=False, stop=k == KT - 1)
                last.then_inc(gemm_done, 1)

            def norm(q, n):
                for k in range(KT):
                    pe.wait_ge(sq_ready, KT * q + k + 1)
                    mm(B[2][:, 0:n], ones[:], sq[:, k % 2, 0:n], start=k == 0, stop=k == KT - 1).then_inc(sq_used, 1)

            def one(out, lhsT, rhs, start=True, stop=True):
                return mm(out, lhsT, rhs, start=start, stop=stop)

            def tr(out, src):
                n = src.shape[0]
                return nc.tensor.transpose(out, src, ident[0:n, 0:n])

            pe.wait_ge(const_in, 16)
            pe.wait_ge(ones_set, 1)
            for n in range(9):
                t, k4 = n // 4, n % 4
                pe.wait_ge(landed[t // 2], 16 * (2, 1)[t // 2])
                if n >= 4:
                    pe.wait_ge((tp_even, tp_odd)[n % 2], (n - 4) // 2 + 1)
                if n < 8:
                    for k in range(4):
                        kk = 4 * k4 + k
                        last = tr(B[2 + n % 4][:, k * P:(k + 1) * P], raw[0][:, t * D + kk * P:t * D + (kk + 1) * P])
                else:
                    for k in range(KT):
                        last = tr(B[2][:, k * NS:(k + 1) * NS], raw[1][0:NS, k * P:(k + 1) * P])
                last.then_inc(tp_done, 1)
            pe.wait_ge(params_in, PARAMS)
            tr(B[6][:, 0:88], grow[:])
            tr(B[7][:, 0:64], n0raw[:]).then_inc(gains_t, 1)
            pe.drain().then_inc(slot_read[0], 1)
            pe.drain().then_inc(slot_read[1], 1)
            pe.wait_ge(tp_even, 5)
            norm(0, NT)
            pe.wait_ge(xn_ready, KT)
            tile(p_gate, 0, 0, 0, 0)

            pe.wait_ge(evac_done[0], 1)
            pe.wait_ge(m_mem, 1)
            tr(B[3][:, 0:16], gT[:, 0:P])
            tr(B[3][:, 16:32], gT[:, P:TP])
            tr(B[3][0:32, 32:48], gT[:, TP:NT]).then_inc(g_t, 1)
            pe.wait_ge(g_lf, 1)
            one(B[4][:, 0:8], K["tri"], lf[:, 0, :])
            one(B[4][:, 8:16], ones[:], lf[:, 0, :], stop=False)
            one(B[4][:, 8:16], K["tri"], lf[:, 1, :], start=False)
            one(B[4][0:32, 16:24], K["tris"][0:32], lf[0:32, 2, :]).then_inc(g_cum, 1)
            pe.wait_ge(g_a, 1)
            tr(B[5][0:8, 0:P], atok[:, 0, :])
            tr(B[5][0:8, P:TP], atok[:, 1, :])
            tr(B[5][0:8, TP:NT], atok[0:32, 2, :]).then_inc(g_aT, 1)
            pe.wait_ge(g_aTs, 1)
            n0v = n0T[:].rearrange("p (b h) -> p h b", h=H)

            def rows(banks, src, n):
                for hh in range(2):
                    tr(banks[hh][:, 0:P], src[:, hh, 0:P])
                    tr(banks[hh][:, P:2 * P], src[:, hh, P:TP])
                    last = tr(banks[hh][0:32, 2 * P:3 * P], src[:, hh, TP:NT])
                return last

            def ml_attn(p, j):
                if j == 0:
                    pe.wait_ge(evac_done[p_ml.bank(5)], p_ml.evacs(p, 5) + 1)
                    pe.wait_ge(evac_done[p_ml.bank(4)], p_ml.evacs(p, 4) + 1)
                    pe.wait_ge(m_arow, 2 * p + 2)
                    pe.wait_ge(m_c0in, 32 * p + 32)
                    pe.wait_ge(m_vc, 2 * p + 2)
                    for hh in range(2):
                        one(B[2 + hh][:, 0:P], mq[:, hh, 0:P], mk[:, hh, 0:P])
                        one(B[2 + hh][:, P:384], mq[:, hh, P:TP], mk[:, hh, 0:TP])
                        one(B[2 + hh][0:32, 384:416], mq[:, hh, TP:NT], mk[:, hh, TP:NT])
                        one(B[4 + hh][:, 0:NT], ones[0:H, :], arow[:, hh, :])
                        for b in range(NB):
                            one(B[6][:, 32 * hh + TS * b:32 * hh + TS * b + TS], C0[:, hh, b, :], mq[:, hh, TP + TS * b:TP + TS * b + TS])
                        last = one(B[6][0:32, 64 + 8 * hh:72 + 8 * hh], mq[:, hh, TP:NT], n0v[:, ds(2 * p + hh, 1), :].rearrange("p a b -> p (a b)"))
                    last.then_inc(m_s1, 1)
                if j == 1:
                    pe.wait_ge(m_g, p + 1)
                    rows((B[7], B[6]), mk, 0).then_inc(m_ktr, 1)
                    one(B[4][:, 0:2], K["lastp"], g[:, 1, :])
                    one(B[4][0:32, 2:4], K["lasts"][0:32], g[0:32, 2, :])
                    one(B[4][:, 4:20], ones[0:32, :], gl8[:].rearrange("p h b -> p (h b)")).then_inc(m_gl, 1)
                if j == 2:
                    pe.wait_ge(m_gls, p + 1)
                    pe.wait_ge(m_kc, 2 * p + 2)
                    for hh in range(2):
                        pe.wait_ge(m_sw, 2 * p + hh + 1)
                        for r in range(3):
                            tr(B[4 + hh][:, r * P:(r + 1) * P], X[:, hh, r * P:(r + 1) * P])
                        tr(B[4 + hh][0:32, 384:416], X[0:32, hh, 384:416])
                        last = tr(B[6][0:32, hh * P:(hh + 1) * P], qc[:, hh, :])
                    last.then_inc(m_s2, 1)
                if j == 3:
                    pe.wait_ge(m_swt, 2 * p + 2)
                    pe.wait_ge(m_kw, p + 1)
                    for hh in range(2):
                        N = B[2 + hh]
                        one(N[:, 0:129], swt[:, hh, 0:P], mV[:, 0, hh, :])
                        one(N[:, 129:258], swt[:, hh, P:2 * P], mV[:, 0, hh, :], stop=False)
                        one(N[:, 129:258], swt[:, hh, 2 * P:3 * P], mV[:, 1, hh, :], start=False)
                        one(N[0:32, 258:387], swt[0:32, hh, 384:416], mV[0:32, 2, hh, :])
                    for hh in range(2):
                        one(B[7][:, 129 * hh:129 * hh + 129], kw[:, 0, hh, :], mV[:, 0, hh, :], stop=False)
                        one(B[7][:, 129 * hh:129 * hh + 129], kw[:, 1, hh, :], mV[:, 1, hh, :], start=False)
                        one(B[7][:, 258 + 8 * hh:266 + 8 * hh], mK[0:32, 2, hh, :], wsel[:, hh, :])
                    pe.wait_ge(m_vx, 2 * p + 1)
                    for q in range(2):
                        last = one(B[4 + q][:, :], mK[0:32, 2, 0, :], vexp[:, 4 * q:4 * q + 4, :].rearrange("p b v -> p (b v)"))
                    last.then_inc(m_s3, 1)
                if j == 4:
                    pe.wait_ge(m_vx, 2 * p + 2)
                    pe.wait_ge(m_cadd, 2 * p + 1)
                    for q in range(2):
                        last = one(B[4 + q][:, :], mK[0:32, 2, 1, :], vexp[:, 4 * q:4 * q + 4, :].rearrange("p b v -> p (b v)"))
                    pe.wait_ge(m_hsr, p + 1)
                    for hh in range(2):
                        tr(B[2 + hh][:, 0:P], hs[:, 0, hh, 0:P])
                        tr(B[2 + hh][:, P:TP], hs[:, 1, hh, 0:P])
                        last = tr(B[2 + hh][:, TP:NT], hs[0:32, 2, hh, 0:P])
                    last.then_inc(m_s4, 1)

                if j == 5:
                    pe.wait_ge(m_tmp, 2 * p + 2)
                    pe.wait_ge(m_cadd, 2 * p + 2)

            def ml_body(i, gemm, attn):
                for j in range(8):
                    if attn:
                        ml_attn(i - 1, j)
                    if gemm:
                        tile(p_ml, i, j // 2, j, j)
                    if gemm and j == 4:
                        pe.wait_ge(evac_done[p_ml.bank(0)], p_ml.evacs(i, 0) + 1)
                        pe.wait_ge(evac_done[p_ml.bank(1)], p_ml.evacs(i, 1) + 1)
                        rows((B[6], B[7]), mv, 0).then_inc(m_vtr, 1)
            ml_body(0, True, False)
            with pe.Fori(1, 4) as i:
                ml_body(i, True, True)
            ml_body(4, False, True)
            pe.wait_ge(m_n, 4)
            pe.wait_ge(m_tmp, 8)
            tr(B[2][0:64, 0:P], nnew[:])
            tr(B[2][0:H, P:2 * P], nP[:]).then_inc(m_nt, 1)

            def mo_attn(p, j):
                if j == 2:
                    pe.wait_ge(evac_done[p_mo.bank(4)], p_mo.evacs(p, 4) + 1)
                    pe.wait_ge(evac_done[p_mo.bank(5)], p_mo.evacs(p, 5) + 1)
                    pe.wait_ge(m_no, 2)
                    for hh in range(2):
                        one(B[2 + hh][:, 0:P], aq[:, hh, 0:P], ak[:, hh, 0:P])
                        last = one(B[2 + hh][:, P:384], aq[:, hh, P:TP], ak[:, hh, 0:TP])
                    last.then_inc(a_s1, 1)
                if j == 3:
                    pe.wait_ge(a_vc, p + 1)
                    pe.wait_ge(a_pn, p + 1)
                    for hh in range(2):
                        for r in range(3):
                            last = tr(B[4 + hh][:, r * P:(r + 1) * P], pX[:, hh, r * P:(r + 1) * P])
                    last.then_inc(a_ptr, 1)
                    rows((B[7], B[2]), ak, 0).then_inc(a_ktr, 1)
                if j == 4:
                    pe.wait_ge(a_ptc, p + 1)
                    for hh in range(2):
                        c = hh * TP
                        one(B[6][:, c:c + TP], vst[:, 0, hh, :], pXT[:, hh, 0:TP], stop=False)
                        last = one(B[6][:, c + P:c + TP], vst[:, 1, hh, :], pXT[:, hh, TP:384], start=False)
                    last.then_inc(a_pv, 1)

                if j == 5:
                    pe.wait_ge(a_kc, p + 1)
                    pe.wait_ge(a_tmp, p + 1)

            def mo_body(i, gemm, attn):
                for j in range(6):
                    if attn:
                        mo_attn(i - 1, j)
                    if gemm:
                        tile(p_mo, i, j // 2, j, j)
                    if gemm and j == 4:
                        pe.wait_ge(evac_done[p_mo.bank(0)], p_mo.evacs(i, 0) + 1)
                        pe.wait_ge(evac_done[p_mo.bank(1)], p_mo.evacs(i, 1) + 1)
                        rows((B[4], B[5]), av, 0).then_inc(a_vtr, 1)
            mo_body(0, True, False)
            with pe.Fori(1, 4) as i:
                mo_body(i, True, True)
            mo_body(4, False, True)

            def k_scores(ph, i, count, kts, base, src, score, between=None):
                for n in range(17):
                    if n == 4 and between:
                        between()
                    if n < 16:
                        if n % 8 == 0:
                            pe.wait_ge(landed[ph.slot(n // 8)], ph.landed(i, n // 8))
                        for m in range(4):
                            last = tr(B[2 + n % 4][:, m * P:(m + 1) * P], src(n, m))
                        last.then_inc(d_tr, 1)
                    if n:
                        pe.wait_ge((d_kta, d_ktd)[(n - 1) % 2], count * 8 + (base // 2 + (n - 1) // 2 + 1))
                        for m in range(4):
                            last = score(n - 1, m, kts[(n - 1) % 2][:, m, :])
                            if m == 0 and n % 8 == 0:
                                last.then_inc(slot_read[ph.slot((n - 1) // 8)], 1)
                        last.then_inc(d_ss, 1)

            pe.wait_ge(d_tab, 16)
            pe.wait_ge(a_vcp, 4)
            pe.wait_ge(evac_done[p_mo.bank(5)], p_mo.evacs(3, 5) + 1)
            pe.wait_ge(a_kc, 4)
            pe.drain().then_inc(d_ss, 2)

            def d_batch(b, k, v):
                def pt():
                    hold(pe, d_pn, b)
                    for n in range(PAGES):
                        tr(B[0][:, n * NS:(n + 1) * NS], DP[:, n * P:(n + 1) * P])
                    tr(B[0][0:NS, PAGES * NS:(PAGES + 1) * NS], DP[:, PAST:PAST + NS]).then_inc(d_ptr, 1)
                if k:
                    ph, i = (p_d, b - 1) if v else (p_d0, 0)

                    def src(n, m):
                        c = (n // 2 % 4) * H * DH + (4 * (n % 2) + m) * DH
                        return raw[ph.slot(n // 8)][:, c:c + DH]

                    def score(n, m, kt):
                        page, h = n // 2, 4 * (n % 2) + m
                        return one(B[6 + page // 4][0:NS, (page % 4) * P:(page % 4 + 1) * P], qpad[:, h * NS:(h + 1) * NS], kt,
                                   start=h == 0, stop=h == H - 1)
                    pe.wait_ge(d_q, b + 1)
                    if v:
                        pe.wait_ge(d_sm, b)
                    k_scores(ph, i, b, KTb, 0, src, score, pt if v else None)
                    pe.wait_ge(d_h, b if v else 1)
                    for h in range(H):
                        last = one(B[1][0:NS, 256:256 + NS], qpad[:, h * NS:(h + 1) * NS], ks[:, h, :], start=h == 0, stop=h == H - 1)
                    last.then_inc(d_sc, 1)
                else:
                    pt()
                if v:
                    ph, i, u0 = (p_d, b - 1, 2) if k else (p_d8, 0, 0)
                    pe.wait_ge(d_ptc, b)
                    for u in range(2):
                        s = ph.slot(u0 + u)
                        pe.wait_ge(landed[s], ph.landed(i, u0 + u))
                        for half in range(2):
                            out = B[2 + half][0:NS, :]
                            for n in range(4):
                                c = n * H * DH + half * 512
                                last = one(out, PT[:, 4 * u + n, :], raw[s][:, c:c + 512], start=u == 0 and n == 0, stop=False)
                            if half:
                                last.then_inc(slot_read[s], 1)
                            if u:
                                last = one(out, PT[0:NS, PAGES, :], Vs[:, 4 * half:4 * half + 4, :].rearrange("p h d -> p (h d)"), start=False)
                                last.then_inc((d_pva, d_pvb)[half], 1)
                    if k:
                        pe.wait_ge(d_sm, b + 1)
                    else:
                        pe.wait_ge(d_h, b)
                    for half in range(2):
                        hold(pe, (d_va, d_vb)[half], b)
                        for h in range(4 * half, 4 * half + 4):
                            last = tr(B[1][:, h * NS:(h + 1) * NS], hrow[:, h * P:(h + 1) * P])
                    last.then_inc(d_ht, 1)
            d_batch(0, True, False)
            with pe.Fori(1, NB) as b:
                d_batch(b, True, True)
            d_batch(NB, False, True)
            pe.wait_ge(d_lo, 1)

            with pe.Fori(0, 8) as i:
                for j in range(4):
                    tile(p_mx, i, j // 2, j, j)
                for j in range(2):
                    c = 4 + j
                    half = p_mx.half(c)
                    pe.wait_ge(slot_read[p_mx.slot(2)], p_mx.reads(i, 2, j + 1))
                    pe.wait_ge(x_pe, 4 * i + (2 * j + 2))
                    for n, (rh, rl) in enumerate(((hmh, hml), (hah, hal))):
                        out = B[2 + 2 * j + n][:, 0:NT]
                        for k in range(H):
                            mm(out, wh[half][:, H * n + k, :], rh[:, k, :], start=k == 0, stop=False)
                            mm(out, wh[half][:, H * n + k, :], rl[:, k, :], start=False, stop=False)
                            last = mm(out, wl[half][:, H * n + k, :], rh[:, k, :], start=False, stop=k == H - 1)
                    last.then_inc(gemm_done, 1)
                    pe.drain().then_inc(x_p, 1)
            pe.wait_ge(x_ulo, 4)
            with pe.Fori(0, 4) as i:
                for j in range(4):
                    tile(p_wo, i, j // 2, j, j)

            pe.wait_ge(landed[0], p_min.landed(0, 0))
            for n in range(8):
                t, k4 = n // 4, n % 4
                if n >= 4:
                    pe.wait_ge((tp_even, tp_odd)[n % 2], (5, 4)[n % 2] + (n - 4) // 2 + 1)
                for k in range(4):
                    kk = 4 * k4 + k
                    last = tr(B[2 + n % 4][:, k * P:(k + 1) * P], raw[0][:, t * D + kk * P:t * D + (kk + 1) * P])
                last.then_inc(tp_done, 1)
            pe.drain().then_inc(slot_read[0], 1)
            pe.wait_ge(tp_even, 5 + 4)
            norm(1, MEM)
            pe.wait_ge(xn_ready, 2 * KT)
            for j in range(8):
                tile(p_mem, 0, j // 2, j, j, n=MEM)
            for b in range(2):
                pe.wait_ge(evac_done[b], p_xq.evacs(0, (b + p_xq.tile0) % 2))
            for n in range(4):
                for h in range(XH):
                    last = tr(B[2 + n][:, h * P:(h + 1) * P], (mvT, mkT)[n // 2][:, h, (n % 2) * P:(n % 2 + 1) * P])
                last.then_inc(c_kvt, 1)
            pe.wait_ge(c_kvc, 4)
            norm(2, NT)
            pe.wait_ge(xn_ready, 3 * KT)
            for j in range(4):
                tile(p_xq, 0, j // 2, j, j)
            for b in range(2):
                pe.wait_ge(evac_done[b], p_up[0].evacs(0, (b + p_up[0].tile0) % 2))
            for h in range(XH):
                for r in range(2):
                    last = one(B[2 + h][:, r * MEM:(r + 1) * MEM], xq[:, h, r * P:(r + 1) * P], mkT[:, h, :])
            last.then_inc(c_s, 1)
            pe.wait_ge(c_pn, 1)
            for h in range(XH):
                for m in range(2):
                    for r in range(2):
                        last = tr(B[2 + h][:, m * MEM + r * P:m * MEM + (r + 1) * P], xP[:, h, r, m * P:(m + 1) * P])
            last.then_inc(c_ptr, 1)
            pe.wait_ge(c_ptc, 1)
            for h in range(XH):
                for m in range(2):
                    last = one(B[6 + h // 2][:, (h % 2) * TP:(h % 2 + 1) * TP], mVt[:, m, h * P:(h + 1) * P], xPT[:, h, m * MEM:(m + 1) * MEM],
                               start=m == 0, stop=m == 1)
                if h % 2:
                    last.then_inc(c_pv, 1)
            pe.wait_ge(c_ctx, 2)

            def xsrc(n, m):
                c = (n % 8) * XH * DH + m * DH
                return raw[p_xk.slot(n // 8)][:, c:c + DH]

            def xscore(n, m, kt):
                c = (n % 2) * P + (n // 2) * 16 + m * TS
                return one(B[6][:, c:c + TS], kt, xq[:, m, TP + TS * (n // 2):TP + TS * (n // 2) + TS])
            k_scores(p_xk, 0, 0, xKT, 128, xsrc, xscore)
            pe.drain().then_inc(c_sc, 1)
            pe.wait_ge(c_st, 1)
            tr(B[2][:, 0:P], xST[:, 0, :])
            tr(B[2][:, P:2 * P], xST[:, 1, :]).then_inc(c_rows, 1)
            pe.wait_ge(c_spn, 1)
            tr(B[2][:, 0:P], xDP[:, 0, :])
            tr(B[2][:, P:2 * P], xDP[:, 1, :]).then_inc(c_spt, 1)
            pe.wait_ge(c_spc, 1)
            for u in range(2):
                s = p_xv.slot(u)
                pe.wait_ge(landed[s], p_xv.landed(0, u))
                for b in range(4):
                    for h in range(XH):
                        col = (4 * u + b) * 16 + h * TS
                        for m in range(2):
                            c = (2 * b + m) * XH * DH + h * DH
                            last = one(B[5 + u][:, b * 16 + h * TS:b * 16 + (h + 1) * TS], raw[s][:, c:c + DH], xPTs[:, m, col:col + TS],
                                       start=m == 0, stop=m == 1)
                last.then_inc(slot_read[s], 1)
            pe.drain().then_inc(c_spv, 1)
            pe.wait_ge(c_clo, 1)
            for c in range(4):
                half = p_xo.half(c)
                pe.wait_ge(slot_read[p_xo.slot(c // 2)], p_xo.reads(0, c // 2, c % 2 + 1))
                if c >= 2:
                    pe.wait_ge(c_xo, c - 1)
                wv = [w[half][:].rearrange("p k c -> p (k c)").rearrange("p (k c) -> p k c", c=512) for w in (wh, wl)]
                for m in range(4):
                    out = B[4 * (c % 2) + m][:, 0:NT]
                    for k in range(XH):
                        cols = slice(m * P, (m + 1) * P)
                        mm(out, wv[0][:, k, cols], ctxh[:, k, :], start=k == 0, stop=False)
                        mm(out, wv[0][:, k, cols], ctxl[:, k, :], start=False, stop=False)
                        last = mm(out, wv[1][:, k, cols], ctxh[:, k, :], start=False, stop=k == XH - 1)
                last.then_inc(gemm_done, 1)
            pe.wait_ge(c_xo, 4)
            norm(3, NT)
            pe.wait_ge(xn_ready, 4 * KT)
            for f in range(2):
                if f:
                    pe.wait_ge(evac_done[0], p_up[1].evacs(0, p_up[1].tile0 % 2))
                with pe.Fori(0, FH // 2) as i:
                    for j in range(4):
                        tile(p_up[f], i, j // 2, j, j)
                pe.wait_ge(f_lo, (f + 1) * (FH // 2))
                ph = p_dn[f]
                with pe.Fori(0, 8) as i:
                    for j in range(4):
                        u, t, half = j // 2, j % 2, ph.half(j)
                        pe.wait_ge(slot_read[ph.slot(u)], ph.reads(i, u, t + 1))
                        if u == 0:
                            pe.wait_ge(evac_done[ph.bank(t)], ph.evacs(i, t))
                        out = G[ph.bank(t)][:, 0:NT]
                        for k in range(FU):
                            kk = u * FU + k
                            mm(out, wh[half][:, k, :], fah[:, kk, :], start=kk == 0, stop=False)
                            mm(out, wh[half][:, k, :], fal[:, kk, :], start=False, stop=False)
                            last = mm(out, wl[half][:, k, :], fah[:, kk, :], start=False, stop=kk == FH - 1)
                        last.then_inc(gemm_done, 1)
            norm(4, NT)
            for n in range(12):
                t, k4 = n // 4, n % 4
                if t == 0:
                    pe.wait_ge(y_r, 4 * k4 + 4)
                if n >= 4:
                    pe.wait_ge((tp_even, tp_odd)[n % 2], (9, 8)[n % 2] + (n - 4) // 2 + 1)
                for k in range(4):
                    rows_ = (P, P, NS)[t]
                    last = tr(B[2 + n % 4][0:rows_, k * P:(k + 1) * P], xT[:, 4 * k4 + k, t * P:t * P + rows_])
                last.then_inc(tp_done, 1)


OUTS = dict(
    y_prompt=(1, TP, D), y_sample=(NB, TS, D), k_prompt=(1, 1, TP, H, DH), v_prompt=(1, 1, TP, H, DH),
    C_prompt=(1, 1, H, DH, DH), n_prompt=(1, 1, H, DH), m_prompt=(1, 1, H),
    mem_k_prompt=(1, 1, MEM, XH, DH), mem_v_prompt=(1, 1, MEM, XH, DH),
    k_sample=(1, NB, TS, H, DH), v_sample=(1, NB, TS, H, DH), C_sample=(1, NB, H, DH, DH),
    n_sample=(1, NB, H, DH), m_sample=(1, NB, H))


def kernel(**inputs):
    import concourse.bacc as bacc
    from concourse.bass_utils import run_bass_kernel_spmd

    nc = bacc.Bacc("TRN2", target_bir_lowering=False, num_devices=1)
    arrays, a, o = {}, {}, {}
    blob, dec = constants()
    for name, x in list(inputs.items()) + [("blob", blob), ("dec", dec)]:
        x = np.ascontiguousarray(x)
        arrays[f"{name}_dram"] = x
        a[name] = nc.dram_tensor(f"{name}_dram", x.shape, mybir.dt.from_np(x.dtype), kind="ExternalInput").ap()
    for name, shape in OUTS.items():
        o[name] = nc.dram_tensor(f"out_{name}_dram", shape, F32, kind="ExternalOutput").ap()
    build(nc, a, o)
    r = run_bass_kernel_spmd(nc, [arrays], core_ids=[0])
    return tuple(r.results[0][f"out_{name}_dram"] for name in OUTS)
```

```python
import numpy as np

import concourse.bass as bass
from concourse import mybir
from contextlib import ExitStack

F32 = mybir.dt.float32
F32R = mybir.dt.float32r
I32 = mybir.dt.int32
ACT = mybir.ActivationFunctionType
ALU = mybir.AluOpType
AX = mybir.AxisListType.X
ds = bass.ds

P = 128
D = 2048
KT = D // P
TP, NB, TS = 256, 8, 4
NS = NB * TS
NT = TP + NS
H, DH = 8, 128
XH = 4
FF = 5632
PAGES, PAST = 8, 1024
BLOCKS = 4
MEM = 256
FH = FF // P // 2
FU = FH // 2
OWN = NS - TS
NEG = -1e30
EPS = 1e-6
SCALE = float(DH) ** -0.5
W_IF = 4 * H * DH
W_QA = W_IF + 2 * H
W_GM = W_QA + 3 * H * DH
W_GA = W_GM + D
SLOTS = 3
UNIT = KT * 256
CONST = dict(ident=128, cadd=384, cdist=384, sadd=32, tri=128, tris=32, lastp=128, lasts=32,
             bmask=8, lastm=8, slopes=8, rank=4)
CW = sum(CONST.values())


def constants():
    at = np.arange(P)
    c = {}
    c["ident"] = np.eye(P)
    late = at[:, None] - at[None, :]
    tri = np.where(late >= 0, 0.0, NEG)
    c["cadd"] = np.concatenate([tri, np.zeros((P, P)), tri], 1)
    c["cdist"] = np.concatenate([np.where(late >= 0, -late, NEG), -(late + P), np.where(late >= 0, -late, NEG)], 1)
    s = np.arange(NS)
    same = s[:, None] // TS == s[None, :] // TS
    c["sadd"] = np.where(same & (s[:, None] >= s[None, :]), 0.0, NEG)
    c["tri"] = (at[:, None] <= at[None, :]) * 1.0
    c["tris"] = (same & (s[:, None] <= s[None, :])) * 1.0
    c["lastp"] = np.repeat((at == P - 1)[:, None] * 1.0, P, 1)
    c["lasts"] = (same & (s[:, None] % TS == TS - 1)) * 1.0
    c["bmask"] = (s[:, None] // TS == np.arange(NB)[None, :]) * 1.0
    c["lastm"] = (s[:, None] == TS * np.arange(NB)[None, :] + TS - 1) * 1.0
    slope = 2.0 ** (-8.0 * np.arange(1, H + 1) / H)
    c["slopes"] = np.repeat(slope[None], P, 0)
    c["rank"] = np.repeat(np.arange(1.0, BLOCKS + 1)[None], P, 0)
    blob = np.zeros((P, CW), np.float32)
    o = 0
    for name, w in CONST.items():
        blob[:c[name].shape[0], o:o + w] = c[name]
        o += w
    r = np.arange(NS)
    h, t = r // TS, r % TS
    dec = np.full((NS, PAST + OWN + NS), NEG, np.float32)
    dec[:, :PAST] = -slope[h][:, None] * (PAST + t[:, None] - np.arange(PAST)[None])
    own = np.arange(TS)[None]
    dec[:, PAST + OWN:PAST + NS] = np.where(own <= t[:, None], -slope[h][:, None] * (t[:, None] - own), NEG)
    return blob, dec


class Phase:

    def __init__(self, plan, iters, units, convs, tiles, slots=range(10 ** 3)):
        self.loads0, self.reads0 = list(plan["loads"]), list(plan["reads"])
        self.conv0, self.tile0 = plan["convs"], plan["tiles"]
        self.units, self.convs, self.tiles, self.iters = units, convs, tiles, iters
        self.slots = [s % SLOTS for s in slots[:len(units)]]
        self.loads_per = [16 * sum(d for u, (d, r) in enumerate(units) if self.slots[u] == s) for s in range(SLOTS)]
        self.reads_per = [sum(r for u, (d, r) in enumerate(units) if self.slots[u] == s) for s in range(SLOTS)]
        for s in range(SLOTS):
            plan["loads"][s] += iters * self.loads_per[s]
            plan["reads"][s] += iters * self.reads_per[s]
        plan["convs"] += iters * convs
        plan["tiles"] += iters * tiles
        assert iters == 1 or (convs % 2 == 0 and tiles % 2 == 0)

    def slot(self, u):
        return self.slots[u]

    def landed(self, i, u):
        s = self.slots[u]
        mine = 16 * sum(d for v, (d, r) in enumerate(self.units) if self.slots[v] == s and v <= u)
        return i * self.loads_per[s] + (self.loads0[s] + mine)

    def reads(self, i, u, n=0):
        s = self.slots[u]
        mine = sum(r for v, (d, r) in enumerate(self.units) if self.slots[v] == s and v < u)
        return i * self.reads_per[s] + (self.reads0[s] + mine + n)

    def conv(self, i, c):
        return i * self.convs + (self.conv0 + c)

    def half(self, c):
        return (self.conv0 + c) % 2

    def bank(self, t):
        return (self.tile0 + t) % 2

    def evacs(self, i, t):
        return i * (self.tiles // 2) + (self.tile0 + t) // 2


def wait(eng, sem, value):
    if not (isinstance(value, int) and value <= 0):
        eng.wait_ge(sem, value)


def hold(eng, sem, value):
    if not (isinstance(value, int) and value <= 0):
        eng.wait_ge(sem, value)
        eng.nop(nofuse=True)


class Chain:

    def __init__(self, eng, sem):
        self.eng, self.sem, self.base, self.k, self.i, self.per = eng, sem, 0, 0, 0, 0

    def loop(self, i, per):
        if isinstance(self.i, int) and self.i == 0 and self.per == 0:
            self.base += self.k
        self.i, self.per, self.k = i, per, 0

    def end(self, n):
        assert self.k == self.per, (self.k, self.per)
        self.base += n * self.per
        self.i, self.per, self.k = 0, 0, 0

    def run(self, ins):
        ins.then_inc(self.sem, 1)
        self.k += 1

    def sync(self):
        self.eng.wait_ge(self.sem, self.i * self.per + (self.base + self.k))


def build(nc, a, o):
    N_PHYS = a["cache_k"].shape[1]
    plan = dict(loads=[0] * SLOTS, reads=[0] * SLOTS, convs=0, tiles=0)
    two = (1, 2)
    rows_in = Phase(plan, 1, [(2, 1), (1, 1)], 0, 0)
    p_gate = Phase(plan, 1, [(1, 1)], 1, 1, (2,))
    p_ml = Phase(plan, 4, [two] * 4, 8, 8)
    p_mo = Phase(plan, 4, [two] * 3, 6, 6)
    p_d0 = Phase(plan, 1, [(4, 1)] * 2, 0, 0)
    p_d = Phase(plan, NB - 1, [(4, 1)] * 4, 0, 0, (0, 1, 0, 2))
    p_d8 = Phase(plan, 1, [(4, 1)] * 2, 0, 0, (0, 2))
    p_mx = Phase(plan, 8, [two, two, (2, 2)], 6, 4)
    p_wo = Phase(plan, 4, [two] * 2, 4, 4)
    p_min = Phase(plan, 1, [(2, 1)], 0, 0, (2,))
    p_mem = Phase(plan, 1, [two] * 4, 8, 8, (0, 1, 2, 0))
    p_xq = Phase(plan, 1, [two] * 2, 4, 4, (1, 2))
    p_xk = Phase(plan, 1, [(1, 1)] * 2, 0, 0, (0, 1))
    p_xv = Phase(plan, 1, [(1, 1)] * 2, 0, 0, (2, 0))
    p_xo = Phase(plan, 1, [two] * 2, 4, 0, (1, 2))
    p_up, p_dn = [], []
    for _ in range(2):
        p_up.append(Phase(plan, FH // 2, [two] * 2, 4, 4))
        p_dn.append(Phase(plan, 8, [two] * 2, 4, 2))

    ctx = ExitStack()
    with ctx:
        arena_at = (nc.sbuf_base + 31) // 32 * 32
        top = [arena_at]

        def at(name, shape, offset, dt=F32):
            return nc.alloc_sbuf_tensor_at(name, shape, dt, offset=offset)

        def put(name, shape, dt=F32):
            off = top[0]
            n = 4 * int(np.prod(shape[1:]))
            top[0] = off + (n + 31) // 32 * 32
            assert top[0] <= nc.sbuf_usable_end, (name, top[0])
            return at(name, shape, off, dt)

        def sem(name):
            return ctx.enter_context(nc.semaphore(name))

        raw = [put(f"raw{s}", [P, UNIT]) for s in range(SLOTS)]
        wh = [put(f"w_hi{s}", [P, KT, P], F32R) for s in range(2)]
        wl = [put(f"w_lo{s}", [P, KT, P], F32R) for s in range(2)]
        xT = put("xT", [P, KT, NT])
        xh, xl = put("xn_hi", [P, KT, NT], F32R), put("xn_lo", [P, KT, NT], F32R)
        blob = put("consts", [P, CW])
        ones = put("ones", [P, P])
        grow = put("gain_rows", [88, P])
        gains = put("gains", [P, 88])
        bif = put("b_if", [16, 1])
        K = {}
        off = 0
        for name, w in CONST.items():
            K[name] = blob[:, off:off + w]
            off += w
        ident = K["ident"]
        free0 = top[0]
        hmh, hml = put("hm_hi", [P, H, NT], F32R), put("hm_lo", [P, H, NT], F32R)
        ha0 = top[0]
        hah, hal = put("ha_hi", [P, H, NT], F32R), put("ha_lo", [P, H, NT], F32R)
        s0 = top[0]

        def norm_scratch(n, names):
            shapes = dict(sq=[4], tmp=[2, 4], ms=[], r=[], u=[])
            return [put(f"n{n}_{name}", [P] + shapes[name] + [NT]) for name in names]
        top[0] = free0
        first_scratch = norm_scratch(0, ("sq", "tmp", "ms", "r", "u"))

        top[0] = ha0
        htmp = put("m_htmp", [P, 2, NT])
        gT = at("m_gT", [16, NT], ha0)
        arow = at("m_arow", [H, 2, NT], ha0)
        gtok = put("m_gtok", [P, 3, 16])
        lf, btok, atok, m0tok, mt = [put(f"m_{n}", [P, 3, H]) for n in ("lf", "b", "a", "m0", "mt")]
        aT = put("m_aT", [H, NT])
        m0bc = put("m_m0bc", [P, NB * H])
        n0raw, n0T, nnew = put("m_n0", [64, P]), put("m_n0T", [P, 64]), put("m_nnew", [P, 64])
        nP = put("m_nP", [P, H])
        noutS, noutP = put("m_noutS", [64, P]), put("m_noutP", [H, P])
        mq, mk, mv, mo = [put(f"m_{n}T", [P, 2, NT]) for n in "qkvo"]
        mK, mV = put("m_Ktok", [P, 3, 2, P]), put("m_Vtok", [P, 3, 2, P + 1])
        C0 = put("m_C0", [P, 2, NB, P])
        vexp = put("m_vexp", [32, NB, P])
        X, swt = put("m_X", [P, 2, 416]), put("m_SwT", [P, 2, 416])
        hs = put("m_hs", [P, 3, 2, P + 1])
        kw = put("m_kw", [P, 2, 2, P])
        gm, g, ng, wprev, emm, wend, den, rden, rd2, ss, sc = [put(f"m_s{n}", [P, 3, 2]) for n in range(11)]
        decay = put("m_decay", [P, 2, NB])
        gl8, qn8, wsel = put("m_gl8", [32, 2, NB]), put("m_qn8", [32, 2, NB]), put("m_wsel", [32, 2, NB])
        qn = put("m_qn", [32, 2])
        qc, tq = put("m_qc", [P, 2, 32]), put("m_tq", [32, 2, P])
        cP = put("m_cP", [P, 2, P + 1])
        ntA = put("m_ntA", [P, 2, NB])

        top[0] = s0
        qs, ks = put("a_qs", [P, H, NS]), put("a_ks", [P, H, NS])
        Vs = put("a_Vs", [NS, H, P])
        aq, ak, av = [put(f"a_{n}T", [P, 2, NT]) for n in "qkv"]
        pX, pXT = put("a_P", [P, 2, 384]), put("a_PT", [P, 2, 384])
        kst, vst = put("a_kst", [P, 3, 2, P]), put("a_vst", [P, 3, 2, P])
        arm, asum = put("a_max", [P, 2, 2]), put("a_sum", [P, 2, 2])
        atmp = put("a_tmp", [P, 2, TP])

        dtab = put("d_table", [NS, PAST + OWN + NS])
        ptab = put("d_pages", [1, NB * PAGES], I32)
        moba_end = top[0]
        top[0] = s0 + 4 * (2 * H * NS + H * P)
        KTb = [put(f"d_KT{n}", [P, 4, P]) for n in range(2)]
        hsd = put("d_h", [P, H, NS])
        qpad = put("d_qpad", [P, H * (NS + TS)])
        gs, geq, pen = put("d_gate", [NS, BLOCKS]), put("d_eq", [NS, BLOCKS]), put("d_pen", [NS, BLOCKS])
        dmn, dmx, dsum = put("d_min", [NS, 1]), put("d_max", [NS, 1]), put("d_sum", [NS, 1])
        DP = put("d_P", [NS, PAST + NS])
        PT = put("d_PT", [P, PAGES + 1, NS])
        hrow = put("d_hrow", [NS, H * P])
        assert top[0] <= moba_end - 4 * (PAST + OWN + NS) - 4 * NB * PAGES

        top[0] = s0
        U = put("x_u", [P, KT, NT])
        sg = put("x_gates", [P, 4, NT])
        ut = put("x_tmp", [P, 2, NT])

        top[0] = s0
        memT = put("c_memT", [P, KT, MEM])
        behind = top[0]
        later_scratch = norm_scratch(1, ("sq", "tmp"))
        top[0] = free0
        mxh, mxl = put("c_mem_hi", [P, KT, MEM], F32R), put("c_mem_lo", [P, KT, MEM], F32R)
        later_scratch += norm_scratch(1, ("ms", "r", "u"))
        assert top[0] <= s0
        top[0] = s0
        mkT, mvT = put("c_mkT", [P, XH, MEM]), put("c_mvT", [P, XH, MEM])
        mKt, mVt = put("c_mKtok", [P, 2, XH * DH]), put("c_mVtok", [P, 2, XH * DH])
        assert top[0] <= behind

        top[0] = free0
        xrow = at("c_rows", [P, 2, XH * DH], free0)
        xP, xPT = put("c_P", [P, XH, 2, MEM]), put("c_PT", [P, XH, 2 * MEM])
        octx = put("c_ctx", [P, XH, NT])
        ctxh, ctxl = put("c_ctx_hi", [P, XH, NT], F32R), put("c_ctx_lo", [P, XH, NT], F32R)
        xmx, xsm = put("c_max", [P, XH, 2]), put("c_sum", [P, XH, 2])
        smx, ssm = put("c_smax", [P, 2]), put("c_ssum", [P, 2])
        xKT = [put(f"c_KT{n}", [P, 4, P]) for n in range(2)]
        assert top[0] <= s0
        top[0] = behind
        xq = put("c_qT", [P, XH, NT])
        xDP, xPTs = put("c_Ps", [P, 2, MEM]), put("c_PTs", [P, 4, P])
        xqpad = put("c_qpad", [P, NB, XH * (NS + TS)])

        top[0] = free0
        fah, fal = put("f_hi", [P, FH, NT], F32R), put("f_lo", [P, FH, NT], F32R)
        fg, fe, fa = [put(f"f_{n}", [P, 2, NT]) for n in ("g", "e", "a")]
        assert top[0] <= nc.sbuf_usable_end
        yout = at("y_tok", [P, 3, D], arena_at)

        B = [ctx.enter_context(nc.psum_tensor(f"bank{b}", [P, 512], F32)) for b in range(8)]
        G = B[0:2]

        PARAMS = 16 * 13
        ML_DVE, MO_DVE = 38, 7
        sqb = X[:].rearrange("p h c -> p (h c)")[:, 0:768].rearrange("p (r h c) -> p r h c", r=3, h=2)

        def sems(prefix, names):
            return [sem(prefix + n) for n in names.split()]
        const_in, ones_set, params_in, outs = sems("", "const_in ones_set params_in small_outputs_stored")
        landed = [sem(f"raw_landed{s}") for s in range(SLOTS)]
        slot_read = [sem(f"slot_read{s}") for s in range(SLOTS)]
        hi_ready, gemm_done = sems("", "hi_ready gemm_done")
        evac_done = [sem(f"evac_done{b}") for b in range(2)]
        tp_done, tp_even, tp_odd, gains_t, gains_set = sems("", "tp_done tp_even_copied tp_odd_copied gains_transposed gains_set")
        sq_ready, sq_odd, sq_used, ms_ready, ln_ready, r_ready, nt_ready, nh_ready, xn_ready = sems(
            "norm_", "sq_even_ready sq_odd_ready sq_used ms_ready ln_ready r_ready tmp_ready hi_ready xn_ready")
        dch, ach = sems("", "dve_order act_order")
        g_t, g_tok, g_abs, g_lf, g_cum, g_a, g_aT, g_aTs = sems(
            "gate_", "transposed tokens softplus lf cumsum a aT aT_copied")
        (m_mem, m_zero, m_arow, m_s1, m_g, m_em, m_w, m_ktr, m_kc, m_gl, m_gls, m_we, m_sw, m_s2, m_swt, m_kw,
         m_vx, m_s3, m_hs, m_sq, m_ms, m_sc, m_hsr, m_s4, m_tmp, m_hi, m_lo, m_cadd, m_cp, m_cdec, m_c0in, m_c0s,
         m_cps, m_vtr, m_vc, m_n, m_nt, m_no) = sems("m_", "buffers_set m0_zeroed arow scores g_ready em_ready "
            "w_ready k_transposed k_copied glast_psum glast_exponents wend_ready sw_ready sw_transposed swt_copied "
            "kw_ready vexp_ready numerators numerators_copied squares meansq rstd h_scaled "
            "h_transposed tmp_ready h_hi h_lo c_added cp_ready c_decayed c_in c_stored cp_stored v_transposed v_copied "
            "n_ready n_transposed n_out_ready")
        (a_s1, a_x, a_p, a_pn, a_ptr, a_ptc, a_pv, a_tmp, a_hi, a_lo, a_ktr, a_kc, a_vtr, a_vc, a_ks, a_vs, a_vcp) = sems(
            "a_", "scores x_ready p_ready p_scaled p_transposed pt_copied pv tmp_ready h_hi h_lo k_transposed k_copied "
            "v_transposed v_copied k_stored v_stored v_sample_copied")
        (d_tab, d_pg, d_q, d_tr, d_ss, d_kta, d_ktd, d_sc, d_sm, d_p, d_pn, d_ptr, d_ptc, d_pva, d_pvb, d_va, d_vb, d_ht, d_h,
         d_hi, d_lo) = sems("d_", "table_in pages_in q_ready k_transposed scores_done k_copied_even k_copied_odd scores_of_batch "
            "exponents_ready p_ready p_scaled p_transposed pt_copied pv_first_heads pv_last_heads "
            "h_rows_first h_rows_last h_transposed h_ready h_hi h_lo")
        x_p, x_pe, x_uhi, x_ulo = sems("x_", "products products_read u_hi u_lo")
        (c_kvt, c_kvc, c_out, c_s, c_x, c_p, c_pn, c_ptr, c_ptc, c_pv,
         c_sc, c_st, c_rows, c_sx, c_sp, c_spn, c_spt, c_spc, c_spv, c_ctx, c_chi, c_clo, c_xo) = sems("c_",
            "kv_transposed kv_copied kv_stored scores x_ready p_ready p_scaled p_transposed "
            "pt_copied pv s_scores_done s_h_rows s_h_transposed s_x_ready "
            "s_p_ready s_p_scaled s_p_transposed s_pt_copied s_pv ctx_ready ctx_hi ctx_lo xo_added")
        f_a, f_hi, f_lo = sems("f_", "a_ready hi lo")
        y_r, y_out = sems("y_", "rows_ready stored")
        block = ctx.enter_context(nc.Block())
        w_in = a["w_in"].rearrange("l (t p) n -> p (l t) n", p=P)

        def src256(s, j):
            return raw[s][:].rearrange("p (k c) -> p k c", c=256)[:, :, j * P:(j + 1) * P]

        def like(half, src):
            k, c = src.shape[1:]
            return half[:].rearrange("p k c -> p (k c)")[:, 0:k * c].rearrange("p (k c) -> p k c", c=c)

        def tok3(bank):
            return bank[:, 0:384].rearrange("p (r c) -> p r c", c=P)

        def xo_src(j):
            return raw[p_xo.slot(j // 2)][:].rearrange("p (k c) -> p k c", c=1024)[:, :, (j % 2) * 512:(j % 2) * 512 + 512]

        gate_src = raw[2][:, 0:KT * P].rearrange("p (k c) -> p k c", c=P)

        @block.sync
        def _(sp):
            sp.dma_start(blob[:], a["blob"]).then_inc(const_in, 16)

            def load(ph, i, u, dst, src):
                s = ph.slot(u)
                hold(sp, slot_read[s], ph.reads(i, u))
                sp.dma_start(dst, src).then_inc(landed[s], 16)

            def full(ph, u):
                return raw[ph.slot(u)][:].rearrange("p (k c) -> p k c", c=256)

            xp = a["x_prompt"].rearrange("b (t p) d -> (b t) p d", p=P)
            for t in range(2):
                sp.dma_start(raw[0][:, t * D:(t + 1) * D], xp[t]).then_inc(landed[0], 16)
            sp.dma_start(raw[1][0:NS, 0:D], a["x_sample"].rearrange("b t d -> (b t) d")).then_inc(landed[1], 16)
            load(p_gate, 0, 0, gate_src, w_in[:, :, W_IF:W_IF + P])
            for n, name in enumerate(("norm_mix", "norm_xattn", "norm_mem", "norm_ffn")):
                sp.dma_start(grow[16 * n:16 * n + 16, :], a[name].rearrange("l (k p) -> (l k) p", p=P)).then_inc(params_in, 16)
            sp.dma_start(grow[64:80, :], a["norm_final"].rearrange("(k p) -> k p", p=P)).then_inc(params_in, 16)
            sp.dma_start(grow[80:88, :], a["mh_gain"].rearrange("l (k p) -> (l k) p", p=P)).then_inc(params_in, 16)
            sp.dma_start(bif[:], a["b_if"].rearrange("l (k a) -> (l k) a", a=1)).then_inc(params_in, 16)
            sp.dma_start(n0raw[:], a["state_n"].rearrange("l b h d -> (l b h) d")).then_inc(params_in, 16)
            sp.dma_start(m0bc[:], a["state_m"].rearrange("l b h -> (l b h)").partition_broadcast(P)).then_inc(params_in, 16)
            sp.wait_ge(m_zero, 1)
            for t in range(TS):
                sp.dma_start(m0tok[t:NS:TS, 2, :], a["state_m"][0]).then_inc(params_in, 16)

            def ml(i):
                for u, part in enumerate((2, 0, 1, 3)):
                    load(p_ml, i, u, full(p_ml, u), w_in[:, :, ds(i * 256 + part * H * DH, 256)])

            def mo_(i):
                for u, part in enumerate((2, 0, 1)):
                    load(p_mo, i, u, full(p_mo, u), w_in[:, :, ds(i * 256 + (W_QA + part * H * DH), 256)])
            ml(0)
            with sp.Fori(1, 4) as i:
                ml(i)
            with sp.Fori(0, 4) as i:
                mo_(i)

            sp.wait_ge(a_s1, 1)
            sp.dma_start(dtab[:], a["dec"]).then_inc(d_tab, 16)
            sp.dma_start(ptab[:], a["page_table"].rearrange("b n -> (b n)").unsqueeze(0)).then_inc(d_pg, 16)
            sp.wait_ge(d_pg, 16)

            def pages(ph, i, u, b, first, cache):
                s = ph.slot(u)
                hold(sp, slot_read[s], ph.reads(i, u))
                for n in range(4):
                    page = sp.value_load(ptab[0:1, ds(b * PAGES + (first + n), 1)], min_val=0, max_val=N_PHYS - 1)
                    sp.dma_start(raw[s][:, n * H * DH:(n + 1) * H * DH],
                                 cache[0, ds(page, 1)].rearrange("a t h d -> (a t) (h d)")).then_inc(landed[s], 16)
            for u in range(2):
                pages(p_d0, 0, u, 0, 4 * u, a["cache_k"])
            with sp.Fori(1, NB) as b:
                for u in range(2):
                    pages(p_d, b - 1, u, b, 4 * u, a["cache_k"])
                for u in range(2):
                    pages(p_d, b - 1, 2 + u, b - 1, 4 * u, a["cache_v"])
            for u in range(2):
                pages(p_d8, 0, u, NB - 1, 4 * u, a["cache_v"])

            def wt(name):
                return a[name].rearrange("l (t p) n -> p (l t) n", p=P)
            w_pm, w_pa, w_out = wt("w_proj_m"), wt("w_proj_a"), wt("w_out")
            with sp.Fori(0, 8) as i:
                load(p_mx, i, 0, full(p_mx, 0), w_in[:, :, ds(i * 256 + W_GM, 256)])
                load(p_mx, i, 1, full(p_mx, 1), w_in[:, :, ds(i * 256 + W_GA, 256)])
                load(p_mx, i, 2, full(p_mx, 2)[:, 0:8], w_pm[:, :, ds(i * 256, 256)])
                sp.dma_start(full(p_mx, 2)[:, 8:16], w_pa[:, :, ds(i * 256, 256)]).then_inc(landed[p_mx.slot(2)], 16)

            def wo_loads(i):
                for u in range(2):
                    load(p_wo, i, u, full(p_wo, u), w_out[:, :, ds(i * 512 + u * 256, 256)])
            wo_loads(0)

            mp = a["mem_prompt"].rearrange("b (t p) d -> (b t) p d", p=P)
            load(p_min, 0, 0, raw[2][:, 0:D], mp[0])
            sp.dma_start(raw[2][:, D:2 * D], mp[1]).then_inc(landed[2], 16)
            with sp.Fori(1, 4) as i:
                wo_loads(i)
            for u in range(4):
                load(p_mem, 0, u, full(p_mem, u), wt(("w_xv", "w_xk")[u // 2])[:, :, (u % 2) * 256:(u % 2) * 256 + 256])
            for u in range(2):
                load(p_xq, 0, u, full(p_xq, u), wt("w_xq")[:, :, u * 256:u * 256 + 256])
            for ph, name in ((p_xk, "cache_mem_k"), (p_xv, "cache_mem_v")):
                for u in range(2):
                    load(ph, 0, u, raw[ph.slot(u)][:].rearrange("p (b c) -> p b c", c=XH * DH),
                         a[name][0, 4 * u:4 * u + 4].rearrange("b (m p) h d -> p (b m) (h d)", p=P))
            for u in range(2):
                load(p_xo, 0, u, raw[p_xo.slot(u)][:].rearrange("p (k c) -> p k c", c=1024), wt("w_xo")[:, :, u * 1024:(u + 1) * 1024])
            w_g, w_u, w_d = wt("w_ffn_gate"), wt("w_ffn_up"), wt("w_ffn_down")
            for f in range(2):
                with sp.Fori(0, FH // 2) as i:
                    load(p_up[f], i, 0, full(p_up[f], 0), w_g[:, :, ds(i * 256 + f * FH * P, 256)])
                    load(p_up[f], i, 1, full(p_up[f], 1), w_u[:, :, ds(i * 256 + f * FH * P, 256)])
                with sp.Fori(0, 8) as i:
                    for u in range(2):
                        k0 = f * FH + u * FU
                        load(p_dn[f], i, u, full(p_dn[f], u)[:, 0:FU], w_d[:, k0:k0 + FU, ds(i * 256, 256)])

        @block.gpsimd
        def _(gp):
            nc.gpsimd.memset(ones[:], 1.0).then_inc(ones_set, 1)
            nc.gpsimd.memset(m0tok[:], 0.0).then_inc(m_zero, 1)
            for buf in (gtok, gm, wend, hs):
                nc.gpsimd.memset(buf[:], 0.0)
            nc.gpsimd.memset(mV[:], 1.0).then_inc(m_mem, 1)
            cs = a["state_C"].rearrange("l b h k v -> k (l h) b v")
            co = o["C_sample"].rearrange("l b h k v -> k (l h) b v")
            cpo = o["C_prompt"].rearrange("l b h k v -> k (l b h) v")

            def load_c(i):
                for hh in range(2):
                    gp.dma_start(C0[:, hh, :, :], cs[:, ds(2 * i + hh, 1), :, :].rearrange("k h b v -> k (h b) v")).then_inc(m_c0in, 16)

            def update(i):
                hold(gp, m_s1, i + 1)
                hold(gp, m_we, 2 * i + 2)
                for hh in range(2):
                    nc.gpsimd.tensor_tensor(C0[:, hh, :, :], C0[:, hh, :, :], decay[:, hh, :].unsqueeze(2).broadcast_to([P, NB, P]),
                                            ALU.mult).then_inc(m_cdec, 1)
                hold(gp, m_cp, i + 1)
                gp.dma_start(cpo[:, ds(2 * i, 2), :], cP[:, :, 0:P]).then_inc(m_cps, 16)
                for hh in range(2):
                    hold(gp, m_cadd, 2 * i + hh + 1)
                    gp.dma_start(co[:, ds(2 * i + hh, 1), :, :].rearrange("k h b v -> k (h b) v"), C0[:, hh, :, :]).then_inc(m_c0s, 16)
            load_c(0)
            with gp.Fori(0, 3) as i:
                update(i)
                hold(gp, m_c0s, 32 * i + 32)
                load_c(i + 1)
            update(3)
            gp.wait_ge(m_no, 2)
            gp.dma_start(o["m_prompt"].rearrange("l b h -> (l b) h"), mt[P - 1:P, 1, :]).then_inc(outs, 16)
            gp.dma_start(o["m_sample"].rearrange("l b h -> (l b) h"), mt[TS - 1:NS:TS, 2, :]).then_inc(outs, 16)
            gp.dma_start(o["n_sample"].rearrange("l b h d -> (l b h) d"), noutS[:]).then_inc(outs, 16)
            gp.dma_start(o["n_prompt"].rearrange("l b h d -> (l b h) d"), noutP[:]).then_inc(outs, 16)

            def store_kv(i, ready, stored, st, op, os_):
                hold(gp, ready, i + 1)
                for t in range(2):
                    gp.dma_start(op[0, 0, t * P:(t + 1) * P, ds(2 * i, 2), :], st[:, t, :, :]).then_inc(stored, 16)
                gp.dma_start(os_.rearrange("l b t h d -> (l b t) h d")[:, ds(2 * i, 2), :], st[0:NS, 2, :, :]).then_inc(stored, 16)
            with gp.Fori(0, 4) as i:
                store_kv(i, a_vc, a_vs, vst, o["v_prompt"], o["v_sample"])
                nc.gpsimd.tensor_copy(Vs[:, ds(2 * i, 2), :], vst[0:NS, 2, :, :]).then_inc(a_vcp, 1)
                store_kv(i, a_kc, a_ks, kst, o["k_prompt"], o["k_sample"])
            gp.wait_ge(c_kvc, 4)
            for st, name in ((mVt, "mem_v_prompt"), (mKt, "mem_k_prompt")):
                for t in range(2):
                    gp.dma_start(o[name][0, 0, t * P:(t + 1) * P].rearrange("t h d -> t (h d)"), st[:, t, :]).then_inc(c_out, 16)
            yp = o["y_prompt"].rearrange("b (t p) d -> (b t) p d", p=P)
            for t in range(3):
                gp.wait_ge(tp_even, 9 + 2 * t + 2)
                gp.wait_ge(tp_odd, 8 + 2 * t + 2)
                dst = yp[t] if t < 2 else o["y_sample"].rearrange("b t d -> (b t) d")
                gp.dma_start(dst, yout[0:(P, P, NS)[t], t, :]).then_inc(y_out, 16)
            gp.wait_ge(c_out, 64)
            gp.wait_ge(y_out, 48)
            gp.wait_ge(m_c0s, 128)
            gp.wait_ge(m_cps, 64)
            gp.wait_ge(a_ks, 16 * 12)
            gp.wait_ge(a_vs, 16 * 12)
            gp.wait_ge(outs, 64)

        @block.scalar
        def _(act):
            ac = Chain(act, ach)

            def hi(ph, i, u, c, src):
                act.wait_ge(landed[ph.slot(u)], ph.landed(i, u))
                wait(act, gemm_done, ph.conv(i, c - 1))
                nc.scalar.activation(like(wh[ph.half(c)], src), src, ACT.Copy).then_inc(hi_ready, 1)

            def norm(q, src, n):
                sq, _, nms, nr, nu = later_scratch if q else first_scratch
                for k in range(0, KT, 2):
                    wait(act, sq_used, KT * q + k - 3)
                    nc.scalar.activation(sq[:, k % 4, 0:n], src[:, k, :], ACT.Square).then_inc(sq_ready, 1)
                act.wait_ge(ms_ready, q + 1)
                nc.scalar.activation(nu[:, 0:n], nms[:, 0:n], ACT.Ln).then_inc(ln_ready, 1)
                act.wait_ge(ln_ready, q + 1)
                nc.scalar.activation(nr[:, 0:n], nu[:, 0:n], ACT.Exp, scale=-0.5).then_inc(r_ready, 1)

            def norm_hi(q, n, g_, dst):
                ntmp = (later_scratch if q else first_scratch)[1]
                act.wait_ge(nt_ready, 4 * q + g_ + 1)
                nc.scalar.activation(dst[:, 4 * g_:4 * g_ + 4, 0:n], ntmp[:, g_ % 2, :, 0:n], ACT.Copy).then_inc(nh_ready, 1)

            for n in (0, 2, 4, 6, 8):
                act.wait_ge(tp_done, n + 1)
                if n < 8:
                    t, k4 = n // 4, n % 4
                    nc.scalar.activation(xT[:, 4 * k4:4 * k4 + 4, t * P:(t + 1) * P],
                                         B[2 + n % 4][:].rearrange("p (k c) -> p k c", c=P), ACT.Copy).then_inc(tp_even, 1)
                else:
                    nc.scalar.activation(xT[:, :, TP:NT], B[2][:].rearrange("p (k c) -> p k c", c=NS), ACT.Copy).then_inc(tp_even, 1)
            act.wait_ge(tp_even, 5)
            act.wait_ge(tp_odd, 4)
            hi(p_gate, 0, 0, 0, gate_src)
            norm(0, xT, NT)
            for g_ in range(4):
                norm_hi(0, NT, g_, xh)

            act.wait_ge(params_in, PARAMS)
            act.wait_ge(gemm_done, 1)
            nc.scalar.activation(gT[:], G[0][0:16, 0:NT], ACT.Identity, bias=bif[:]).then_inc(evac_done[0], 1)
            act.wait_ge(g_tok, 1)
            ac.run(nc.scalar.activation(lf[:], gtok[:, :, H:2 * H], ACT.Abs))
            ac.sync()
            ac.run(nc.scalar.activation(lf[:], lf[:], ACT.Exp, scale=-1.0))
            ac.sync()
            nc.scalar.activation(lf[:], lf[:], ACT.Ln, bias=1.0).then_inc(g_abs, 1)

            def ml_evac(i, t):
                u, hh = t // 2, t % 2
                act.wait_ge(gemm_done, p_ml.conv(i, t + 1))
                src = G[p_ml.bank(t)][:, 0:NT]
                if u == 3:
                    ins = nc.scalar.activation(mo[:, hh, :], src, ACT.Exp, scale=-1.0)
                else:
                    ins = nc.scalar.activation((mv, mq, mk)[u][:, hh, :], src, ACT.Copy, scale=SCALE if u == 2 else 1.0)
                ins.then_inc(evac_done[p_ml.bank(t)], 1)

            def ml_attn(p, j):
                if j == 0:
                    act.wait_ge(m_g, p + 1)
                    nc.scalar.activation(wprev[:], wprev[:], ACT.Exp).then_inc(m_em, 1)
                    nc.scalar.activation(emm[:], emm[:], ACT.Exp).then_inc(m_em, 1)
                    for hh in range(2):
                        nc.scalar.activation(X[:, hh, 0:P], X[:, hh, 0:P], ACT.Exp, bias=ng[:, 0, hh:hh + 1])
                        nc.scalar.activation(X[:, hh, P:384], X[:, hh, P:384], ACT.Exp, bias=ng[:, 1, hh:hh + 1])
                        nc.scalar.activation(X[0:32, hh, 384:416], X[0:32, hh, 384:416], ACT.Exp,
                                             bias=ng[0:32, 2, hh:hh + 1]).then_inc(m_w, 1)
                if j == 1:
                    act.wait_ge(m_gls, p + 1)
                    nc.scalar.activation(wend[:], wend[:], ACT.Exp).then_inc(m_we, 1)
                    nc.scalar.activation(decay[:], decay[:], ACT.Exp).then_inc(m_we, 1)
                    act.wait_ge(m_ktr, p + 1)
                    for hh in range(2):
                        src = tok3(B[7 - hh])
                        nc.scalar.activation(mK[:, 0:2, hh, :], src[:, 0:2, :], ACT.Copy)
                        nc.scalar.activation(mK[0:32, 2, hh, :], src[0:32, 2, :], ACT.Copy).then_inc(m_kc, 1)
                if j == 2:
                    act.wait_ge(m_s2, p + 1)
                    for hh in range(2):
                        nc.scalar.activation(swt[:, hh, 0:384], B[4 + hh][:, 0:384], ACT.Copy)
                        nc.scalar.activation(swt[0:32, hh, 384:416], B[4 + hh][0:32, 384:416], ACT.Copy).then_inc(m_swt, 1)
                if j == 3:
                    act.wait_ge(m_hs, p + 1)
                    nc.scalar.activation(sqb, hs[:, :, :, 0:P], ACT.Square).then_inc(m_sq, 1)
                    act.wait_ge(m_ms, p + 1)
                    ac.run(nc.scalar.activation(ss[:], ss[:], ACT.Ln))
                    ac.sync()
                    nc.scalar.activation(ss[:], ss[:], ACT.Exp, scale=-0.5).then_inc(m_sc, 1)
                if j == 5:
                    act.wait_ge(m_tmp, 2 * p + 2)
                    nc.scalar.activation(hmh[:, ds(2 * p, 2), :], htmp[:], ACT.Copy).then_inc(m_hi, 1)

            def ml_body(i, gemm, attn):
                for j in range(8):
                    if gemm:
                        hi(p_ml, i, j // 2, j, src256(p_ml.slot(j // 2), j % 2))
                        if j >= 2:
                            ml_evac(i, j - 2)
                    if attn:
                        if j < 2:
                            ml_evac(i - 1, 6 + j)
                        ml_attn(i - 1, j)
                    if not gemm and 0 < j < 3:
                        hi(p_mo, 0, 0, j - 1, src256(p_mo.slot(0), j - 1))
                    if gemm and j == 5:
                        act.wait_ge(m_vtr, i + 1)
                        for hh in range(2):
                            src = tok3(B[6 + hh])
                            nc.scalar.activation(mV[:, 0:2, hh, 0:P], src[:, 0:2, :], ACT.Copy)
                            nc.scalar.activation(mV[0:32, 2, hh, 0:P], src[0:32, 2, :], ACT.Copy).then_inc(m_vc, 1)
            act.wait_ge(m_mem, 1)
            ml_body(0, True, False)
            with act.Fori(1, 4) as i:
                ac.loop(i - 1, 1)
                ml_body(i, True, True)
            ac.loop(3, 1)
            ml_body(4, False, True)
            ac.end(4)

            def mo_evac(i, t):
                u, hh = t // 2, t % 2
                act.wait_ge(gemm_done, p_mo.conv(i, t + 1))
                src = G[p_mo.bank(t)]
                scale = SCALE if u == 1 else 1.0
                if u:
                    nc.scalar.activation((qs, ks)[u - 1][:, ds(2 * i + hh, 1), :], src[:, TP:NT].unsqueeze(1), ACT.Copy, scale=scale)
                nc.scalar.activation((av, aq, ak)[u][:, hh, :], src[:, 0:NT], ACT.Copy, scale=scale).then_inc(evac_done[p_mo.bank(t)], 1)

            def tok_copy(transposed, n, banks, dst, copied):
                act.wait_ge(transposed, n)
                for hh in range(2):
                    src = tok3(banks[hh])
                    nc.scalar.activation(dst[:, 0:2, hh, :], src[:, 0:2, :], ACT.Copy)
                    last = nc.scalar.activation(dst[0:32, 2, hh, :], src[0:32, 2, :], ACT.Copy)
                last.then_inc(copied, 1)

            def mo_attn(p, j):
                if j == 2:
                    act.wait_ge(a_x, p + 1)
                    for hh in range(2):
                        nc.scalar.activation(pX[:, hh, 0:P], pX[:, hh, 0:P], ACT.Exp, bias=arm[:, hh, 0:1], accum_out=asum[:, hh, 0:1])
                        last = nc.scalar.activation(pX[:, hh, P:384], pX[:, hh, P:384], ACT.Exp, bias=arm[:, hh, 1:2], accum_out=asum[:, hh, 1:2])
                    last.then_inc(a_p, 1)
                if j == 3:
                    act.wait_ge(a_ptr, p + 1)
                    for hh in range(2):
                        last = nc.scalar.activation(pXT[:, hh, :], B[4 + hh][:, 0:384], ACT.Copy)
                    last.then_inc(a_ptc, 1)
                    tok_copy(a_ktr, p + 1, (B[7], B[2]), kst, a_kc)
                if j == 4:
                    act.wait_ge(a_tmp, p + 1)
                    nc.scalar.activation(hah[:, ds(2 * p, 2), 0:TP], atmp[:], ACT.Copy).then_inc(a_hi, 1)
                if j == 5:
                    act.wait_ge(a_ks, 48 * p + 48)

            def mo_body(i, gemm, attn):
                for j in range(6):
                    if gemm and (attn or j >= 2):
                        hi(p_mo, i, j // 2, j, src256(p_mo.slot(j // 2), j % 2))
                        if j == 2 and not attn:
                            act.wait_ge(m_c0s, 128)
                            act.wait_ge(m_cps, 64)
                            act.wait_ge(outs, 64)
                    if gemm and j >= 2:
                        mo_evac(i, j - 2)
                    if attn:
                        if j < 2:
                            mo_evac(i - 1, 4 + j)
                        mo_attn(i - 1, j)
                    if gemm and j == 5:
                        wait(act, a_vs, 48 * i)
                        wait(act, a_vcp, i)
                        tok_copy(a_vtr, i + 1, (B[4], B[5]), vst, a_vc)
            mo_body(0, True, False)
            with act.Fori(1, 4) as i:
                mo_body(i, True, True)
            mo_body(4, False, True)

            def k_copies(kts, tr_sem, ss_sem, mine, base, i, parity, copy, between=None):
                for n in range(parity, 16, 2):
                    act.wait_ge(tr_sem, i * 16 + (base + n + 1))
                    act.wait_ge(ss_sem, i * 16 + (base + n + 1))
                    copy(kts[n % 2][:], B[2 + n % 4][:].rearrange("p (h c) -> p h c", c=P)).then_inc(mine, 1)
                    if n == 4 and between:
                        between()

            def a_copy(dst, src):
                return nc.scalar.activation(dst, src, ACT.Copy)

            def d_batch(b, k, v):
                def pt_copy():
                    act.wait_ge(d_ptr, b)
                    a_copy(PT[:, 0:PAGES, :], B[0][:, 0:PAGES * NS].rearrange("p (n c) -> p n c", c=NS))
                    a_copy(PT[0:NS, PAGES, :], B[0][0:NS, PAGES * NS:(PAGES + 1) * NS]).then_inc(d_ptc, 1)
                if k:
                    k_copies(KTb, d_tr, d_ss, d_kta, 0, b, 0, a_copy, pt_copy if v else None)
                    act.wait_ge(d_sm, b + 1)
                    nc.scalar.activation(DP[:], DP[:], ACT.Exp, bias=dmx[:], accum_out=dsum[:]).then_inc(d_p, 1)
                else:
                    pt_copy()
                if v:
                    act.wait_ge(d_pva, b)
                    a_copy(hrow[:, 0:4 * P], B[2][0:NS, :]).then_inc(d_va, 1)
            d_batch(0, True, False)
            with act.Fori(1, NB) as b:
                d_batch(b, True, True)
            d_batch(NB, False, True)
            act.wait_ge(d_h, NB + 1)
            a_copy(hah[:, :, TP:NT], hsd[:]).then_inc(d_hi, 1)

            def mx_evac(i, t):
                act.wait_ge(gemm_done, p_mx.conv(i, t + 1))
                nc.scalar.activation(sg[:, t, :], G[p_mx.bank(t)][:, 0:NT], ACT.Exp, scale=-1.0).then_inc(evac_done[p_mx.bank(t)], 1)

            def mx_body(i):
                for j in range(6):
                    hi(p_mx, i, j // 2, j, src256(p_mx.slot(j // 2), j % 2))
                    if j == 2:
                        act.wait_ge(x_pe, 4 * i + 4)
                    if j >= 2:
                        mx_evac(i, j - 2)
            with act.Fori(0, 8) as i:
                mx_body(i)
            hi(p_wo, 0, 0, 0, src256(p_wo.slot(0), 0))
            act.wait_ge(x_pe, 4 * 8 + 4)
            for q in range(4):
                a_copy(xh[:, 4 * q:4 * q + 4, :], U[:, 4 * q:4 * q + 4, :]).then_inc(x_uhi, 1)
            for j in range(1, 4):
                hi(p_wo, 0, j // 2, j, src256(p_wo.slot(j // 2), j % 2))
            for n in (0, 2, 4, 6):
                act.wait_ge(tp_done, 9 + n + 1)
                t, k4 = n // 4, n % 4
                a_copy(memT[:, 4 * k4:4 * k4 + 4, t * P:(t + 1) * P], B[2 + n % 4][:].rearrange("p (k c) -> p k c", c=P)).then_inc(tp_even, 1)
            with act.Fori(1, 3) as i:
                for j in range(4):
                    hi(p_wo, i, j // 2, j, src256(p_wo.slot(j // 2), j % 2))

            def mem_hi(j):
                hi(p_mem, 0, j // 2, j, src256(p_mem.slot(j // 2), j % 2))

            def mem_evac(t):
                act.wait_ge(gemm_done, p_mem.conv(0, t + 1))
                a_copy((mvT, mkT)[t // 4][:, t % 4, :], G[p_mem.bank(t)][:, 0:MEM]).then_inc(evac_done[p_mem.bank(t)], 1)

            def xq_hi(j):
                hi(p_xq, 0, j // 2, j, src256(p_xq.slot(j // 2), j % 2))
            for j in range(4):
                hi(p_wo, 3, j // 2, j, src256(p_wo.slot(j // 2), j % 2))
                if j == 0:
                    act.wait_ge(tp_even, 5 + 4)
                    act.wait_ge(tp_odd, 4 + 4)
                    norm(1, memT, MEM)
                else:
                    norm_hi(1, MEM, j - 1, mxh)
            mem_hi(0)
            norm_hi(1, MEM, 3, mxh)
            mem_hi(1)
            for j in range(2, 8):
                mem_hi(j)
                mem_evac(j - 2)
                if j == 4:
                    act.wait_ge(evac_done[0], p_mem.evacs(0, (0 + p_mem.tile0) % 2))
                    act.wait_ge(evac_done[1], p_mem.evacs(0, (1 + p_mem.tile0) % 2))
                    norm(2, xT, NT)
                if j > 4:
                    norm_hi(2, NT, j - 5, xh)
            xq_hi(0)
            mem_evac(6)
            norm_hi(2, NT, 3, xh)
            xq_hi(1)
            mem_evac(7)
            for n in range(4):
                act.wait_ge(c_kvt, n + 1)
                a_copy((mVt, mKt)[n // 2][:, n % 2, :], B[2 + n][:]).then_inc(c_kvc, 1)
            for j in range(2, 6):
                if j < 4:
                    xq_hi(j)
                t = j - 2
                act.wait_ge(gemm_done, p_xq.conv(0, t + 1))
                nc.scalar.activation(xq[:, t, :], G[p_xq.bank(t)][:, 0:NT], ACT.Copy, scale=SCALE).then_inc(evac_done[p_xq.bank(t)], 1)
            act.wait_ge(c_x, 1)
            for h in range(XH):
                for r in range(2):
                    last = nc.scalar.activation(xP[:, h, r, :], xP[:, h, r, :], ACT.Exp, bias=xmx[:, h, r:r + 1], accum_out=xsm[:, h, r:r + 1])
            last.then_inc(c_p, 1)
            k_copies(xKT, d_tr, d_ss, d_kta, 128, 0, 0, a_copy)
            act.wait_ge(c_ptr, 1)
            for h in range(XH):
                last = a_copy(xPT[:, h, :], B[2 + h][:])
            last.then_inc(c_ptc, 1)
            act.wait_ge(c_sx, 1)
            for u in range(2):
                last = nc.scalar.activation(xDP[:, u, :], xDP[:, u, :], ACT.Exp, bias=smx[:, u:u + 1], accum_out=ssm[:, u:u + 1])
            last.then_inc(c_sp, 1)
            act.wait_ge(c_spt, 1)
            a_copy(xPTs[:], B[2][:].rearrange("p (m c) -> p m c", c=P)).then_inc(c_spc, 1)
            act.wait_ge(c_ctx, 3)
            a_copy(ctxh[:], octx[:]).then_inc(c_chi, 1)
            for j in range(4):
                hi(p_xo, 0, j // 2, j, xo_src(j))

            act.wait_ge(c_xo, 4)
            act.wait_ge(c_out, 64)
            hi(p_up[0], 0, 0, 0, src256(p_up[0].slot(0), 0))
            norm(3, xT, NT)
            for g_ in range(4):
                norm_hi(3, NT, g_, xh)

            def up_evac(f, i, t):
                ph = p_up[f]
                act.wait_ge(gemm_done, ph.conv(i, t + 1))
                a_copy(fg[:, t, :], G[ph.bank(t)][:, 0:NT])
                nc.scalar.activation(fe[:, t, :], G[ph.bank(t)][:, 0:NT], ACT.Exp, scale=-1.0).then_inc(evac_done[ph.bank(t)], 1)

            def up_hi(f, i):
                act.wait_ge(f_a, i * 2 + (2 + f * FH))
                a_copy(fah[:, ds(i * 2, 2), :], fa[:]).then_inc(f_hi, 1)

            def up_body(f, i, first):
                for j in range(4):
                    if j or f or not first:
                        hi(p_up[f], i, j // 2, j, src256(p_up[f].slot(j // 2), j % 2))
                    if j == 2 and not first:
                        up_hi(f, i - 1)
                    if j >= 2:
                        up_evac(f, i, j - 2)
            for f in range(2):
                up_body(f, 0, True)
                with act.Fori(1, FH // 2) as i:
                    up_body(f, i, False)

                def dn_hi(i, j):
                    hi(p_dn[f], i, j // 2, j, src256(p_dn[f].slot(j // 2), j % 2)[:, 0:FU])
                dn_hi(0, 0)
                up_hi(f, FH // 2 - 1)
                for j in range(1, 4):
                    dn_hi(0, j)
                with act.Fori(1, 8) as i:
                    for j in range(4):
                        dn_hi(i, j)
            act.wait_ge(evac_done[p_dn[1].bank(0)], p_dn[1].evacs(8, 0))
            act.wait_ge(evac_done[p_dn[1].bank(1)], p_dn[1].evacs(8, 1))
            norm(4, xT, NT)
            for n in range(0, 12, 2):
                act.wait_ge(tp_done, 17 + n + 1)
                rows_ = (P, P, NS)[n // 4]
                a_copy(yout[0:rows_, n // 4, (n % 4) * 512:(n % 4) * 512 + 512], B[2 + n % 4][0:rows_, :]).then_inc(tp_even, 1)

        @block.vector
        def _(dve):
            dc = Chain(dve, dch)

            def lo(ph, i, u, c, src):
                dve.wait_ge(hi_ready, ph.conv(i, c + 1))
                nc.vector.tensor_tensor(like(wl[ph.half(c)], src), src, like(wh[ph.half(c)], src).bitcast(F32),
                                        ALU.subtract).then_inc(slot_read[ph.slot(u)], 1)

            def norm(q, src, n, lo_first=None):
                sq, _, nms, nr, nu = later_scratch if q else first_scratch
                for k in range(1, KT, 2):
                    wait(dve, sq_used, KT * q + k - 3)
                    nc.vector.tensor_tensor(sq[:, k % 4, 0:n], src[:, k, :], src[:, k, :], ALU.mult).then_inc(sq_odd, 1)
                if lo_first:
                    lo_first()
                dve.wait_ge(sq_used, KT * (q + 1))
                nc.vector.tensor_scalar(nms[:, 0:n], B[2][:, 0:n], 1.0 / D, EPS, ALU.mult, ALU.add).then_inc(ms_ready, 1)
                dve.wait_ge(r_ready, q + 1)
                dve.wait_ge(ms_ready, q + 1)
                dc.run(nc.vector.tensor_tensor(nu[:, 0:n], nr[:, 0:n], nr[:, 0:n], ALU.mult))
                dc.sync()
                dc.run(nc.vector.tensor_tensor(nu[:, 0:n], nu[:, 0:n], nms[:, 0:n], ALU.mult))
                dc.sync()
                dc.run(nc.vector.tensor_scalar(nu[:, 0:n], nu[:, 0:n], -0.5, 1.5, ALU.mult, ALU.add))
                dc.sync()
                dc.run(nc.vector.tensor_tensor(nr[:, 0:n], nr[:, 0:n], nu[:, 0:n], ALU.mult))
                dc.sync()

            def norm_x(q, src, gain, n, g_):
                _, ntmp, _, nr, _ = later_scratch if q else first_scratch
                if g_ >= 2:
                    dve.wait_ge(xn_ready, 4 * q + g_ - 1)
                for m in range(4):
                    k = 4 * g_ + m
                    last = nc.vector.scalar_tensor_tensor(ntmp[:, g_ % 2, m, 0:n], src[:, k, :], gains[:, gain + k:gain + k + 1],
                                                          nr[:, 0:n], ALU.mult, ALU.mult)
                last.then_inc(nt_ready, 1)

            def norm_lo(q, n, g_, dh, dl):
                ntmp = (later_scratch if q else first_scratch)[1]
                dve.wait_ge(nh_ready, 4 * q + g_ + 1)
                nc.vector.tensor_tensor(dl[:, 4 * g_:4 * g_ + 4, 0:n], ntmp[:, g_ % 2, :, 0:n],
                                        dh[:, 4 * g_:4 * g_ + 4, 0:n].bitcast(F32), ALU.subtract).then_inc(xn_ready, 1)

            def norm_step(q, src, gain, n, g_, dh, dl):
                norm_x(q, src, gain, n, g_)
                if g_:
                    norm_lo(q, n, g_ - 1, dh, dl)
                if g_ == 3:
                    norm_lo(q, n, 3, dh, dl)

            def norm_apply(q, src, gain, n):
                for g_ in range(4):
                    norm_step(q, src, gain, n, g_, xh, xl)

            for n in (1, 3, 5, 7):
                dve.wait_ge(tp_done, n + 1)
                t, k4 = n // 4, n % 4
                nc.vector.tensor_copy(xT[:, 4 * k4:4 * k4 + 4, t * P:(t + 1) * P],
                                      B[2 + n % 4][:].rearrange("p (k c) -> p k c", c=P)).then_inc(tp_odd, 1)
            dve.wait_ge(gains_t, 1)
            nc.vector.tensor_copy(gains[:], B[6][:, 0:88]).then_inc(gains_set, 1)
            nc.vector.tensor_copy(n0T[:], B[7][:, 0:64]).then_inc(gains_set, 1)
            dve.wait_ge(gains_set, 2)
            dve.wait_ge(tp_even, 5)
            dve.wait_ge(tp_odd, 4)
            norm(0, xT, NT, lambda: lo(p_gate, 0, 0, 0, gate_src))
            norm_apply(0, xT, 0, NT)
            dve.wait_ge(g_t, 1)
            dve.wait_ge(m_mem, 1)
            dc.run(nc.vector.tensor_copy(gtok[:, 0:2, :], B[3][:, 0:32].rearrange("p (r c) -> p r c", c=16)))
            nc.vector.tensor_copy(gtok[0:32, 2, :], B[3][0:32, 32:48]).then_inc(g_tok, 1)
            dve.wait_ge(g_tok, 1)
            dve.wait_ge(g_abs, 1)
            dc.sync()
            nc.vector.scalar_tensor_tensor(lf[:], gtok[:, :, H:2 * H], 0.0, lf[:], ALU.min, ALU.subtract).then_inc(g_lf, 1)
            dc.run(nc.vector.memset(btok[:], 0.0))
            dc.sync()
            dve.wait_ge(g_cum, 1)
            dc.run(nc.vector.tensor_copy(btok[:, 0:2, :], B[4][:, 0:16].rearrange("p (r c) -> p r c", c=H)))
            dc.run(nc.vector.tensor_copy(btok[0:32, 2, :], B[4][0:32, 16:24]))
            dc.sync()
            nc.vector.tensor_tensor(atok[:], gtok[:, :, 0:H], btok[:], ALU.subtract).then_inc(g_a, 1)
            dve.wait_ge(g_aT, 1)
            nc.vector.tensor_copy(aT[:], B[5][0:H, 0:NT]).then_inc(g_aTs, 1)
            dve.wait_ge(g_aTs, 1)
            dve.wait_ge(params_in, PARAMS)
            m0v = m0bc[:].rearrange("p (b h) -> p h b", h=H)
            n0v = n0T[:].rearrange("p (b h) -> p h b", h=H)
            nnv = nnew[:].rearrange("p (b h) -> p h b", h=H)

            def ml_arow(p):
                for hh in range(2):
                    nc.vector.tensor_scalar(arow[:, hh, :], aT[:], ident[0:H, ds(2 * p + hh, 1)], None, ALU.mult).then_inc(m_arow, 1)

            def vexp_of(hh):
                nc.vector.tensor_tensor(vexp[:], mV[0:32, 2, hh, 0:P].unsqueeze(1).broadcast_to([32, NB, P]),
                                        wsel[:, hh, :].unsqueeze(2).broadcast_to([32, NB, P]), ALU.mult).then_inc(m_vx, 1)

            def c_add(p, hh):
                dve.wait_ge(m_cdec, 2 * p + hh + 1)
                for q in range(2):
                    half = C0[:, hh, 4 * q:4 * q + 4, :].rearrange("p b v -> p (b v)")
                    last = nc.vector.tensor_tensor(half, half, B[4 + q][:, :], ALU.add)
                last.then_inc(m_cadd, 1)

            def ml_attn(p, j):
                pair = ds(2 * p, 2)
                if j == 0:
                    dve.wait_ge(m_s1, p + 1)
                    dc.run(nc.vector.tensor_copy(qc[:], B[6][:, 0:64].rearrange("p (h c) -> p h c", h=2)))
                    dc.run(nc.vector.tensor_tensor(qn8[:], B[6][0:32, 64:80].rearrange("p (h b) -> p h b", b=NB),
                                                   K["bmask"][0:32].unsqueeze(1).broadcast_to([32, 2, NB]), ALU.mult))
                    for hh in range(2):
                        A = B[4 + hh]
                        dc.run(nc.vector.tensor_tensor_reduce(out=X[:, hh, 0:P], in0=A[:, 0:P], in1=K["cadd"][:, 0:P], scale=1.0,
                                                              scalar=NEG, op0=ALU.add, op1=ALU.max, accum_out=gm[:, 0, hh:hh + 1]))
                        dc.run(nc.vector.tensor_tensor_reduce(out=X[:, hh, P:384], in0=A[:, 0:TP], in1=K["cadd"][:, P:384], scale=1.0,
                                                              scalar=NEG, op0=ALU.add, op1=ALU.max, accum_out=gm[:, 1, hh:hh + 1]))
                        dc.run(nc.vector.tensor_tensor_reduce(out=X[0:32, hh, 384:416], in0=A[0:32, TP:NT], in1=K["sadd"][0:32], scale=1.0,
                                                              scalar=NEG, op0=ALU.add, op1=ALU.max, accum_out=gm[0:32, 2, hh:hh + 1]))
                    dc.sync()
                    dc.run(nc.vector.tensor_tensor(g[:], gm[:], m0tok[:, :, pair], ALU.max))
                    dc.sync()
                    dc.run(nc.vector.tensor_scalar(ng[:], g[:], -1.0, None, ALU.mult))
                    dc.run(nc.vector.tensor_tensor(wprev[:], m0tok[:, :, pair], g[:], ALU.subtract))
                    dc.run(nc.vector.tensor_tensor(mt[:, :, pair], btok[:, :, pair], g[:], ALU.add))
                    dc.run(nc.vector.tensor_tensor(gl8[:], g[0:32, 2, :].unsqueeze(2).broadcast_to([32, 2, NB]),
                                                   K["lastm"][0:32].unsqueeze(1).broadcast_to([32, 2, NB]), ALU.mult))
                    dc.sync()
                    dc.run(nc.vector.reduce_sum(qn[:], qn8[:], AX))
                    nc.vector.tensor_scalar(emm[:], mt[:, :, pair], -1.0, None, ALU.mult).then_inc(m_g, 1)
                if j == 1:
                    dve.wait_ge(m_gl, p + 1)
                    dc.run(nc.vector.tensor_tensor(wend[:, 0:2, :], atok[:, 0:2, pair], B[4][:, 0:2].unsqueeze(1).broadcast_to([P, 2, 2]), ALU.subtract))
                    dc.run(nc.vector.tensor_tensor(wend[0:32, 2, :], atok[0:32, 2, pair], B[4][0:32, 2:4], ALU.subtract))
                    nc.vector.tensor_tensor(decay[:], m0v[:, pair, :], B[4][:, 4:20].rearrange("p (h b) -> p h b", b=NB), ALU.subtract).then_inc(m_gls, 1)
                    for hh in range(2):
                        dve.wait_ge(m_w, 2 * p + hh + 1)
                        dc.run(nc.vector.tensor_tensor(X[:, hh, 0:384], X[:, hh, 0:384], B[2 + hh][:, 0:384], ALU.mult))
                        nc.vector.tensor_tensor(X[0:32, hh, 384:416], X[0:32, hh, 384:416], B[2 + hh][0:32, 384:416], ALU.mult).then_inc(m_sw, 1)
                if j == 2:
                    dve.wait_ge(m_we, 2 * p + 2)
                    dve.wait_ge(m_kc, 2 * p + 2)
                    for hh in range(2):
                        dc.run(nc.vector.tensor_scalar(wsel[:, hh, :], K["bmask"][0:32], wend[0:32, 2, hh:hh + 1], None, ALU.mult))
                    for hh in range(2):
                        for r in range(2):
                            last = nc.vector.tensor_scalar(kw[:, r, hh, :], mK[:, r, hh, :], wend[:, r, hh:hh + 1], None, ALU.mult)
                    last.then_inc(m_kw, 1)
                    dc.sync()
                    vexp_of(0)
                    dve.wait_ge(m_s2, p + 1)
                    dve.wait_ge(m_em, 2 * p + 2)
                    for hh in range(2):
                        dc.run(nc.vector.tensor_scalar(tq[:, hh, :], B[6][0:32, hh * P:(hh + 1) * P], wprev[0:32, 2, hh:hh + 1], None, ALU.mult))
                    dve.wait_ge(evac_done[p_ml.bank(7)], p_ml.evacs(p, 7) + 1)
                    dve.wait_ge(evac_done[p_ml.bank(6)], p_ml.evacs(p, 6) + 1)
                    dc.run(nc.vector.tensor_scalar(mo[:], mo[:], 1.0, None, ALU.add))
                    dc.sync()
                    dc.run(nc.vector.reciprocal(mo[:], mo[:]))
                    dc.run(nc.vector.tensor_tensor(qn[:], qn[:], wprev[0:32, 2, :], ALU.mult))
                    dc.sync()
                if j == 3:
                    dve.wait_ge(m_s3, p + 1)
                    for hh in range(2):
                        N = B[2 + hh]
                        dc.run(nc.vector.tensor_copy(hs[:, 0:2, hh, :], N[:, 0:2 * (P + 1)].rearrange("p (r c) -> p r c", c=P + 1)))
                        dc.run(nc.vector.tensor_tensor(hs[0:32, 2, hh, 0:P], tq[:, hh, :], N[0:32, 258:386], ALU.add))
                        last = nc.vector.tensor_tensor(hs[0:32, 2, hh, P:P + 1], qn[:, hh:hh + 1], N[0:32, 386:387], ALU.add)
                    last.then_inc(m_hs, 1)
                    dve.wait_ge(m_hs, p + 1)
                    dc.sync()
                    dc.run(nc.vector.scalar_tensor_tensor(den[:], hs[:, :, :, P], -1.0, hs[:, :, :, P], ALU.mult, ALU.max))
                    dc.sync()
                    dc.run(nc.vector.tensor_tensor(den[:], den[:], emm[:], ALU.max))
                    dc.sync()
                    dc.run(nc.vector.reciprocal(rden[:], den[:]))
                    dc.sync()
                    dc.run(nc.vector.tensor_tensor(rd2[:], rden[:], rden[:], ALU.mult))
                    dve.wait_ge(m_sq, p + 1)
                    dc.run(nc.vector.reduce_sum(ss[:], sqb, AX))
                    dc.sync()
                    dc.run(nc.vector.tensor_tensor(ss[:], ss[:], rd2[:], ALU.mult))
                    dc.sync()
                    nc.vector.tensor_scalar(ss[:], ss[:], 1.0 / DH, EPS, ALU.mult, ALU.add).then_inc(m_ms, 1)
                    c_add(p, 0)
                    vexp_of(1)
                    nc.vector.tensor_copy(cP[:], B[7][:, 0:2 * (P + 1)].rearrange("p (h c) -> p h c", h=2)).then_inc(m_cp, 1)
                    dc.run(nc.vector.tensor_tensor(ntA[:], n0v[:, pair, :], decay[:], ALU.mult))
                    dc.sync()
                    dc.run(nc.vector.tensor_tensor(nnv[:, pair, :], ntA[:], B[7][:, 258:274].rearrange("p (h b) -> p h b", b=NB), ALU.add))
                    dve.wait_ge(m_cp, p + 1)
                    nc.vector.tensor_copy(nP[:, pair], cP[:, :, P]).then_inc(m_n, 1)
                    dve.wait_ge(m_sc, p + 1)
                    dc.run(nc.vector.tensor_tensor(sc[:], ss[:], rden[:], ALU.mult))
                    dc.sync()
                    nc.vector.tensor_tensor(hs[:, :, :, 0:P], hs[:, :, :, 0:P], sc[:].unsqueeze(3).broadcast_to([P, 3, 2, P]), ALU.mult).then_inc(m_hsr, 1)
                if j == 4:
                    dve.wait_ge(m_s4, p + 1)
                    for hh in range(2):
                        nc.vector.scalar_tensor_tensor(htmp[:, hh, :], B[2 + hh][:, 0:NT], gains[:, ds(2 * p + (80 + hh), 1)], mo[:, hh, :],
                                                       ALU.mult, ALU.mult).then_inc(m_tmp, 1)
                    c_add(p, 1)
                if j == 6:
                    dve.wait_ge(m_hi, p + 1)
                    nc.vector.tensor_tensor(hml[:, pair, :], htmp[:], hmh[:, pair, :].bitcast(F32), ALU.subtract).then_inc(m_lo, 1)
                if j == 7:
                    dve.wait_ge(m_lo, p + 1)
                    dve.wait_ge(m_cps, 16 * p + 16)

            def ml_body(i, gemm, attn):
                if attn:
                    ml_arow(i - 1)
                for j in range(8):
                    if gemm:
                        lo(p_ml, i, j // 2, j, src256(p_ml.slot(j // 2), j % 2))
                    elif 2 < j < 5:
                        lo(p_mo, 0, 0, j - 3, src256(p_mo.slot(0), j - 3))
                    if attn:
                        ml_attn(i - 1, j)
            ml_body(0, True, False)
            with dve.Fori(1, 4) as i:
                dc.loop(i - 1, ML_DVE)
                ml_body(i, True, True)
            dc.loop(3, ML_DVE)
            ml_body(4, False, True)
            dc.end(4)
            dve.wait_ge(m_nt, 1)
            nc.vector.tensor_copy(noutS[:], B[2][0:64, 0:P]).then_inc(m_no, 1)
            nc.vector.tensor_copy(noutP[:], B[2][0:H, P:2 * P]).then_inc(m_no, 1)

            def mo_attn(p, j):
                pair = ds(2 * p, 2)
                if j == 2:
                    dve.wait_ge(a_s1, p + 1)
                    for hh in range(2):
                        dc.run(nc.vector.scalar_tensor_tensor(pX[:, hh, :], K["cdist"], K["slopes"][:, ds(2 * p + hh, 1)], B[2 + hh][:, 0:384],
                                                              ALU.mult, ALU.add))
                    dc.sync()
                    for hh in range(2):
                        dc.run(nc.vector.reduce_max(arm[:, hh, 0:1], pX[:, hh, 0:P], AX))
                        dc.run(nc.vector.reduce_max(arm[:, hh, 1:2], pX[:, hh, P:384], AX))
                    dc.sync()
                    nc.vector.tensor_scalar(arm[:], arm[:], -1.0, None, ALU.mult).then_inc(a_x, 1)
                    dve.wait_ge(a_p, p + 1)
                    dc.run(nc.vector.reciprocal(asum[:], asum[:]))
                    dc.sync()
                    for hh in range(2):
                        nc.vector.tensor_scalar(pX[:, hh, 0:P], pX[:, hh, 0:P], asum[:, hh, 0:1], None, ALU.mult)
                        last = nc.vector.tensor_scalar(pX[:, hh, P:384], pX[:, hh, P:384], asum[:, hh, 1:2], None, ALU.mult)
                    last.then_inc(a_pn, 1)
                if j == 4:
                    dve.wait_ge(a_pv, p + 1)
                    nc.vector.tensor_copy(atmp[:], B[6][:].rearrange("p (h c) -> p h c", h=2)).then_inc(a_tmp, 1)
                    dve.wait_ge(a_hi, p + 1)
                    nc.vector.tensor_tensor(hal[:, pair, 0:TP], atmp[:], hah[:, pair, 0:TP].bitcast(F32), ALU.subtract).then_inc(a_lo, 1)

            def mo_body(i, gemm, attn):
                for j in range(6):
                    if gemm and (attn or j >= 2):
                        lo(p_mo, i, j // 2, j, src256(p_mo.slot(j // 2), j % 2))
                    if attn:
                        mo_attn(i - 1, j)
            mo_body(0, True, False)
            with dve.Fori(1, 4) as i:
                dc.loop(i - 1, MO_DVE)
                mo_body(i, True, True)
            dc.loop(3, MO_DVE)
            mo_body(4, False, True)
            dc.end(4)

            def k_copies(kts, tr_sem, ss_sem, mine, base, i):
                for n in range(1, 16, 2):
                    dve.wait_ge(tr_sem, i * 16 + (base + n + 1))
                    dve.wait_ge(ss_sem, i * 16 + (base + n + 1))
                    nc.vector.tensor_copy(kts[1][:], B[2 + n % 4][:].rearrange("p (h c) -> p h c", c=P)).then_inc(mine, 1)

            def d_batch(b, k, v):
                if k:
                    nc.vector.tensor_copy(qpad[:].rearrange("p (h c) -> p h c", c=NS + TS)[:, :, 0:TS],
                                          qs[:, :, ds(b * TS, TS)]).then_inc(d_q, 1)
                    k_copies(KTb, d_tr, d_ss, d_ktd, 0, b)
                    dve.wait_ge(d_sc, b + 1)
                    for q in range(2):
                        dc.run(nc.vector.reduce_sum(gs[:, 2 * q:2 * q + 2], B[6 + q][0:NS, :].rearrange("p (n c) -> p n c", c=256), AX))
                    dc.sync()
                    dc.run(nc.vector.tensor_reduce(dmn[:], gs[:], AX, ALU.min))
                    dc.sync()
                    dc.run(nc.vector.scalar_tensor_tensor(geq[:], gs[:], dmn[:], K["rank"][0:NS], ALU.is_equal, ALU.mult))
                    dc.sync()
                    dc.run(nc.vector.reduce_max(dmx[:], geq[:], AX))
                    dc.sync()
                    dc.run(nc.vector.tensor_scalar(pen[:], geq[:], dmx[:], NEG, ALU.is_equal, ALU.mult))
                    dc.sync()
                    for n in range(BLOCKS):
                        dc.run(nc.vector.scalar_tensor_tensor(DP[:, n * 256:(n + 1) * 256], B[6 + n // 2][0:NS, (n % 2) * 256:(n % 2) * 256 + 256],
                                                              pen[:, n:n + 1], dtab[:, n * 256:(n + 1) * 256], ALU.add, ALU.add))
                    dc.run(nc.vector.tensor_tensor(DP[:, PAST:], B[1][0:NS, 256:256 + NS], dtab[:, ds(b * -TS + (PAST + OWN), NS)], ALU.add))
                    dc.sync()
                    dc.run(nc.vector.reduce_max(dmx[:], DP[:], AX))
                    dc.sync()
                    nc.vector.tensor_scalar(dmx[:], dmx[:], -1.0, None, ALU.mult).then_inc(d_sm, 1)
                    dve.wait_ge(d_p, b + 1)
                    dc.run(nc.vector.reciprocal(dsum[:], dsum[:]))
                    dc.sync()
                    nc.vector.tensor_scalar(DP[:], DP[:], dsum[:], None, ALU.mult).then_inc(d_pn, 1)
                if v:
                    dve.wait_ge(d_pvb, b)
                    nc.vector.tensor_copy(hrow[:, 4 * P:], B[3][0:NS, :]).then_inc(d_vb, 1)
                    dve.wait_ge(d_ht, b)
                    nc.vector.tensor_copy(hsd[:, :, ds(b * TS - TS, TS)],
                                          B[1][:, 0:H * (NS + TS)].rearrange("p (h c) -> p h c", c=NS + TS)[:, :, 0:TS]).then_inc(d_h, 1)
            dve.wait_ge(a_kc, 4)
            dve.wait_ge(a_ks, 16 * 12)
            dve.wait_ge(a_vs, 16 * 12)
            dve.wait_ge(a_vcp, 4)
            dve.wait_ge(a_lo, 4)
            dve.wait_ge(d_tab, 16)
            dc.run(nc.vector.memset(qpad[:], 0.0))
            dc.sync()
            nc.vector.engine_nop().then_inc(d_h, 1)
            d_batch(0, True, False)
            D_DVE = 13
            with dve.Fori(1, NB) as b:
                dc.loop(b - 1, D_DVE)
                d_batch(b, True, True)
            dc.end(NB - 1)
            d_batch(NB, False, True)
            dve.wait_ge(d_hi, 1)
            nc.vector.tensor_tensor(hal[:, :, TP:NT], hsd[:], hah[:, :, TP:NT].bitcast(F32), ALU.subtract).then_inc(d_lo, 1)
            dve.wait_ge(d_lo, 1)

            def mx_tail(i, j):
                dve.wait_ge(x_p, i * 2 + (j + 1))
                dc.run(nc.vector.tensor_tensor(ut[:, 0, :], B[2 + 2 * j][:, 0:NT], sg[:, j, :], ALU.mult))
                dc.run(nc.vector.tensor_tensor(ut[:, 1, :], B[3 + 2 * j][:, 0:NT], sg[:, 2 + j, :], ALU.mult))
                dc.sync()
                nc.vector.tensor_tensor(U[:, ds(i * 2 + j, 1), :], ut[:, 0:1, :], ut[:, 1:2, :], ALU.add).then_inc(x_pe, 2)
                dve.wait_ge(x_pe, 4 * i + (2 * j + 6))

            nc.vector.engine_nop().then_inc(x_pe, 4)
            def mx_sig(i, t):
                for b in (t, t + 1):
                    dve.wait_ge(evac_done[p_mx.bank(b)], p_mx.evacs(i, b) + 1)
                dc.run(nc.vector.tensor_scalar(sg[:, t:t + 2, :], sg[:, t:t + 2, :], 1.0, None, ALU.add))
                dc.sync()
                dc.run(nc.vector.reciprocal(sg[:, t:t + 2, :], sg[:, t:t + 2, :]))
                dc.sync()

            def mx_body(i, first):
                for j in range(6):
                    if 0 < j < 3 and not first:
                        mx_tail(i - 1, j - 1)
                    lo(p_mx, i, j // 2, j, src256(p_mx.slot(j // 2), j % 2))
                    if j == 3:
                        mx_sig(i, 0)
                mx_sig(i, 2)
            mx_body(0, True)
            with dve.Fori(1, 8) as i:
                dc.loop(i - 1, 8)
                mx_body(i, False)
            dc.end(7)
            mx_tail(7, 0)
            lo(p_wo, 0, 0, 0, src256(p_wo.slot(0), 0))
            mx_tail(7, 1)
            for q in range(4):
                dve.wait_ge(x_uhi, q + 1)
                nc.vector.tensor_tensor(xl[:, 4 * q:4 * q + 4, :], U[:, 4 * q:4 * q + 4, :], xh[:, 4 * q:4 * q + 4, :].bitcast(F32),
                                        ALU.subtract).then_inc(x_ulo, 1)

            def add_to_x(ph, i, t, conv, m):
                dve.wait_ge(gemm_done, ph.conv(i, conv + 1))
                nc.vector.tensor_tensor(xT[:, m, :], xT[:, m, :], G[ph.bank(t)][:, 0:NT].unsqueeze(1), ALU.add).then_inc(evac_done[ph.bank(t)], 1)

            def wo_body(i, first):
                for j in range(4):
                    if j or not first:
                        lo(p_wo, i, j // 2, j, src256(p_wo.slot(j // 2), j % 2))
                    if j >= 2:
                        add_to_x(p_wo, i, j - 2, j - 2, ds(i * 4 + (j - 2), 1))
                    elif not first:
                        add_to_x(p_wo, i - 1, j + 2, j + 2, ds(i * 4 + (j - 2), 1))
            wo_body(0, True)
            for n in (1, 3, 5, 7):
                dve.wait_ge(tp_done, 9 + n + 1)
                t, k4 = n // 4, n % 4
                nc.vector.tensor_copy(memT[:, 4 * k4:4 * k4 + 4, t * P:(t + 1) * P],
                                      B[2 + n % 4][:].rearrange("p (k c) -> p k c", c=P)).then_inc(tp_odd, 1)
            with dve.Fori(1, 3) as i:
                wo_body(i, False)

            def mem_lo(j):
                lo(p_mem, 0, j // 2, j, src256(p_mem.slot(j // 2), j % 2))

            def xq_lo(j):
                lo(p_xq, 0, j // 2, j, src256(p_xq.slot(j // 2), j % 2))
            for j in range(4):
                lo(p_wo, 3, j // 2, j, src256(p_wo.slot(j // 2), j % 2))
                if j < 2:
                    add_to_x(p_wo, 2, j + 2, j + 2, ds(10 + j, 1))
                else:
                    add_to_x(p_wo, 3, j - 2, j - 2, ds(10 + j, 1))
                if j == 0:
                    dve.wait_ge(tp_even, 5 + 4)
                    dve.wait_ge(tp_odd, 4 + 4)
                    norm(1, memT, MEM)
                else:
                    norm_step(1, memT, 32, MEM, j - 1, mxh, mxl)
            mem_lo(0)
            add_to_x(p_wo, 3, 2, 2, ds(14, 1))
            norm_step(1, memT, 32, MEM, 3, mxh, mxl)
            mem_lo(1)
            add_to_x(p_wo, 3, 3, 3, ds(15, 1))
            for j in range(2, 8):
                mem_lo(j)
                if j == 4:
                    for b in range(2):
                        dve.wait_ge(evac_done[b], p_mem.evacs(0, (b + p_mem.tile0) % 2))
                    norm(2, xT, NT)
                if j > 4:
                    norm_step(2, xT, 16, NT, j - 5, xh, xl)
            xq_lo(0)
            norm_step(2, xT, 16, NT, 3, xh, xl)
            for j in range(1, 4):
                xq_lo(j)

            for b in range(2):
                dve.wait_ge(evac_done[b], p_up[0].evacs(0, (b + p_up[0].tile0) % 2))
            dc.run(nc.vector.memset(xqpad[:], 0.0))
            dc.sync()
            dve.wait_ge(c_s, 1)
            for h in range(XH):
                dc.run(nc.vector.tensor_copy(xP[:, h, :, :], B[2 + h][:].rearrange("p (r c) -> p r c", c=MEM)))
            dc.sync()
            nc.vector.tensor_copy(xqpad[:].rearrange("p b (h c) -> p b h c", c=NS + TS)[:, :, :, 0:TS],
                                  xq[:, :, TP:NT].rearrange("p h (b t) -> p b h t", t=TS)).then_inc(d_q, 1)
            dc.run(nc.vector.reduce_max(xmx[:], xP[:], AX))
            dc.sync()
            nc.vector.tensor_scalar(xmx[:], xmx[:], -1.0, None, ALU.mult).then_inc(c_x, 1)
            k_copies(xKT, d_tr, d_ss, d_ktd, 128, 0)
            dve.wait_ge(c_p, 1)
            dc.run(nc.vector.reciprocal(xsm[:], xsm[:]))
            dc.sync()
            nc.vector.tensor_tensor(xP[:], xP[:], xsm[:].unsqueeze(3).broadcast_to([P, XH, 2, MEM]), ALU.mult).then_inc(c_pn, 1)
            dve.wait_ge(c_sc, 1)
            dc.run(nc.vector.tensor_copy(xDP[:], B[6][:].rearrange("p (u c) -> p u c", c=MEM)))
            dc.sync()
            dc.run(nc.vector.reduce_max(smx[:], xDP[:], AX))
            dc.sync()
            nc.vector.tensor_scalar(smx[:], smx[:], -1.0, None, ALU.mult).then_inc(c_sx, 1)
            dve.wait_ge(c_sp, 1)
            dc.run(nc.vector.reciprocal(ssm[:], ssm[:]))
            dc.sync()
            nc.vector.tensor_tensor(xDP[:], xDP[:], ssm[:].unsqueeze(2).broadcast_to([P, 2, MEM]), ALU.mult).then_inc(c_spn, 1)
            for q in range(2):
                dve.wait_ge(c_pv, q + 1)
                nc.vector.tensor_copy(octx[:, 2 * q:2 * q + 2, 0:TP], B[6 + q][:].rearrange("p (h c) -> p h c", c=TP)).then_inc(c_ctx, 1)
            for u in range(2):
                dve.wait_ge(c_spv, u + 1)
                nc.vector.tensor_copy(xrow[:, u, :], B[5 + u][:]).then_inc(c_st, 1)
            for u in range(2):
                dve.wait_ge(c_rows, u + 1)
                for h in range(XH):
                    last = nc.vector.tensor_copy(octx[:, h, TP + 16 * u:TP + 16 * u + 16].rearrange("p (b t) -> p b t", t=TS),
                                                 B[2 + u][:, h * P:(h + 1) * P].rearrange("p (b c) -> p b c", c=NS)[:, :, h * TS:(h + 1) * TS])
            last.then_inc(c_ctx, 1)
            dve.wait_ge(c_ctx, 3)
            dve.wait_ge(c_chi, 1)
            nc.vector.tensor_tensor(ctxl[:], octx[:], ctxh[:].bitcast(F32), ALU.subtract).then_inc(c_clo, 1)

            def xo_add(c):
                dve.wait_ge(gemm_done, p_xo.conv(0, c + 1))
                for m in range(4):
                    last = nc.vector.tensor_tensor(xT[:, 4 * c + m, :], xT[:, 4 * c + m, :], B[4 * (c % 2) + m][:, 0:NT], ALU.add)
                last.then_inc(c_xo, 1)
            for j in range(6):
                if j < 4:
                    lo(p_xo, 0, j // 2, j, xo_src(j))
                if j >= 2:
                    xo_add(j - 2)
            dve.wait_ge(c_xo, 4)
            dve.wait_ge(c_out, 64)

            norm(3, xT, NT, lambda: lo(p_up[0], 0, 0, 0, src256(p_up[0].slot(0), 0)))
            norm_apply(3, xT, 48, NT)

            def up_sig(f, i, t):
                dve.wait_ge(evac_done[p_up[f].bank(t)], p_up[f].evacs(i, t) + 1)
                dc.run(nc.vector.tensor_scalar(fe[:, t, :], fe[:, t, :], 1.0, None, ALU.add))
                dc.sync()
                dc.run(nc.vector.reciprocal(fe[:, t, :], fe[:, t, :]))
                dc.sync()
                dc.run(nc.vector.tensor_tensor(fg[:, t, :], fg[:, t, :], fe[:, t, :], ALU.mult))
                dc.sync()

            def up_mul(f, i, t):
                dve.wait_ge(gemm_done, p_up[f].conv(i, t + 3))
                nc.vector.tensor_tensor(fa[:, t, :], fg[:, t, :], G[p_up[f].bank(t + 2)][:, 0:NT], ALU.mult).then_inc(f_a, 1)
                nc.vector.engine_nop().then_inc(evac_done[p_up[f].bank(t + 2)], 1)

            def up_lo(f, i):
                dve.wait_ge(f_hi, i + (1 + f * (FH // 2)))
                nc.vector.tensor_tensor(fal[:, ds(i * 2, 2), :], fa[:], fah[:, ds(i * 2, 2), :].bitcast(F32), ALU.subtract).then_inc(f_lo, 1)

            def up_body(f, i, first):
                for j in range(4):
                    if j < 2 and not first:
                        up_mul(f, i - 1, j)
                    if j or not first:
                        lo(p_up[f], i, j // 2, j, src256(p_up[f].slot(j // 2), j % 2))
                    if j >= 2:
                        up_sig(f, i, j - 2)
                    if j == 2 and not first:
                        up_lo(f, i - 1)
                if not first:
                    dve.wait_ge(f_lo, i + f * (FH // 2))
            for f in range(2):
                up_body(f, 0, True)
                with dve.Fori(1, FH // 2) as i:
                    dc.loop(i - 1, 6)
                    up_body(f, i, False)
                dc.end(FH // 2 - 1)
                ph = p_dn[f]
                up_mul(f, FH // 2 - 1, 0)
                lo(ph, 0, 0, 0, src256(ph.slot(0), 0)[:, 0:FU])
                up_mul(f, FH // 2 - 1, 1)
                up_lo(f, FH // 2 - 1)

                def dn_body(i, first):
                    for j in range(4):
                        if j or not first:
                            lo(ph, i, j // 2, j, src256(ph.slot(j // 2), j % 2)[:, 0:FU])
                        if j < 2 and not first:
                            add_to_x(ph, i - 1, j, j + 2, ds(i * 2 + (j - 2), 1))
                dn_body(0, True)
                with dve.Fori(1, 8) as i:
                    dn_body(i, False)
                add_to_x(ph, 7, 0, 2, ds(14, 1))
                if f == 0:
                    lo(p_up[1], 0, 0, 0, src256(p_up[1].slot(0), 0))
                add_to_x(ph, 7, 1, 3, ds(15, 1))
                dve.wait_ge(f_lo, (f + 1) * (FH // 2))
            dve.wait_ge(evac_done[p_dn[1].bank(0)], p_dn[1].evacs(8, 0))
            dve.wait_ge(evac_done[p_dn[1].bank(1)], p_dn[1].evacs(8, 1))
            norm(4, xT, NT)
            nr = later_scratch[3]
            for k in range(KT):
                nc.vector.scalar_tensor_tensor(xT[:, k, :], xT[:, k, :], gains[:, 64 + k:65 + k], nr[:], ALU.mult, ALU.mult).then_inc(y_r, 1)
            for n in range(1, 12, 2):
                dve.wait_ge(tp_done, 17 + n + 1)
                rows_ = (P, P, NS)[n // 4]
                nc.vector.tensor_copy(yout[0:rows_, n // 4, (n % 4) * 512:(n % 4) * 512 + 512], B[2 + n % 4][0:rows_, :]).then_inc(tp_odd, 1)

        @block.tensor
        def _(pe):
            mm = nc.tensor.matmul

            def tile(ph, i, u, c, t, n=NT, x_sem=None, x0=0, x=None):
                s, half, bank = ph.slot(u), ph.half(c), ph.bank(t)
                rh, rl = x or (xh, xl)
                pe.wait_ge(slot_read[s], ph.reads(i, u, c % 2 + 1))
                wait(pe, evac_done[bank], ph.evacs(i, t))
                for k in range(KT):
                    out = G[bank][:, 0:n]
                    if x_sem and k % 4 == 0:
                        pe.wait_ge(x_sem, x0 + k // 4 + 1)
                    mm(out, wh[half][:, k, :], rh[:, k, 0:n], start=k == 0, stop=False)
                    mm(out, wh[half][:, k, :], rl[:, k, 0:n], start=False, stop=False)
                    last = mm(out, wl[half][:, k, :], rh[:, k, 0:n], start=False, stop=k == KT - 1)
                last.then_inc(gemm_done, 1)

            def norm(q, n):
                sq = (later_scratch if q else first_scratch)[0]
                for k in range(KT):
                    pe.wait_ge((sq_ready, sq_odd)[k % 2], KT // 2 * q + k // 2 + 1)
                    mm(B[2][:, 0:n], ones[:], sq[:, k % 4, 0:n], start=k == 0, stop=k == KT - 1).then_inc(sq_used, 1)

            def one(out, lhsT, rhs, start=True, stop=True):
                return mm(out, lhsT, rhs, start=start, stop=stop)

            def tr(out, src):
                n = src.shape[0]
                return nc.tensor.transpose(out, src, ident[0:n, 0:n])

            pe.wait_ge(const_in, 16)
            pe.wait_ge(ones_set, 1)
            for n in range(9):
                t, k4 = n // 4, n % 4
                pe.wait_ge(landed[t // 2], 16 * (2, 1)[t // 2])
                if n >= 4:
                    pe.wait_ge((tp_even, tp_odd)[n % 2], (n - 4) // 2 + 1)
                if n < 8:
                    for k in range(4):
                        kk = 4 * k4 + k
                        last = tr(B[2 + n % 4][:, k * P:(k + 1) * P], raw[0][:, t * D + kk * P:t * D + (kk + 1) * P])
                else:
                    for k in range(KT):
                        last = tr(B[2][:, k * NS:(k + 1) * NS], raw[1][0:NS, k * P:(k + 1) * P])
                last.then_inc(tp_done, 1)
            pe.wait_ge(params_in, PARAMS)
            tr(B[6][:, 0:88], grow[:])
            tr(B[7][:, 0:64], n0raw[:]).then_inc(gains_t, 1)
            pe.drain().then_inc(slot_read[0], 1)
            pe.drain().then_inc(slot_read[1], 1)
            pe.wait_ge(tp_even, 5)
            norm(0, NT)
            tile(p_gate, 0, 0, 0, 0, x_sem=xn_ready)

            pe.wait_ge(evac_done[0], 1)
            pe.wait_ge(m_mem, 1)
            tr(B[3][:, 0:16], gT[:, 0:P])
            tr(B[3][:, 16:32], gT[:, P:TP])
            tr(B[3][0:32, 32:48], gT[:, TP:NT]).then_inc(g_t, 1)
            pe.wait_ge(g_lf, 1)
            one(B[4][:, 0:8], K["tri"], lf[:, 0, :])
            one(B[4][:, 8:16], ones[:], lf[:, 0, :], stop=False)
            one(B[4][:, 8:16], K["tri"], lf[:, 1, :], start=False)
            one(B[4][0:32, 16:24], K["tris"][0:32], lf[0:32, 2, :]).then_inc(g_cum, 1)
            pe.wait_ge(g_a, 1)
            tr(B[5][0:8, 0:P], atok[:, 0, :])
            tr(B[5][0:8, P:TP], atok[:, 1, :])
            tr(B[5][0:8, TP:NT], atok[0:32, 2, :]).then_inc(g_aT, 1)
            pe.wait_ge(g_aTs, 1)
            n0v = n0T[:].rearrange("p (b h) -> p h b", h=H)

            def rows(banks, src, n):
                for hh in range(2):
                    tr(banks[hh][:, 0:P], src[:, hh, 0:P])
                    tr(banks[hh][:, P:2 * P], src[:, hh, P:TP])
                    last = tr(banks[hh][0:32, 2 * P:3 * P], src[:, hh, TP:NT])
                return last

            def ml_attn(p, j):
                if j == 0:
                    pe.wait_ge(evac_done[p_ml.bank(5)], p_ml.evacs(p, 5) + 1)
                    pe.wait_ge(evac_done[p_ml.bank(4)], p_ml.evacs(p, 4) + 1)
                    pe.wait_ge(m_arow, 2 * p + 2)
                    pe.wait_ge(m_c0in, 32 * p + 32)
                    pe.wait_ge(m_vc, 2 * p + 2)
                    for hh in range(2):
                        one(B[2 + hh][:, 0:P], mq[:, hh, 0:P], mk[:, hh, 0:P])
                        one(B[2 + hh][:, P:384], mq[:, hh, P:TP], mk[:, hh, 0:TP])
                        one(B[2 + hh][0:32, 384:416], mq[:, hh, TP:NT], mk[:, hh, TP:NT])
                        one(B[4 + hh][:, 0:NT], ones[0:H, :], arow[:, hh, :])
                        for b in range(NB):
                            one(B[6][:, 32 * hh + TS * b:32 * hh + TS * b + TS], C0[:, hh, b, :], mq[:, hh, TP + TS * b:TP + TS * b + TS])
                        last = one(B[6][0:32, 64 + 8 * hh:72 + 8 * hh], mq[:, hh, TP:NT], n0v[:, ds(2 * p + hh, 1), :].rearrange("p a b -> p (a b)"))
                    last.then_inc(m_s1, 1)
                if j == 1:
                    pe.wait_ge(m_g, p + 1)
                    rows((B[7], B[6]), mk, 0).then_inc(m_ktr, 1)
                    one(B[4][:, 0:2], K["lastp"], g[:, 1, :])
                    one(B[4][0:32, 2:4], K["lasts"][0:32], g[0:32, 2, :])
                    one(B[4][:, 4:20], ones[0:32, :], gl8[:].rearrange("p h b -> p (h b)")).then_inc(m_gl, 1)
                if j == 2:
                    pe.wait_ge(m_gls, p + 1)
                    pe.wait_ge(m_kc, 2 * p + 2)
                    for hh in range(2):
                        pe.wait_ge(m_sw, 2 * p + hh + 1)
                        for r in range(3):
                            tr(B[4 + hh][:, r * P:(r + 1) * P], X[:, hh, r * P:(r + 1) * P])
                        tr(B[4 + hh][0:32, 384:416], X[0:32, hh, 384:416])
                        last = tr(B[6][0:32, hh * P:(hh + 1) * P], qc[:, hh, :])
                    last.then_inc(m_s2, 1)
                if j == 3:
                    pe.wait_ge(m_swt, 2 * p + 2)
                    pe.wait_ge(m_kw, p + 1)
                    for hh in range(2):
                        N = B[2 + hh]
                        one(N[:, 0:129], swt[:, hh, 0:P], mV[:, 0, hh, :])
                        one(N[:, 129:258], swt[:, hh, P:2 * P], mV[:, 0, hh, :], stop=False)
                        one(N[:, 129:258], swt[:, hh, 2 * P:3 * P], mV[:, 1, hh, :], start=False)
                        one(N[0:32, 258:387], swt[0:32, hh, 384:416], mV[0:32, 2, hh, :])
                    for hh in range(2):
                        one(B[7][:, 129 * hh:129 * hh + 129], kw[:, 0, hh, :], mV[:, 0, hh, :], stop=False)
                        one(B[7][:, 129 * hh:129 * hh + 129], kw[:, 1, hh, :], mV[:, 1, hh, :], start=False)
                        one(B[7][:, 258 + 8 * hh:266 + 8 * hh], mK[0:32, 2, hh, :], wsel[:, hh, :])
                    pe.wait_ge(m_vx, 2 * p + 1)
                    for q in range(2):
                        last = one(B[4 + q][:, :], mK[0:32, 2, 0, :], vexp[:, 4 * q:4 * q + 4, :].rearrange("p b v -> p (b v)"))
                    last.then_inc(m_s3, 1)
                if j == 4:
                    pe.wait_ge(m_vx, 2 * p + 2)
                    pe.wait_ge(m_cadd, 2 * p + 1)
                    for q in range(2):
                        last = one(B[4 + q][:, :], mK[0:32, 2, 1, :], vexp[:, 4 * q:4 * q + 4, :].rearrange("p b v -> p (b v)"))
                    pe.wait_ge(m_hsr, p + 1)
                    for hh in range(2):
                        tr(B[2 + hh][:, 0:P], hs[:, 0, hh, 0:P])
                        tr(B[2 + hh][:, P:TP], hs[:, 1, hh, 0:P])
                        last = tr(B[2 + hh][:, TP:NT], hs[0:32, 2, hh, 0:P])
                    last.then_inc(m_s4, 1)
                if j == 5:
                    pe.wait_ge(m_tmp, 2 * p + 2)
                    pe.wait_ge(m_cadd, 2 * p + 2)

            def ml_body(i, gemm, attn):
                for j in range(8):
                    if attn:
                        ml_attn(i - 1, j)
                    if gemm:
                        tile(p_ml, i, j // 2, j, j)
                    if not gemm and j in (3, 5):
                        tile(p_mo, 0, 0, j // 2 - 1, j // 2 - 1)
                    if gemm and j == 4:
                        pe.wait_ge(evac_done[p_ml.bank(0)], p_ml.evacs(i, 0) + 1)
                        pe.wait_ge(evac_done[p_ml.bank(1)], p_ml.evacs(i, 1) + 1)
                        rows((B[6], B[7]), mv, 0).then_inc(m_vtr, 1)
            ml_body(0, True, False)
            with pe.Fori(1, 4) as i:
                ml_body(i, True, True)
            ml_body(4, False, True)
            pe.wait_ge(m_n, 4)
            pe.wait_ge(m_tmp, 8)
            tr(B[2][0:64, 0:P], nnew[:])
            tr(B[2][0:H, P:2 * P], nP[:]).then_inc(m_nt, 1)

            def mo_attn(p, j):
                if j == 2:
                    pe.wait_ge(evac_done[p_mo.bank(4)], p_mo.evacs(p, 4) + 1)
                    pe.wait_ge(evac_done[p_mo.bank(5)], p_mo.evacs(p, 5) + 1)
                    pe.wait_ge(m_no, 2)
                    for hh in range(2):
                        one(B[2 + hh][:, 0:P], aq[:, hh, 0:P], ak[:, hh, 0:P])
                        last = one(B[2 + hh][:, P:384], aq[:, hh, P:TP], ak[:, hh, 0:TP])
                    last.then_inc(a_s1, 1)
                if j == 3:
                    pe.wait_ge(a_vc, p + 1)
                    pe.wait_ge(a_pn, p + 1)
                    for hh in range(2):
                        for r in range(3):
                            last = tr(B[4 + hh][:, r * P:(r + 1) * P], pX[:, hh, r * P:(r + 1) * P])
                    last.then_inc(a_ptr, 1)
                    rows((B[7], B[2]), ak, 0).then_inc(a_ktr, 1)
                if j == 4:
                    pe.wait_ge(a_ptc, p + 1)
                    for hh in range(2):
                        c = hh * TP
                        one(B[6][:, c:c + TP], vst[:, 0, hh, :], pXT[:, hh, 0:TP], stop=False)
                        last = one(B[6][:, c + P:c + TP], vst[:, 1, hh, :], pXT[:, hh, TP:384], start=False)
                    last.then_inc(a_pv, 1)
                if j == 5:
                    pe.wait_ge(a_kc, p + 1)
                    pe.wait_ge(a_tmp, p + 1)

            def mo_body(i, gemm, attn):
                for j in range(6):
                    if attn:
                        mo_attn(i - 1, j)
                    if gemm and (attn or j >= 2):
                        tile(p_mo, i, j // 2, j, j)
                    if gemm and j == 4:
                        pe.wait_ge(evac_done[p_mo.bank(0)], p_mo.evacs(i, 0) + 1)
                        pe.wait_ge(evac_done[p_mo.bank(1)], p_mo.evacs(i, 1) + 1)
                        rows((B[4], B[5]), av, 0).then_inc(a_vtr, 1)
            mo_body(0, True, False)
            with pe.Fori(1, 4) as i:
                mo_body(i, True, True)
            mo_body(4, False, True)

            def k_scores(ph, i, count, kts, base, src, score, between=None):
                for n in range(17):
                    if n == 4 and between:
                        between()
                    if n < 16:
                        if n % 8 == 0:
                            pe.wait_ge(landed[ph.slot(n // 8)], ph.landed(i, n // 8))
                        for m in range(4):
                            last = tr(B[2 + n % 4][:, m * P:(m + 1) * P], src(n, m))
                        last.then_inc(d_tr, 1)
                    if n:
                        pe.wait_ge((d_kta, d_ktd)[(n - 1) % 2], count * 8 + (base // 2 + (n - 1) // 2 + 1))
                        for m in range(4):
                            last = score(n - 1, m, kts[(n - 1) % 2][:, m, :])
                            if m == 0 and n % 8 == 0:
                                last.then_inc(slot_read[ph.slot((n - 1) // 8)], 1)
                        last.then_inc(d_ss, 1)

            pe.wait_ge(d_tab, 16)
            pe.wait_ge(a_vcp, 4)
            pe.wait_ge(evac_done[p_mo.bank(5)], p_mo.evacs(3, 5) + 1)
            pe.wait_ge(a_kc, 4)
            pe.drain().then_inc(d_ss, 2)

            def d_batch(b, k, v):
                def pt():
                    hold(pe, d_pn, b)
                    for n in range(PAGES):
                        tr(B[0][:, n * NS:(n + 1) * NS], DP[:, n * P:(n + 1) * P])
                    tr(B[0][0:NS, PAGES * NS:(PAGES + 1) * NS], DP[:, PAST:PAST + NS]).then_inc(d_ptr, 1)
                if k:
                    ph, i = (p_d, b - 1) if v else (p_d0, 0)

                    def src(n, m):
                        c = (n // 2 % 4) * H * DH + (4 * (n % 2) + m) * DH
                        return raw[ph.slot(n // 8)][:, c:c + DH]

                    def score(n, m, kt):
                        page, h = n // 2, 4 * (n % 2) + m
                        return one(B[6 + page // 4][0:NS, (page % 4) * P:(page % 4 + 1) * P], qpad[:, h * NS:(h + 1) * NS], kt,
                                   start=h == 0, stop=h == H - 1)
                    pe.wait_ge(d_q, b + 1)
                    if v:
                        pe.wait_ge(d_sm, b)
                    k_scores(ph, i, b, KTb, 0, src, score, pt if v else None)
                    pe.wait_ge(d_h, b if v else 1)
                    for h in range(H):
                        last = one(B[1][0:NS, 256:256 + NS], qpad[:, h * NS:(h + 1) * NS], ks[:, h, :], start=h == 0, stop=h == H - 1)
                    last.then_inc(d_sc, 1)
                else:
                    pt()
                if v:
                    ph, i, u0 = (p_d, b - 1, 2) if k else (p_d8, 0, 0)
                    pe.wait_ge(d_ptc, b)
                    for u in range(2):
                        s = ph.slot(u0 + u)
                        pe.wait_ge(landed[s], ph.landed(i, u0 + u))
                        for half in range(2):
                            out = B[2 + half][0:NS, :]
                            for n in range(4):
                                c = n * H * DH + half * 512
                                last = one(out, PT[:, 4 * u + n, :], raw[s][:, c:c + 512], start=u == 0 and n == 0, stop=False)
                            if half:
                                last.then_inc(slot_read[s], 1)
                            if u:
                                last = one(out, PT[0:NS, PAGES, :], Vs[:, 4 * half:4 * half + 4, :].rearrange("p h d -> p (h d)"), start=False)
                                last.then_inc((d_pva, d_pvb)[half], 1)
                    if k:
                        pe.wait_ge(d_sm, b + 1)
                    else:
                        pe.wait_ge(d_h, b)
                    for half in range(2):
                        hold(pe, (d_va, d_vb)[half], b)
                        for h in range(4 * half, 4 * half + 4):
                            last = tr(B[1][:, h * NS:(h + 1) * NS], hrow[:, h * P:(h + 1) * P])
                    last.then_inc(d_ht, 1)
            d_batch(0, True, False)
            with pe.Fori(1, NB) as b:
                d_batch(b, True, True)
            d_batch(NB, False, True)
            pe.wait_ge(d_lo, 1)

            with pe.Fori(0, 8) as i:
                for j in range(4):
                    tile(p_mx, i, j // 2, j, j)
                for j in range(2):
                    c = 4 + j
                    half = p_mx.half(c)
                    pe.wait_ge(slot_read[p_mx.slot(2)], p_mx.reads(i, 2, j + 1))
                    pe.wait_ge(x_pe, 4 * i + (2 * j + 2))
                    for n, (rh, rl) in enumerate(((hmh, hml), (hah, hal))):
                        out = B[2 + 2 * j + n][:, 0:NT]
                        for k in range(H):
                            mm(out, wh[half][:, H * n + k, :], rh[:, k, :], start=k == 0, stop=False)
                            mm(out, wh[half][:, H * n + k, :], rl[:, k, :], start=False, stop=False)
                            last = mm(out, wl[half][:, H * n + k, :], rh[:, k, :], start=False, stop=k == H - 1)
                    last.then_inc(gemm_done, 1)
                    pe.drain().then_inc(x_p, 1)
            for j in range(4):
                tile(p_wo, 0, j // 2, j, j, x_sem=None if j else x_ulo)

            pe.wait_ge(landed[2], p_min.landed(0, 0))
            for n in range(8):
                t, k4 = n // 4, n % 4
                if n >= 4:
                    pe.wait_ge((tp_even, tp_odd)[n % 2], (5, 4)[n % 2] + (n - 4) // 2 + 1)
                for k in range(4):
                    kk = 4 * k4 + k
                    last = tr(B[2 + n % 4][:, k * P:(k + 1) * P], raw[2][:, t * D + kk * P:t * D + (kk + 1) * P])
                last.then_inc(tp_done, 1)
            pe.drain().then_inc(slot_read[2], 1)
            with pe.Fori(1, 3) as i:
                for j in range(4):
                    tile(p_wo, i, j // 2, j, j)
            pe.wait_ge(tp_even, 5 + 4)
            pe.wait_ge(tp_odd, 4 + 4)
            norm(1, MEM)
            for j in range(4):
                tile(p_wo, 3, j // 2, j, j)
            for j in range(8):
                if j == 4:
                    pe.wait_ge(ms_ready, 2)
                    norm(2, NT)
                tile(p_mem, 0, j // 2, j, j, n=MEM, x_sem=None if j else xn_ready, x0=4, x=(mxh, mxl))
            for j in range(4):
                tile(p_xq, 0, j // 2, j, j, x_sem=None if j else xn_ready, x0=8)
                if j == 0:
                    for b in range(2):
                        pe.wait_ge(evac_done[b], p_xq.evacs(0, (b + p_xq.tile0) % 2))
                    for n in range(4):
                        for h in range(XH):
                            last = tr(B[2 + n][:, h * P:(h + 1) * P], (mvT, mkT)[n // 2][:, h, (n % 2) * P:(n % 2 + 1) * P])
                        last.then_inc(c_kvt, 1)
            pe.wait_ge(c_kvc, 4)
            for b in range(2):
                pe.wait_ge(evac_done[b], p_up[0].evacs(0, (b + p_up[0].tile0) % 2))
            for h in range(XH):
                for r in range(2):
                    last = one(B[2 + h][:, r * MEM:(r + 1) * MEM], xq[:, h, r * P:(r + 1) * P], mkT[:, h, :])
            last.then_inc(c_s, 1)

            def xsrc(n, m):
                c = (n % 8) * XH * DH + m * DH
                return raw[p_xk.slot(n // 8)][:, c:c + DH]

            def xscore(n, m, kt):
                b, c = n // 2, n // 8 * MEM + (n % 2) * P
                return one(B[6][b % 4 * NS:b % 4 * NS + NS, c:c + P], xqpad[:, b, m * NS:(m + 1) * NS], kt, start=m == 0, stop=m == XH - 1)
            pe.wait_ge(d_q, NB + 1)
            k_scores(p_xk, 0, 0, xKT, 128, xsrc, xscore)
            pe.drain().then_inc(c_sc, 1)
            pe.wait_ge(c_pn, 1)
            for h in range(XH):
                for m in range(2):
                    for r in range(2):
                        last = tr(B[2 + h][:, m * MEM + r * P:m * MEM + (r + 1) * P], xP[:, h, r, m * P:(m + 1) * P])
            last.then_inc(c_ptr, 1)
            pe.wait_ge(c_ptc, 1)
            pe.wait_ge(c_sx, 1)
            for h in range(XH):
                for m in range(2):
                    last = one(B[6 + h // 2][:, (h % 2) * TP:(h % 2 + 1) * TP], mVt[:, m, h * P:(h + 1) * P], xPT[:, h, m * MEM:(m + 1) * MEM],
                               start=m == 0, stop=m == 1)
                if h % 2:
                    last.then_inc(c_pv, 1)
            pe.wait_ge(c_spn, 1)
            for u in range(2):
                for m in range(2):
                    last = tr(B[2][:, (2 * u + m) * P:(2 * u + m + 1) * P], xDP[:, u, m * P:(m + 1) * P])
            last.then_inc(c_spt, 1)
            pe.wait_ge(c_spc, 1)
            pe.wait_ge(c_ctx, 2)
            for u in range(2):
                s = p_xv.slot(u)
                pe.wait_ge(landed[s], p_xv.landed(0, u))
                for b in range(4):
                    for m in range(2):
                        c = (2 * b + m) * XH * DH
                        last = one(B[5 + u][b * NS:(b + 1) * NS, :], xPTs[:, 2 * u + m, b * NS:(b + 1) * NS], raw[s][:, c:c + XH * DH],
                                   start=m == 0, stop=m == 1)
                last.then_inc(slot_read[s], 1)
                pe.drain().then_inc(c_spv, 1)
            for u in range(2):
                pe.wait_ge(c_st, u + 1)
                for h in range(XH):
                    last = tr(B[2 + u][:, h * P:(h + 1) * P], xrow[:, u, h * P:(h + 1) * P])
                last.then_inc(c_rows, 1)
            pe.wait_ge(c_clo, 1)
            for c in range(4):
                half = p_xo.half(c)
                pe.wait_ge(slot_read[p_xo.slot(c // 2)], p_xo.reads(0, c // 2, c % 2 + 1))
                if c >= 2:
                    pe.wait_ge(c_xo, c - 1)
                wv = [w[half][:].rearrange("p k c -> p (k c)").rearrange("p (k c) -> p k c", c=512) for w in (wh, wl)]
                for m in range(4):
                    out = B[4 * (c % 2) + m][:, 0:NT]
                    for k in range(XH):
                        cols = slice(m * P, (m + 1) * P)
                        mm(out, wv[0][:, k, cols], ctxh[:, k, :], start=k == 0, stop=False)
                        mm(out, wv[0][:, k, cols], ctxl[:, k, :], start=False, stop=False)
                        last = mm(out, wv[1][:, k, cols], ctxh[:, k, :], start=False, stop=k == XH - 1)
                last.then_inc(gemm_done, 1)
            pe.wait_ge(c_xo, 4)
            norm(3, NT)
            for f in range(2):
                if f:
                    pe.wait_ge(evac_done[0], p_up[1].evacs(0, p_up[1].tile0 % 2))
                for j in range(4):
                    tile(p_up[f], 0, j // 2, j, j, x_sem=None if j or f else xn_ready, x0=12)
                with pe.Fori(1, FH // 2) as i:
                    for j in range(4):
                        tile(p_up[f], i, j // 2, j, j)
                ph = p_dn[f]

                def dn_tile(i, j, first):
                    u, t, half = j // 2, j % 2, ph.half(j)
                    if first and j % 2 == 0:
                        pe.wait_ge(f_lo, f * (FH // 2) + (FU // 2 + 1, FH // 2)[u])
                    pe.wait_ge(slot_read[ph.slot(u)], ph.reads(i, u, t + 1))
                    if u == 0:
                        pe.wait_ge(evac_done[ph.bank(t)], ph.evacs(i, t))
                    out = G[ph.bank(t)][:, 0:NT]
                    for k in range(FU):
                        kk = u * FU + k
                        mm(out, wh[half][:, k, :], fah[:, kk, :], start=kk == 0, stop=False)
                        mm(out, wh[half][:, k, :], fal[:, kk, :], start=False, stop=False)
                        last = mm(out, wl[half][:, k, :], fah[:, kk, :], start=False, stop=kk == FH - 1)
                    last.then_inc(gemm_done, 1)
                for j in range(4):
                    dn_tile(0, j, True)
                with pe.Fori(1, 8) as i:
                    for j in range(4):
                        dn_tile(i, j, False)
            norm(4, NT)
            for n in range(12):
                t, k4 = n // 4, n % 4
                if t == 0:
                    pe.wait_ge(y_r, 4 * k4 + 4)
                if n >= 4:
                    pe.wait_ge((tp_even, tp_odd)[n % 2], (9, 8)[n % 2] + (n - 4) // 2 + 1)
                for k in range(4):
                    rows_ = (P, P, NS)[t]
                    last = tr(B[2 + n % 4][0:rows_, k * P:(k + 1) * P], xT[:, 4 * k4 + k, t * P:t * P + rows_])
                last.then_inc(tp_done, 1)


OUTS = dict(
    y_prompt=(1, TP, D), y_sample=(NB, TS, D), k_prompt=(1, 1, TP, H, DH), v_prompt=(1, 1, TP, H, DH),
    C_prompt=(1, 1, H, DH, DH), n_prompt=(1, 1, H, DH), m_prompt=(1, 1, H),
    mem_k_prompt=(1, 1, MEM, XH, DH), mem_v_prompt=(1, 1, MEM, XH, DH),
    k_sample=(1, NB, TS, H, DH), v_sample=(1, NB, TS, H, DH), C_sample=(1, NB, H, DH, DH),
    n_sample=(1, NB, H, DH), m_sample=(1, NB, H))


def kernel(**inputs):
    import concourse.bacc as bacc
    from concourse.bass_utils import run_bass_kernel_spmd

    nc = bacc.Bacc("TRN2", target_bir_lowering=False, num_devices=1)
    arrays, a, o = {}, {}, {}
    blob, dec = constants()
    for name, x in list(inputs.items()) + [("blob", blob), ("dec", dec)]:
        x = np.ascontiguousarray(x)
        arrays[f"{name}_dram"] = x
        a[name] = nc.dram_tensor(f"{name}_dram", x.shape, mybir.dt.from_np(x.dtype), kind="ExternalInput").ap()
    for name, shape in OUTS.items():
        o[name] = nc.dram_tensor(f"out_{name}_dram", shape, F32, kind="ExternalOutput").ap()
    build(nc, a, o)
    r = run_bass_kernel_spmd(nc, [arrays], core_ids=[0])
    return tuple(r.results[0][f"out_{name}_dram"] for name in OUTS)
```
